# Optimizing a Trainium2 kernel written in Bass

```python
import math
import jax, jax.numpy as jnp
from jax import lax
import numpy as np

D_MODEL = 1024
BATCH = 1
SEQ = 2048
DEPTH = 1
DEC_BATCH = 8
DEC_SEQ = 8
PAST_LEN = 8192
PAGE_SIZE = 128

N_HEADS_A = 4
DK = 64
DV = 2 * DK
ROT = DK // 4
ROPE_THETA = 500000.0
A_WIDTH = N_HEADS_A * DV
QK_WIDTH = N_HEADS_A * 2 * DK
B_WIDTH = D_MODEL - A_WIDTH
N_GROUPS_B = 4
C_B = B_WIDTH // N_GROUPS_B
CHUNK = 128
IN_WIDTH = 2 * QK_WIDTH + A_WIDTH + 2 * B_WIDTH
N_EXPERT_GROUPS = 4
EXPERTS_PER_GROUP = 8
N_EXPERTS = N_EXPERT_GROUPS * EXPERTS_PER_GROUP
TOP_K = 2
D_EXPERT = 512
EXPERT_BLOCK = 128
Q_BLOCK = 128
EPS = 1e-6
NEG = -1e30

kernel_name = "hymba_diffattn_chunkgmlp_hmoe_step"

def rms_norm(x, g):
    xf = x.astype(jnp.float32)
    y = xf * lax.rsqrt(jnp.mean(xf * xf, axis=-1, keepdims=True) + EPS)
    return (y * g.astype(jnp.float32)).astype(x.dtype)

def modulate(x, g, shift, scale):
    return rms_norm(x, g) * (1 + scale[:, None, :]) + shift[:, None, :]

def partial_rope(x, pos):
    inv = ROPE_THETA ** (-jnp.arange(0, ROT, 2, dtype=jnp.float32) / ROT)
    ang = pos.astype(jnp.float32)[:, None] * inv[None, :]
    cos = jnp.cos(ang)[:, None, None, :]
    sin = jnp.sin(ang)[:, None, None, :]
    xr = x[..., :ROT].astype(jnp.float32)
    x1, x2 = xr[..., :ROT // 2], xr[..., ROT // 2:]
    rot = jnp.concatenate([x1 * cos - x2 * sin, x2 * cos + x1 * sin], axis=-1).astype(x.dtype)
    return jnp.concatenate([rot, x[..., ROT:]], axis=-1)

def project_in(h, w_in, pos):
    z = h @ w_in
    lead = z.shape[:-1]
    q = z[..., :QK_WIDTH].reshape(*lead, N_HEADS_A, 2, DK)
    k = z[..., QK_WIDTH:2 * QK_WIDTH].reshape(*lead, N_HEADS_A, 2, DK)
    v = z[..., 2 * QK_WIDTH:2 * QK_WIDTH + A_WIDTH].reshape(*lead, N_HEADS_A, DV)
    uv = jax.nn.gelu(z[..., 2 * QK_WIDTH + A_WIDTH:])
    u = uv[..., :B_WIDTH].reshape(*lead, N_GROUPS_B, C_B)
    gv = uv[..., B_WIDTH:].reshape(*lead, N_GROUPS_B, C_B)
    return partial_rope(q, pos), partial_rope(k, pos), v, u, gv

def diff_lambda(lam_p, lam_init):
    lp = lam_p.astype(jnp.float32)
    return jnp.exp(jnp.sum(lp[0] * lp[1])) - jnp.exp(jnp.sum(lp[2] * lp[3])) + lam_init

def diff_attn_prompt(q, k, v, lam):
    b, s = q.shape[:2]
    n_qb = s // Q_BLOCK
    scale = DK ** -0.5
    qb = q.reshape(b, n_qb, Q_BLOCK, N_HEADS_A, 2, DK).transpose(1, 0, 2, 3, 4, 5)
    kpos = jnp.arange(s)

    def block(args):
        qi, i = args
        sc = jnp.einsum('bqhmd,bkhmd->bhmqk', qi, k, preferred_element_type=jnp.float32) * scale
        qpos = i * Q_BLOCK + jnp.arange(Q_BLOCK)
        sc = jnp.where(kpos[None, :] <= qpos[:, None], sc, NEG)
        p = jax.nn.softmax(sc, axis=-1)
        a = (p[:, :, 0] - lam * p[:, :, 1]).astype(v.dtype)
        return jnp.einsum('bhqk,bkhe->bqhe', a, v)

    o = lax.map(block, (qb, jnp.arange(n_qb)))
    return o.transpose(1, 0, 2, 3, 4).reshape(b, s, N_HEADS_A, DV)

def diff_attn_sample(q, k_new, v_new, k_past, v_past, lam):
    ds = q.shape[1]
    n_past = k_past.shape[1]
    scale = DK ** -0.5
    s_past = jnp.einsum('bqhmd,bkhmd->bhmqk', q, k_past, preferred_element_type=jnp.float32) * scale
    s_new = jnp.einsum('bqhmd,bkhmd->bhmqk', q, k_new, preferred_element_type=jnp.float32) * scale
    causal = jnp.tril(jnp.ones((ds, ds), dtype=bool))
    s_new = jnp.where(causal, s_new, NEG)
    p = jax.nn.softmax(jnp.concatenate([s_past, s_new], axis=-1), axis=-1)
    a = (p[:, :, 0] - lam * p[:, :, 1]).astype(v_new.dtype)
    return (jnp.einsum('bhqk,bkhe->bqhe', a[..., :n_past], v_past)
            + jnp.einsum('bhqk,bkhe->bqhe', a[..., n_past:], v_new))

def diff_head_out(o, g_attn, lam_init):
    o = rms_norm(o, g_attn) * (1 - lam_init)
    return o.reshape(*o.shape[:-2], A_WIDTH)

def chunk_spatial_gate(u, gv, g_v, g_mlp, w_s, b_s, chunk_len):
    n, s = u.shape[:2]
    nc = s // chunk_len
    u = u.reshape(n, nc, chunk_len, N_GROUPS_B, C_B)
    v = rms_norm(gv.reshape(n, nc, chunk_len, N_GROUPS_B, C_B), g_v.reshape(N_GROUPS_B, C_B))
    ws = (w_s * jnp.tril(jnp.ones((CHUNK, CHUNK), w_s.dtype)))[:, :chunk_len, :chunk_len]
    mixed = jnp.einsum('gts,bnsgc->bntgc', ws, v) + b_s[:, :chunk_len].T[None, None, :, :, None]
    out = rms_norm(u * mixed, g_mlp.reshape(N_GROUPS_B, C_B))
    return out.reshape(n, s, B_WIDTH), v.reshape(n, s, B_WIDTH)

def routed_experts(t, expert, gate, w_eg, w_eu, w_ed):
    n_tok = t.shape[0]
    n_asg = n_tok * TOP_K
    flat_e = expert.reshape(-1)
    flat_tok = jnp.arange(n_asg, dtype=jnp.int32) // TOP_K
    flat_w = gate.reshape(-1)
    order = jnp.argsort(flat_e)
    se = flat_e[order]
    counts = jnp.bincount(flat_e, length=N_EXPERTS)
    padded = ((counts + EXPERT_BLOCK - 1) // EXPERT_BLOCK) * EXPERT_BLOCK
    pend = jnp.cumsum(padded)
    pstart = pend - padded
    start = jnp.cumsum(counts) - counts
    dest = pstart[se] + jnp.arange(n_asg) - start[se]
    n_blocks = (n_asg + N_EXPERTS * (EXPERT_BLOCK - 1) + EXPERT_BLOCK - 1) // EXPERT_BLOCK
    n_rows = n_blocks * EXPERT_BLOCK
    row_tok = jnp.full((n_rows,), n_tok, jnp.int32).at[dest].set(flat_tok[order])
    row_w = jnp.zeros((n_rows,), jnp.float32).at[dest].set(flat_w[order])
    block_e = jnp.minimum(jnp.searchsorted(pend, jnp.arange(n_blocks) * EXPERT_BLOCK, side='right'),
                          N_EXPERTS - 1)
    x_pad = jnp.concatenate([t, jnp.zeros((1, D_MODEL), t.dtype)], axis=0)
    xb = x_pad[row_tok].reshape(n_blocks, EXPERT_BLOCK, D_MODEL)

    def expert_block(args):
        xblk, e = args
        return (jax.nn.silu(xblk @ w_eg[e]) * (xblk @ w_eu[e])) @ w_ed[e]

    yb = lax.map(expert_block, (xb, block_e)).reshape(n_rows, D_MODEL)
    out = jnp.zeros((n_tok + 1, D_MODEL), t.dtype).at[row_tok].add(yb * row_w[:, None].astype(yb.dtype))
    return out[:n_tok]

def hier_moe(h, w_rg, b_rg, w_re, b_re, w_eg, w_eu, w_ed):
    lead = h.shape[:-1]
    t = h.reshape(-1, D_MODEL)
    n_tok = t.shape[0]
    g_prob = jax.nn.softmax((t @ w_rg + b_rg).astype(jnp.float32), axis=-1)
    g_p, g_idx = lax.top_k(g_prob, 1)
    e_logits = (t @ w_re + b_re).astype(jnp.float32).reshape(n_tok, N_EXPERT_GROUPS, EXPERTS_PER_GROUP)
    e_logits = e_logits[jnp.arange(n_tok), g_idx[:, 0]]
    e_top, e_idx = lax.top_k(e_logits, TOP_K)
    gate = jax.nn.softmax(e_top, axis=-1) * g_p
    expert = g_idx * EXPERTS_PER_GROUP + e_idx
    y = routed_experts(t, expert, gate, w_eg, w_eu, w_ed)
    return y.reshape(*lead, D_MODEL)

def decoder_layer(x, c, pos, chunk_len, attend, lam, lam_init, p):
    mod = jnp.split(jax.nn.silu(c) @ p['w_ada'] + p['b_ada'], 6, axis=-1)
    h = modulate(x, p['g_norm1'], mod[0], mod[1])
    q, k, v, u, gv = project_in(h, p['w_in'], pos)
    o_a = diff_head_out(attend(q, k, v, lam), p['g_attn'], lam_init)
    o_b, v_rows = chunk_spatial_gate(u, gv, p['g_v'], p['g_mlp'], p['w_s'], p['b_s'], chunk_len)
    mix = jnp.concatenate([o_a, o_b], axis=-1) @ p['w_out']
    x = x + mod[2][:, None, :] * mix
    h2 = modulate(x, p['g_norm2'], mod[3], mod[4])
    ff = hier_moe(h2, p['w_router_g'], p['b_router_g'], p['w_router_e'], p['b_router_e'],
                  p['w_exp_gate'], p['w_exp_up'], p['w_exp_down'])
    x = x + mod[5][:, None, :] * ff
    return x, k, v, v_rows

def setup_inputs(seed: int = 0) -> dict:
    key = jax.random.key(seed)
    ks = jax.random.split(key, 32)
    n_pages = PAST_LEN // PAGE_SIZE
    n_used = DEC_BATCH * n_pages
    n_pool = n_used + n_used // 4
    f32 = jnp.float32

    def nrm(k, shape, s):
        return jax.random.normal(k, shape, f32) * s

    def gain(k, shape):
        return 1.0 + 0.1 * jax.random.normal(k, shape, f32)

    page_table = jax.random.permutation(ks[4], n_pool)[:n_used].reshape(DEC_BATCH, n_pages).astype(jnp.int32)
    return {
        "x_prompt": nrm(ks[0], (BATCH, SEQ, D_MODEL), 1.0),
        "x_sample": nrm(ks[1], (DEC_BATCH, DEC_SEQ, D_MODEL), 1.0),
        "cache_k": nrm(ks[2], (DEPTH, n_pool, PAGE_SIZE, N_HEADS_A, 2, DK), 1.0),
        "cache_v": nrm(ks[3], (DEPTH, n_pool, PAGE_SIZE, N_HEADS_A, DV), 1.0),
        "page_table": page_table,
        "c_prompt": nrm(ks[5], (BATCH, D_MODEL), 1.0),
        "c_sample": nrm(ks[6], (DEC_BATCH, D_MODEL), 1.0),
        "w_ada": nrm(ks[7], (DEPTH, D_MODEL, 6 * D_MODEL), D_MODEL ** -0.5),
        "b_ada": nrm(ks[8], (DEPTH, 6 * D_MODEL), 0.02),
        "g_norm1": gain(ks[9], (DEPTH, D_MODEL)),
        "w_in": nrm(ks[10], (DEPTH, D_MODEL, IN_WIDTH), D_MODEL ** -0.5),
        "lam_p": nrm(ks[11], (DEPTH, 4, DK), 0.1),
        "g_attn": gain(ks[12], (DEPTH, N_HEADS_A, DV)),
        "g_v": gain(ks[13], (DEPTH, B_WIDTH)),
        "w_s": nrm(ks[14], (DEPTH, N_GROUPS_B, CHUNK, CHUNK), CHUNK ** -0.5),
        "b_s": gain(ks[15], (DEPTH, N_GROUPS_B, CHUNK)),
        "g_mlp": gain(ks[16], (DEPTH, B_WIDTH)),
        "w_out": nrm(ks[17], (DEPTH, D_MODEL, D_MODEL), D_MODEL ** -0.5),
        "g_norm2": gain(ks[18], (DEPTH, D_MODEL)),
        "w_router_g": nrm(ks[19], (DEPTH, D_MODEL, N_EXPERT_GROUPS), D_MODEL ** -0.5),
        "b_router_g": nrm(ks[20], (DEPTH, N_EXPERT_GROUPS), 0.01),
        "w_router_e": nrm(ks[21], (DEPTH, D_MODEL, N_EXPERTS), D_MODEL ** -0.5),
        "b_router_e": nrm(ks[22], (DEPTH, N_EXPERTS), 0.01),
        "w_exp_gate": nrm(ks[23], (DEPTH, N_EXPERTS, D_MODEL, D_EXPERT), D_MODEL ** -0.5),
        "w_exp_up": nrm(ks[24], (DEPTH, N_EXPERTS, D_MODEL, D_EXPERT), D_MODEL ** -0.5),
        "w_exp_down": nrm(ks[25], (DEPTH, N_EXPERTS, D_EXPERT, D_MODEL), D_EXPERT ** -0.5),
        "g_final": gain(ks[26], (D_MODEL,)),
    }

def reference(x_prompt, x_sample, cache_k, cache_v, page_table, c_prompt, c_sample,
              w_ada, b_ada, g_norm1, w_in, lam_p, g_attn, g_v, w_s, b_s, g_mlp, w_out,
              g_norm2, w_router_g, b_router_g, w_router_e, b_router_e,
              w_exp_gate, w_exp_up, w_exp_down, g_final):
    n_seq_p = x_prompt.shape[1]
    n_seq_s = x_sample.shape[1]
    n_dec = x_sample.shape[0]
    pos_p = jnp.arange(n_seq_p)
    pos_s = PAST_LEN + jnp.arange(n_seq_s)
    xp, xs = x_prompt, x_sample
    kp_l, vp_l, ks_l, vs_l, cv_l = [], [], [], [], []
    for l in range(DEPTH):
        lam_init = 0.8 - 0.6 * math.exp(-0.3 * l)
        lam = diff_lambda(lam_p[l], lam_init)
        p = {
            'w_ada': w_ada[l], 'b_ada': b_ada[l], 'g_norm1': g_norm1[l], 'w_in': w_in[l],
            'g_attn': g_attn[l], 'g_v': g_v[l], 'w_s': w_s[l], 'b_s': b_s[l], 'g_mlp': g_mlp[l],
            'w_out': w_out[l], 'g_norm2': g_norm2[l],
            'w_router_g': w_router_g[l], 'b_router_g': b_router_g[l],
            'w_router_e': w_router_e[l], 'b_router_e': b_router_e[l],
            'w_exp_gate': w_exp_gate[l], 'w_exp_up': w_exp_up[l], 'w_exp_down': w_exp_down[l],
        }
        xp, k_p, v_p, _ = decoder_layer(xp, c_prompt, pos_p, CHUNK, diff_attn_prompt, lam, lam_init, p)
        k_past = cache_k[l][page_table].reshape(n_dec, -1, N_HEADS_A, 2, DK)
        v_past = cache_v[l][page_table].reshape(n_dec, -1, N_HEADS_A, DV)

        def attend_sample(q, k, v, lam_, k_past=k_past, v_past=v_past):
            return diff_attn_sample(q, k, v, k_past, v_past, lam_)

        xs, k_s, v_s, cv_s = decoder_layer(xs, c_sample, pos_s, n_seq_s, attend_sample, lam, lam_init, p)
        kp_l.append(k_p)
        vp_l.append(v_p)
        ks_l.append(k_s)
        vs_l.append(v_s)
        cv_l.append(cv_s)
    y_prompt = rms_norm(xp, g_final)
    y_sample = rms_norm(xs, g_final)
    k_prompt = jnp.stack(kp_l)
    v_prompt = jnp.stack(vp_l)
    k_sample = jnp.stack(ks_l)
    v_sample = jnp.stack(vs_l)
    chunk_v_sample = jnp.stack(cv_l)
    return (y_prompt, y_sample, k_prompt, v_prompt, k_sample, v_sample, chunk_v_sample)


_drawn_inputs = setup_inputs


def setup_inputs(seed=0):
    import zlib

    import numpy as np

    out = dict(_drawn_inputs(seed))
    spreads = {}
    factors = {'b_router_g': 3.659, 'b_router_e': 4.988}
    for name, (base, spread) in spreads.items():
        noise = np.random.default_rng([zlib.crc32(name.encode()), seed]).standard_normal(out[name].shape)
        drawn = base * np.exp(spread * noise) if base else spread * noise
        out[name] = __import__('jax').numpy.asarray(drawn.astype(out[name].dtype))
    for name, factor in factors.items():
        out[name] = (out[name] * factor).astype(out[name].dtype)
    return out
```

```python
import math
from contextlib import ExitStack

import numpy as np
import concourse.bass as bass
from concourse import mybir

F32 = mybir.dt.float32
I32 = mybir.dt.int32
ALU = mybir.AluOpType
ACT = mybir.ActivationFunctionType
AX = mybir.AxisListType
ds = bass.ds

P = 128
D = 1024
KD = D // P
SEQ = 2048
NT = SEQ // P
DB, DQ = 8, 8
ST = DB * DQ
PAST, PAGE = 8192, 128
NPG = PAST // PAGE
H, DK, DV = 4, 64, 128
AW = H * DV
QKW = H * 2 * DK
BW = D - AW
GB = 4
ROT = DK // 4
INW = 2 * QKW + AW + 2 * BW
NEG_G, EPG = 4, 8
NE = NEG_G * EPG
DE = 512
EPS = 1e-6
NEG = -1e30
LAM_INIT = 0.8 - 0.6 * math.exp(0.0)
SCALE = DK ** -0.5
NTOK = SEQ + ST
NB = (2 * NTOK + NE * (P - 1)) // P
MOD_SHIFT1, MOD_GAIN1, MOD_GATE1, MOD_SHIFT2, MOD_GAIN2, MOD_GATE2 = range(6)


def waited(eng, sem, value):
    if not isinstance(value, int) or value > 0:
        eng.wait_ge(sem, value)


def stage_semaphore(nc, used, name):
    used.append(nc.alloc_semaphore(name=name))
    return used[-1]


class Chain:

    def __init__(self, eng, sem, base=0):
        self.eng, self.sem, self.base, self.n = eng, sem, base, 0

    def step(self, ins):
        ins.then_inc(self.sem, 1)
        self.n += 1

    def wait(self):
        self.eng.wait_ge(self.sem, self.base + self.n)

    def link(self, ins):
        self.step(ins)
        self.wait()


def modulation(nc, io, mod_dram, ident, sel, room, used):
    with ExitStack() as ctx:
        def sb(name, shape, dt=F32):
            return ctx.enter_context(nc.sbuf_tensor(name, shape, dt))

        def sem(name):
            return stage_semaphore(nc, used, name)

        NC9 = 1 + DB
        CH = 6 * D // 512
        c_rows = sb("c_rows", [NC9, D])
        c_silu = sb("c_silu", [NC9, D])
        c_T = sb("c_T", [P, KD, NC9])
        w_ring = room.rearrange("p h t -> p (h t)").rearrange("p (r k n) -> p r k n", r=2, k=KD)
        b_rows = sb("b_ada_rows", [NC9, 2, 512])
        gains = sb("mod_gains", [P, 2, D])
        m_row = sb("mod_row", [NC9, 2, 512])
        spread = sb("mod_spread", [P, 2, 2, 512])
        ps_t = ctx.enter_context(nc.psum_tensor("mod_ps_t", [P, KD, 16], F32))
        ps_m = ctx.enter_context(nc.psum_tensor("mod_ps_m", [P, 2, 512], F32))
        ps_s = ctx.enter_context(nc.psum_tensor("mod_ps_s", [P, 2, 2, 512], F32))
        c_in = sem("c_in")
        g_in = sem("mod_g_in")
        w_in = [sem("w_ada_in0"), sem("w_ada_in1")]
        b_in = [sem("b_ada_in0"), sem("b_ada_in1")]
        silu_done = sem("silu_done")
        ct_done = sem("ct_done")
        ct_ready = sem("ct_ready")
        row_done = sem("mod_row_done")
        row_ready = sem("mod_row_ready")
        spread_done = sem("spread_done")
        spread_ready = sem("spread_ready")
        stored = [sem("mod_stored0"), sem("mod_stored1")]
        w_dram = io["w_ada"][0].rearrange("(k p) n -> p k n", p=P)
        with nc.Block() as block:
            @block.sync
            def _(sp):
                sp.dma_start(c_rows[0:1, :], io["c_prompt"]).then_inc(c_in, 16)
                sp.dma_start(c_rows[1:NC9, :], io["c_sample"]).then_inc(c_in, 16)
                sp.dma_start(gains[:, 0, :], io["g_norm1"].broadcast_to([P, D])).then_inc(g_in, 16)
                sp.dma_start(gains[:, 1, :], io["g_norm2"].broadcast_to([P, D])).then_inc(g_in, 16)
                for c in range(CH):
                    if c >= 2:
                        sp.wait_ge(row_done, c - 1)
                    sp.dma_start(w_ring[:, c % 2], w_dram[:, :, c * 512:(c + 1) * 512]).then_inc(w_in[c % 2], 16)
                    if c >= 2:
                        sp.wait_ge(row_ready, c - 1)
                    sp.dma_start(b_rows[:, c % 2, :],
                                 io["b_ada"][:, c * 512:(c + 1) * 512].broadcast_to([NC9, 512])).then_inc(b_in[c % 2], 16)

            @block.tensor
            def _(pe):
                pe.wait_ge(silu_done, 1)
                for k in range(KD):
                    last = pe.transpose(ps_t[:, k, 0:NC9], c_silu[:, k * P:(k + 1) * P], ident[0:NC9, 0:NC9])
                last.then_inc(ct_done, 1)
                pe.wait_ge(ct_ready, 1)
                for c in range(CH + 1):
                    if c < CH:
                        pe.wait_ge(w_in[c % 2], 16 * (c // 2 + 1))
                        if c >= 2:
                            pe.wait_ge(row_ready, c - 1)
                        for k in range(KD):
                            last = pe.matmul(ps_m[0:NC9, c % 2, :], c_T[:, k, :], w_ring[:, c % 2, k, :],
                                             start=(k == 0), stop=(k == KD - 1))
                        last.then_inc(row_done, 1)
                    if c >= 1:
                        pe.wait_ge(row_ready, c)
                        if c >= 3:
                            pe.wait_ge(spread_ready, c - 2)
                        b = (c - 1) % 2
                        pe.matmul(ps_s[:, b, 0, :], sel[:, 0:P], m_row[:, b, :], start=True, stop=True)
                        pe.matmul(ps_s[:, b, 1, :], sel[:, P:2 * P], m_row[:, b, :],
                                  start=True, stop=True).then_inc(spread_done, 1)

            @block.scalar
            def _(act):
                act.wait_ge(c_in, 32)
                nc.scalar.activation(c_silu[:], c_rows[:], ACT.Silu).then_inc(silu_done, 1)
                for c in range(CH):
                    act.wait_ge(spread_ready, c + 1)
                    part, half = c // 2, c % 2
                    act.dma_start(mod_dram[:, part, :, half * 512:(half + 1) * 512].rearrange("w p n -> p w n"),
                                  spread[:, c % 2]).then_inc(stored[c % 2], 16)
                act.wait_ge(stored[0], 16 * (CH // 2))
                act.wait_ge(stored[1], 16 * (CH // 2))

            @block.vector
            def _(dve):
                dve.wait_ge(ct_done, 1)
                nc.vector.tensor_copy(c_T[:], ps_t[:, :, 0:NC9]).then_inc(ct_ready, 1)
                for c in range(CH + 1):
                    if c < CH:
                        dve.wait_ge(row_done, c + 1)
                        dve.wait_ge(b_in[c % 2], 16 * (c // 2 + 1))
                        if c >= 2:
                            dve.wait_ge(spread_done, c - 1)
                        nc.vector.tensor_tensor(m_row[:, c % 2, :], ps_m[0:NC9, c % 2, :], b_rows[:, c % 2, :],
                                                ALU.add).then_inc(row_ready, 1)
                    if c >= 1:
                        j = c - 1
                        part, half = j // 2, j % 2
                        dve.wait_ge(spread_done, j + 1)
                        dve.wait_ge(g_in, 32)
                        if j >= 2:
                            dve.wait_ge(stored[j % 2], 16 * (j // 2))
                        if part in (MOD_GAIN1, MOD_GAIN2):
                            g = gains[:, part // 3, half * 512:(half + 1) * 512]
                            nc.vector.scalar_tensor_tensor(out=spread[:, j % 2, 0, :], in0=ps_s[:, j % 2, 0, :], scalar=1.0,
                                                           in1=g, op0=ALU.add, op1=ALU.mult)
                            nc.vector.scalar_tensor_tensor(out=spread[:, j % 2, 1, :], in0=ps_s[:, j % 2, 1, :], scalar=1.0,
                                                           in1=g, op0=ALU.add, op1=ALU.mult).then_inc(spread_ready, 1)
                        else:
                            nc.vector.tensor_copy(spread[:, j % 2], ps_s[:, j % 2]).then_inc(spread_ready, 1)


def front(nc, io, out, dram, mem):
    with ExitStack() as ctx:
        def sb(name, shape, dt=F32):
            return ctx.enter_context(nc.sbuf_tensor(name, shape, dt))

        def sem(name):
            return stage_semaphore(nc, used, name)

        ident, used = mem["ident"], mem["used_semaphores"]
        w = mem["w_in"]
        kT, V = mem["kT"], mem["V"]
        kT_new, V_new, qT_new, obT_new = mem["kT_new"], mem["V_new"], mem["qT_new"], mem["obT_new"]
        gain = sb("gain1", [P, D])
        shift = sb("shift1", [P, D])
        g_v = sb("g_v_b", [P, BW])
        g_mlp = sb("g_mlp_b", [P, BW])
        x = sb("x_in", [P, D])
        h = sb("h", [P, D])
        hT = sb("hT", [P, KD, P])
        qk = sb("qk", [P, 2 * QKW])
        r1 = sb("rope_t1", [P, 16, 2, ROT // 2])
        r2 = sb("rope_t2", [P, 16, 2, ROT // 2])
        u = sb("u", [P, BW])
        gv = sb("gv", [P, BW])
        sq = sb("sq", [P, BW])
        vn = sb("vn", [P, BW])
        ob = sb("ob", [P, BW])
        qT = sb("qT", [P, H, P])
        obT = sb("obT", [P, GB, P])
        st = sb("stats", [P, 32])
        eps = mem["eps"]
        wsT = [mem["wsT_s"], mem["wsT_p"]]
        bs = [mem["bs_s"], mem["bs_p"]]
        z = ctx.enter_context(nc.psum_tensor("z", [P, 5, 512], F32))
        tr = ctx.enter_context(nc.psum_tensor("tr", [P, 8, P], F32))
        mix = ctx.enter_context(nc.psum_tensor("mix", [P, GB, P], F32))
        ZQ, ZK, ZV, ZU, ZG = range(5)

        par_in = sem("front_params_in")
        par_p_in = sem("front_prompt_mod_in")
        held_sp = sem("front_held_sp")
        held_pool = sem("front_held_pool")
        held_act = sem("front_held_act")
        x_in = sem("x_in_sem")
        rope_in = [sem("rope_in0"), sem("rope_in1")]
        x_ss = sem("x_ss")
        x_std = sem("x_std")
        h_ready = sem("h_ready")
        hT_done = sem("hT_done")
        hT_ready = sem("hT_ready")
        z_done = [sem(f"z_done{i}") for i in range(5)]
        gv_ready = sem("gv_ready")
        u_ready = sem("u_ready")
        gv_ss = sem("gv_ss")
        gv_std = sem("gv_std")
        vn_ready = sem("vn_ready")
        mix_done = sem("mix_done")
        ob_ss = sem("ob_ss")
        ob_std = sem("ob_std")
        ob_ready = sem("ob_ready")
        qk_copied = sem("qk_copied")
        qk_ready = sem("qk_ready")
        v_ready = sem("v_ready")
        qkT_done = sem("qkT_done")
        obT_done = sem("obT_done")
        qT_ready = sem("qT_ready")
        kT_ready = sem("kT_ready")
        obT_ready = sem("obT_ready")
        k_out = sem("k_out")
        v_out = sem("v_out")
        cv_out = sem("cv_out")
        q_out = sem("q_out")
        ob_out = sem("ob_out")
        own = sem("front_dve_own")

        def each_tile(eng, step):
            step(0, None, ST, False)
            step(1, 0, P, False)
            with eng.Fori(1, NT - 1) as p:
                step(p + 1, p, P, False)
            step(NT, NT - 1, P, True)

        with nc.Block() as block:
            @block.sync
            def _(sp):
                sp.dma_start(gain[:], dram["mod"][1, MOD_GAIN1]).then_inc(par_in, 16)
                sp.dma_start(shift[:], dram["mod"][1, MOD_SHIFT1]).then_inc(par_in, 16)
                sp.dma_start(g_v[:], io["g_v"].broadcast_to([P, BW])).then_inc(par_in, 16)
                sp.dma_start(g_mlp[:], io["g_mlp"].broadcast_to([P, BW])).then_inc(par_in, 16)
                sp.dma_start(x[0:ST, :], io["x_sample"].rearrange("b q d -> (b q) d")).then_inc(x_in, 16)

                def step(n, p, R, last):
                    if not last:
                        sp.wait_ge(h_ready, n + 1)
                        nxt = 0 if p is None else p + 1
                        if p is None:
                            sp.dma_start(gain[:], dram["mod"][0, MOD_GAIN1]).then_inc(par_p_in, 16)
                            sp.dma_start(shift[:], dram["mod"][0, MOD_SHIFT1]).then_inc(par_p_in, 16)
                        sp.sem_inc(held_sp, 1)
                        sp.dma_start(x[:], io["x_prompt"][0, ds(nxt * P, P), :]).then_inc(x_in, 16)
                each_tile(sp, step)

            @block.gpsimd
            def _(pool):
                def step(n, p, R, last):
                    if p is not None:
                        pool.wait_ge(qk_ready, n + 1)
                        pool.sem_inc(held_pool, 1)
                        pool.dma_start(out["k_prompt"][ds(p * P, P), :], qk[:, QKW:2 * QKW]).then_inc(k_out, 16)
                        pool.wait_ge(v_ready, n + 1)
                        pool.sem_inc(held_pool, 1)
                        pool.dma_start(out["v_prompt"][ds(p * P, P), :], V[:, ds(p, 1), :]).then_inc(v_out, 16)
                        pool.wait_ge(qT_ready, n + 1)
                        pool.sem_inc(held_pool, 1)
                        pool.dma_start(dram["qT"][ds(p, 1)], qT[:]).then_inc(q_out, 16)
                        pool.wait_ge(obT_ready, n + 1)
                        pool.sem_inc(held_pool, 1)
                        pool.dma_start(dram["obT"][ds(p, 1)], obT[:]).then_inc(ob_out, 16)
                        pool.wait_ge(k_out, (n + 1) * 16)
                        pool.wait_ge(v_out, (n + 1) * 16)
                        pool.wait_ge(q_out, n * 16)
                        pool.wait_ge(ob_out, n * 16)
                    else:
                        pool.wait_ge(vn_ready, 1)
                        pool.dma_start(out["cv_sample"], vn[0:ST, :]).then_inc(cv_out, 16)
                        pool.wait_ge(qk_ready, 1)
                        pool.dma_start(out["k_sample"], qk[0:ST, QKW:2 * QKW]).then_inc(k_out, 16)
                        pool.wait_ge(v_ready, 1)
                        pool.dma_start(out["v_sample"], V_new[:]).then_inc(v_out, 16)
                        pool.wait_ge(cv_out, 16)
                        pool.wait_ge(k_out, 16)
                        pool.wait_ge(v_out, 16)
                each_tile(pool, step)

            @block.tensor
            def _(pe):
                def transpose_h(n, R):
                    pe.wait_ge(h_ready, n + 1)
                    for k in range(KD):
                        last = pe.transpose(z[:, ZQ + k // 4, (k % 4) * P:(k % 4) * P + R], h[0:R, k * P:(k + 1) * P],
                                            ident[0:R, 0:R])
                    last.then_inc(hT_done, 1)

                def step(n, p, R, last_tile):
                    who = int(p is not None)
                    pe.wait_ge(hT_ready, n + 1)
                    for c in (ZG, ZU, ZQ, ZK, ZV):
                        if c == ZG:
                            waited(pe, gv_ready, n)
                        if c == ZU:
                            waited(pe, u_ready, n)
                        if c == ZV:
                            waited(pe, v_ready, n)
                        for k in range(KD):
                            last = pe.matmul(z[0:R, c, :], hT[:, k, 0:R], w[:, k, c * 512:(c + 1) * 512],
                                             start=(k == 0), stop=(k == KD - 1))
                        last.then_inc(z_done[c], 1)
                        if c == ZK:
                            pe.wait_ge(vn_ready, n + 1)
                            waited(pe, obT_ready, n)
                            for g in range(GB):
                                last = pe.matmul(mix[0:R, g, :], wsT[who][0:R, g, 0:R], vn[0:R, g * P:(g + 1) * P],
                                                 start=True, stop=True)
                            last.then_inc(mix_done, 1)
                    if not last_tile:
                        pe.wait_ge(qk_ready, n + 1)
                        transpose_h(n + 1, P)
                    pe.wait_ge(qk_ready, n + 1)
                    waited(pe, kT_ready, n)
                    for b in range(8):
                        last = pe.transpose(tr[:, b, 0:R], qk[0:R, b * P:(b + 1) * P], ident[0:R, 0:R])
                    last.then_inc(qkT_done, 1)
                    pe.wait_ge(ob_ready, n + 1)
                    for b in range(GB):
                        last = pe.transpose(mix[:, b, 0:R], ob[0:R, b * P:(b + 1) * P], ident[0:R, 0:R])
                    last.then_inc(obT_done, 1)

                pe.wait_ge(mem["w_in_sem"], mem["w_in_count"])
                transpose_h(0, ST)
                each_tile(pe, step)

            @block.scalar
            def _(act):
                def root(done, ready, n, R, s, cnt, width):
                    act.wait_ge(done, n + 1)
                    nc.scalar.activation(st[0:R, s + 8:s + 8 + cnt], st[0:R, s:s + cnt], ACT.Sqrt,
                                         bias=eps[0:R, 0:1], scale=1.0 / width).then_inc(ready, 1)

                def hT_copy(n, R):
                    act.wait_ge(hT_done, n + 1)
                    nc.scalar.activation(hT[:, :, 0:R],
                                         z[:, ZQ:ZQ + 2, :].rearrange("p a (b r) -> p (a b) r", r=P)[:, :, 0:R],
                                         ACT.Copy).then_inc(hT_ready, 1)

                def step(n, p, R, last):
                    act.wait_ge(z_done[ZG], n + 1)
                    nc.scalar.activation(gv[0:R, :], z[0:R, ZG, :], ACT.Gelu_apprx_tanh).then_inc(gv_ready, 1)
                    act.wait_ge(z_done[ZU], n + 1)
                    waited(act, ob_ready, n)
                    nc.scalar.activation(u[0:R, :], z[0:R, ZU, :], ACT.Gelu_apprx_tanh).then_inc(u_ready, 1)
                    root(gv_ss, gv_std, n, R, 0, GB, P)
                    act.wait_ge(z_done[ZK], n + 1)
                    waited(act, qkT_done, n)
                    waited(act, k_out, 16 * n)
                    nc.scalar.activation(qk[0:R, :], z[0:R, ZQ:ZQ + 2, :].rearrange("p a b -> p (a b)"),
                                         ACT.Copy).then_inc(qk_copied, 1)
                    if not last:
                        root(x_ss, x_std, n + 1, P, 4, 1, D)
                    act.wait_ge(z_done[ZV], n + 1)
                    act.sem_inc(held_act, 1)
                    dst = V_new[:] if p is None else V[:, ds(p, 1), :]
                    nc.scalar.activation(dst, z[0:R, ZV, :], ACT.Copy).then_inc(v_ready, 1)
                    root(ob_ss, ob_std, n, R, 16, GB, P)
                    if not last:
                        hT_copy(n + 1, P)
                    act.wait_ge(qkT_done, n + 1)
                    waited(act, q_out, 16 * (n - 1))
                    nc.scalar.activation((qT_new if p is None else qT)[:, :, 0:R], tr[:, 0:4, 0:R],
                                         ACT.Copy).then_inc(qT_ready, 1)
                    dst = kT_new[:] if p is None else kT[:, :, ds(p * P, P)]
                    nc.scalar.activation(dst, tr[:, 4:8, 0:R], ACT.Copy).then_inc(kT_ready, 1)
                    act.wait_ge(obT_done, n + 1)
                    waited(act, ob_out, 16 * (n - 1))
                    nc.scalar.activation((obT_new if p is None else obT)[:, :, 0:R], mix[:, :, 0:R],
                                         ACT.Copy).then_inc(obT_ready, 1)

                root(x_ss, x_std, 0, ST, 4, 1, D)
                hT_copy(0, ST)
                each_tile(act, step)

            LINKS = 14

            @block.vector
            def _(dve):
                v = nc.vector

                def norm_x(n, R, chain):
                    dve.wait_ge(x_in, 16 * (n + 1))
                    if isinstance(n, int) and n == 1:
                        dve.wait_ge(par_p_in, 32)
                    v.tensor_tensor_reduce(out=h[0:R, :], in0=x[0:R, :], in1=x[0:R, :], scale=1.0, scalar=0.0,
                                           op0=ALU.mult, op1=ALU.add, accum_out=st[0:R, 4:5]).then_inc(x_ss, 1)
                    dve.wait_ge(x_std, n + 1)
                    chain.link(v.reciprocal(st[0:R, 5:6], st[0:R, 12:13]))
                    chain.link(v.scalar_tensor_tensor(out=h[0:R, :], in0=x[0:R, :], scalar=st[0:R, 5:6],
                                                      in1=gain[0:R, :], op0=ALU.mult, op1=ALU.mult))
                    v.tensor_tensor(h[0:R, :], h[0:R, :], shift[0:R, :], ALU.add).then_inc(h_ready, 1)

                def group_norm(src, dst, gains, R, s, ss, std, done, n, chain):
                    g3 = "p (g c) -> p g c"
                    chain.link(v.tensor_tensor(sq[0:R, :], src[0:R, :], src[0:R, :], ALU.mult))
                    v.tensor_reduce(st[0:R, s:s + GB], sq[0:R, :].rearrange(g3, g=GB), AX.X, ALU.add).then_inc(ss, 1)
                    dve.wait_ge(std, n + 1)
                    chain.link(v.reciprocal(st[0:R, 28:28 + GB], st[0:R, s + 8:s + 8 + GB]))
                    chain.link(v.tensor_tensor(sq[0:R, :].rearrange(g3, g=GB), src[0:R, :].rearrange(g3, g=GB),
                                               st[0:R, 28:28 + GB].unsqueeze(2).to_broadcast([R, GB, P]), ALU.mult))
                    v.tensor_tensor(dst[0:R, :], sq[0:R, :], gains[0:R, :], ALU.mult).then_inc(done, 1)

                def step(n, p, R, last):
                    who = int(p is not None)
                    chain = Chain(dve, own, n * LINKS + 2)
                    waited(dve, cv_out, 16 if not isinstance(n, int) or n else 0)
                    dve.wait_ge(gv_ready, n + 1)
                    group_norm(gv, vn, g_v, R, 0, gv_ss, gv_std, vn_ready, n, chain)
                    dve.wait_ge(qk_copied, n + 1)
                    zz = qk[0:R, :].rearrange("p (m d) -> p m d", d=DK)
                    hr = ROT // 2
                    tab = rope_at(n, R)
                    chain.step(v.tensor_tensor(r1[0:R], zz[:, :, 0:hr].unsqueeze(2).to_broadcast([R, 16, 2, hr]),
                                               tab(0), ALU.mult))
                    chain.link(v.tensor_tensor(r2[0:R], zz[:, :, hr:ROT].unsqueeze(2).to_broadcast([R, 16, 2, hr]),
                                               tab(1), ALU.mult))
                    v.tensor_tensor(qk[0:R, :].rearrange("p (m d) -> p m d", d=DK)[:, :, 0:ROT],
                                    r1[0:R].rearrange("p m t j -> p m (t j)"), r2[0:R].rearrange("p m t j -> p m (t j)"),
                                    ALU.add).then_inc(qk_ready, 1)
                    if not last:
                        dve.wait_ge(hT_done, n + 1)
                        norm_x(n + 1, P, chain)
                    dve.wait_ge(mix_done, n + 1)
                    dve.wait_ge(u_ready, n + 1)
                    waited(dve, obT_done, n)
                    for g in range(GB):
                        chain.step(v.scalar_tensor_tensor(out=u[0:R, g * P:(g + 1) * P], in0=mix[0:R, g, :],
                                                          scalar=bs[who][0:R, g:g + 1], in1=u[0:R, g * P:(g + 1) * P],
                                                          op0=ALU.add, op1=ALU.mult))
                    chain.wait()
                    group_norm(u, ob, g_mlp, R, 16, ob_ss, ob_std, ob_ready, n, chain)
                    assert chain.n == (LINKS if not last else LINKS - 2), chain.n

                def rope_at(n, R):
                    t = mem["rope"]
                    src = t[0:R, ds(n, 1)].rearrange("p o a t j -> p (o a) t j")
                    return lambda a: src[:, a].unsqueeze(1).to_broadcast([R, 16, 2, ROT // 2])

                dve.wait_ge(par_in, 64)
                norm_x(0, ST, Chain(dve, own, 0))
                each_tile(dve, step)
def constants():
    f = np.float32
    inv = (f(500000.0) ** (-np.arange(0, ROT, 2, dtype=f) / f(ROT))).astype(f)
    pos = np.zeros((NT + 1, P), f)
    pos[0, :ST] = PAST + np.arange(ST) % DQ
    pos[1:] = np.arange(SEQ).reshape(NT, P)
    ang = pos[:, :, None] * inv
    cos, sin = np.cos(ang), np.sin(ang)
    rope = np.stack([np.stack([cos, sin], 2), np.stack([-sin, cos], 2)], 2)
    t = np.arange(P)
    s = np.arange(ST)
    sel = np.zeros((1 + DB, 2 * P), f)
    sel[0, :P] = 1
    sel[1 + s // DQ, P + s] = 1
    same = s[:, None] // DQ == s[None, :] // DQ
    row = np.arange(P)
    rq, rm, used = row % DQ, (row // DQ) % 2, row % 32 < 2 * DQ
    key_b, key_q = s // DQ, s % DQ
    ok = (key_b[None, :, None] == np.arange(DB)[:, None, None]) & (key_q[None, :, None] <= rq[None, None, :])
    mask_new = np.where(ok.transpose(2, 0, 1), 0, NEG).astype(f)
    pick = np.zeros((P, DB, H, ST), f)
    for b in range(DB):
        for r in row[used]:
            pick[r, b, r // 32, DQ * b + rq[r]] = 1
    kk = np.arange(512)
    mask_p = np.where(kk[None, None, :] <= (np.arange(4)[None, :, None] * P + t[:, None, None]), 0, NEG).astype(f)
    e = np.arange(NE)
    return {
        "c_ident": np.eye(P, dtype=f),
        "c_rope": np.ascontiguousarray(rope.transpose(1, 0, 2, 3, 4)).astype(f),
        "c_tril": (t[None, :] <= t[:, None]).astype(f),
        "c_tril_s": (same & (s[None, :] <= s[:, None])).astype(f),
        "c_sel": sel,
        "c_mask_new": mask_new,
        "c_pick": pick,
        "c_coef": np.stack([(used & (rm == 0)), -1.0 * (used & (rm == 1))], 1).astype(f),
        "c_coef_p": np.tile(np.array([1, -1], f), (P, 1)),
        "c_mask_p": mask_p,
        "c_before": (t[:, None] < t[None, :]).astype(f),
        "c_iota": np.tile(np.arange(P, dtype=f), (P, 1)),
        "c_first": (e[None, :] < e[:, None]).astype(f).reshape(1, NE * NE),
        "c_tok": (np.arange(P)[:, None] + np.array([SEQ] + [P * i for i in range(NT)])[None, :]).astype(f),
    }


def decode(nc, io, dram, mem):
    with ExitStack() as ctx:
        def sb(name, shape, dt=F32):
            return ctx.enter_context(nc.sbuf_tensor(name, shape, dt))

        def sem(name):
            return ctx.enter_context(nc.semaphore(name))

        PS = 4
        STEPS = NPG // PS
        W = PS * PAGE
        CREDIT = 2
        ident = mem["ident"]
        kT_new, V_new, qT_new = mem["kT_new"], mem["V_new"], mem["qT_new"]
        table = sb("pages", [1, DB * NPG], I32)
        k_ring = sb("k_ring", [P, 2, PS, QKW])
        v_ring = sb("v_ring", [P, 2, PS, AW])
        kTs = sb("kTs", [P, 2, H, W])
        scores = sb("scores", [P, 2, PAST + ST])
        probs = sb("probs", [P, 2, W])
        probs_new = sb("probs_new", [P, ST])
        pT = sb("pT", [P, 2, PS, P])
        pT_new = sb("pT_new", [ST, P])
        q_cur = sb("q_cur", [P, H, 32])
        mask_new = sb("mask_new", [P, DB, ST])
        maxes = sb("maxes", [P, DB, STEPS + 1])
        sums = sb("sums", [P, DB, STEPS + 1])
        neg_max = sb("neg_max", [P, DB])
        top = sb("top", [P, 1])
        total = sb("total", [P, 2])
        coef = sb("coef", [P, 4])
        o_all = sb("o_all", [P, DB, DV])
        pick = k_ring[:, 0].rearrange("p j n -> p (j n)").rearrange("p (b h s) -> p b h s", b=DB, h=H)
        ps_k = ctx.enter_context(nc.psum_tensor("ps_k", [P, H, W], F32))
        ps_s = ctx.enter_context(nc.psum_tensor("ps_s", [P, 2, W], F32))
        ps_p = ctx.enter_context(nc.psum_tensor("ps_p", [P, PS, P], F32))
        ps_o = ctx.enter_context(nc.psum_tensor("ps_o", [P, 512], F32))

        params_in = sem("dec_params_in")
        table_in = sem("table_in")
        k_in = [sem("k_in0"), sem("k_in1")]
        v_in = [sem("v_in0"), sem("v_in1")]
        held_sp = sem("dec_held_sp")
        held_act = sem("dec_held_act")
        held_pe = sem("dec_held_pe")
        held_dve = sem("dec_held_dve")
        q_made = sem("q_made")
        q_ready = sem("q_ready")
        kT_done = [sem(f"dkT_done{h}") for h in range(H)]
        kT_kept = [sem(f"dkT_kept{h}") for h in range(H)]
        s_done = sem("s_done")
        s_kept = sem("s_kept")
        max_done = sem("max_done")
        max_new = sem("max_new")
        pick_in = sem("pick_in")
        picked = sem("picked")
        new_done = sem("new_done")
        new_kept = sem("new_kept")
        bias_ready = sem("bias_ready")
        e_new = sem("e_new")
        e_done = sem("e_done")
        pT_new_done = sem("pT_new_done")
        pT_new_kept = sem("pT_new_kept")
        pT_done = sem("pT_done")
        pT_kept = sem("pT_kept")
        pv_new = sem("pv_new")
        pv_done = sem("pv_done")
        o_kept = sem("o_kept")
        own = sem("dec_dve_own")

        def sequences(eng, k_start, k_step, v_start, v_step, v_end):
            k_start(0)
            with eng.Fori(0, STEPS // 2) as i:
                for u in range(2):
                    k_step(0, i, u)
            with eng.Fori(0, DB - 1) as b:
                k_start(b + 1)
                v_start(b)
                with eng.Fori(0, STEPS // 2) as i:
                    for u in range(2):
                        v_step(b, i, u)
                        k_step(b + 1, i, u)
                v_end(b)
            v_start(DB - 1)
            with eng.Fori(0, STEPS // 2) as i:
                for u in range(2):
                    v_step(DB - 1, i, u)
            v_end(DB - 1)

        CACHE = {"cache_k": "o p h m d -> p (o h m d)", "cache_v": "o p h e -> p (o h e)"}

        def nothing(*_):
            return None

        with nc.Block() as block:
            @block.sync
            def _(sp):
                sp.dma_start(table[:], io["page_table"].rearrange("(o b) n -> o (b n)", o=1)).then_inc(table_in, 16)
                sp.dma_start(mask_new[:], io["c_mask_new"]).then_inc(params_in, 16)
                sp.dma_start(coef[:, 0:2], io["c_coef"]).then_inc(params_in, 16)
                sp.wait_ge(table_in, 16)

                def load(cache, ring, sems, freed):
                    def step(b, i, u):
                        g = 2 * i + u
                        n = b * STEPS + g
                        sp.wait_ge(freed, n + CREDIT - 1)
                        sp.sem_inc(held_sp, 1)
                        for j in range(PS):
                            page = sp.value_load(table[0:1, ds(b * NPG + g * PS + j, 1)], min_val=0,
                                                 max_val=io["cache_k"].shape[1] - 1)
                            sp.dma_start(ring[:, u, j, :], io[cache][0, ds(page, 1)].rearrange(CACHE[cache]))\
                                .then_inc(sems[u], 16)
                    return step
                sequences(sp, nothing, load("cache_k", k_ring, k_in, kT_done[H - 1]), nothing,
                          load("cache_v", v_ring, v_in, pv_done), nothing)
                sp.wait_ge(kT_done[H - 1], DB * STEPS + CREDIT)
                sp.dma_start(pick, io["c_pick"]).then_inc(pick_in, 16)

            @block.tensor
            def _(pe):
                for s in (*kT_done, s_done, pT_done, pv_done):
                    for _ in range(CREDIT):
                        pe.sem_inc(s, 1)
                pe.sem_inc(pT_new_done, 1)
                pe.sem_inc(pv_new, 1)

                def k_start(b):
                    pe.wait_ge(q_ready, 2 * b + 2)
                    pe.wait_ge(kT_kept[0], b * STEPS + CREDIT)
                    for h in range(H):
                        last = pe.matmul(ps_k[32 * h:32 * h + 32, 0, 0:ST], q_cur[:, h, :], kT_new[:, h, :],
                                         start=True, stop=True, skip_group_check=True)
                    last.then_inc(new_done, 1)
                    pe.wait_ge(new_kept, b + 1)

                def turn_k(b, i, u):
                    g = 2 * i + u
                    n = b * STEPS + g
                    pe.wait_ge(k_in[u], 16 * PS * (b * (STEPS // 2) + i + 1))
                    for h in range(H):
                        pe.wait_ge(kT_kept[h], n + CREDIT)
                        for j in range(PS):
                            last = pe.transpose(ps_k[:, h, j * P:(j + 1) * P], k_ring[:, u, j, h * P:(h + 1) * P], ident[:])
                        last.then_inc(kT_done[h], 1)

                def score(b, i, u):
                    g = 2 * i + u
                    n = b * STEPS + g
                    for h in range(H):
                        pe.wait_ge(kT_kept[h], n + CREDIT + 1)
                    pe.wait_ge(s_kept, n + CREDIT - 1)
                    for h in range(H):
                        last = pe.matmul(ps_s[32 * h:32 * h + 32, u, :], q_cur[:, h, :], kTs[:, u, h, :],
                                         start=True, stop=True, skip_group_check=True)
                    last.then_inc(s_done, 1)

                def v_start(b):
                    pe.wait_ge(e_new, b + 1)
                    pe.wait_ge(pT_kept, b * STEPS + CREDIT)
                    pe.sem_inc(held_pe, 1)
                    pe.transpose(ps_p[0:ST, 0, :], probs_new[:], ident[:]).then_inc(pT_new_done, 1)
                    pe.wait_ge(pT_new_kept, b + 1)
                    pe.wait_ge(o_kept, b + 1)
                    pe.sem_inc(held_pe, 1)
                    for h in range(H):
                        last = pe.matmul(ps_o[32 * h:32 * h + 32, 0:DV], pT_new[:, 32 * h:32 * h + 32],
                                         V_new[:, h * DV:(h + 1) * DV], start=True, stop=False, skip_group_check=True)
                    last.then_inc(pv_new, 1)

                def turn_p(b, i, u):
                    g = 2 * i + u
                    n = b * STEPS + g
                    pe.wait_ge(e_done, n + 1)
                    pe.wait_ge(pT_kept, n + CREDIT)
                    for j in range(PS):
                        last = pe.transpose(ps_p[:, j, :], probs[:, u, j * P:(j + 1) * P], ident[:])
                    last.then_inc(pT_done, 1)

                def times_v(b, i, u):
                    g = 2 * i + u
                    n = b * STEPS + g
                    pe.wait_ge(pT_kept, n + CREDIT + 1)
                    pe.wait_ge(v_in[u], 16 * PS * (b * (STEPS // 2) + i + 1))
                    for j in range(PS):
                        for h in range(H):
                            last = pe.matmul(ps_o[32 * h:32 * h + 32, 0:DV], pT[:, u, j, 32 * h:32 * h + 32],
                                             v_ring[:, u, j, h * DV:(h + 1) * DV], start=False, stop=False,
                                             skip_group_check=True)
                    last.then_inc(pv_done, 1)

                k_start(0)
                with pe.Fori(0, STEPS // 2) as i:
                    for u in range(2):
                        turn_k(0, i, u)
                        score(0, i, u)
                with pe.Fori(0, DB - 1) as b:
                    k_start(b + 1)
                    v_start(b)
                    with pe.Fori(0, STEPS // 2) as i:
                        for u in range(2):
                            turn_k(b + 1, i, u)
                            turn_p(b, i, u)
                            score(b + 1, i, u)
                            times_v(b, i, u)
                v_start(DB - 1)
                with pe.Fori(0, STEPS // 2) as i:
                    for u in range(2):
                        turn_p(DB - 1, i, u)
                        times_v(DB - 1, i, u)
                pe.wait_ge(pick_in, 16)
                pe.wait_ge(o_kept, DB + 1)
                for h in range(H):
                    for b in range(DB):
                        last = pe.matmul(ps_s[0:ST, 0, h * DV:(h + 1) * DV], pick[:, b, h, :], o_all[:, b, :],
                                         start=(b == 0), stop=(b == DB - 1))
                last.then_inc(picked, 1)

            @block.scalar
            def _(act):
                for h in (0, 1):
                    for _ in range(CREDIT):
                        act.sem_inc(kT_kept[h], 1)
                for _ in range(CREDIT):
                    act.sem_inc(s_kept, 1)

                def k_step(b, i, u):
                    g = 2 * i + u
                    n = b * STEPS + g
                    act.wait_ge(s_done, n + CREDIT - 1)
                    for h in (0, 1):
                        act.wait_ge(kT_done[h], n + CREDIT + 1)
                        nc.scalar.activation(kTs[:, u, h, :], ps_k[:, h, :], ACT.Copy).then_inc(kT_kept[h], 1)
                    act.wait_ge(s_done, n + CREDIT + 1)
                    act.sem_inc(held_act, 1)
                    nc.scalar.activation(scores[:, ds(b % 2, 1), ds(g * W, W)], ps_s[:, u, :], ACT.Copy)\
                        .then_inc(s_kept, 1)

                def v_start(b):
                    act.wait_ge(bias_ready, b + 1)
                    act.wait_ge(pT_new_done, b + 1)
                    act.sem_inc(held_act, 1)
                    nc.scalar.activation(probs_new[:], scores[:, ds(b % 2, 1), PAST:PAST + ST], ACT.Exp,
                                         bias=neg_max[:, ds(b, 1)], scale=SCALE,
                                         accum_out=sums[:, ds(b, 1), STEPS:STEPS + 1]).then_inc(e_new, 1)

                def v_step(b, i, u):
                    g = 2 * i + u
                    n = b * STEPS + g
                    act.wait_ge(pT_done, n + CREDIT - 1)
                    act.sem_inc(held_act, 1)
                    nc.scalar.activation(probs[:, u, :], scores[:, ds(b % 2, 1), ds(g * W, W)], ACT.Exp,
                                         bias=neg_max[:, ds(b, 1)], scale=SCALE,
                                         accum_out=sums[:, ds(b, 1), ds(g, 1)]).then_inc(e_done, 1)
                sequences(act, nothing, k_step, v_start, v_step, nothing)

            @block.vector
            def _(dve):
                v = nc.vector
                for s in (kT_kept[2], kT_kept[3], pT_kept):
                    for _ in range(CREDIT):
                        dve.sem_inc(s, 1)
                dve.sem_inc(o_kept, 1)
                chain = Chain(dve, own)
                chain.link(v.memset(q_cur[:], 0.0))
                dve.wait_ge(params_in, 32)
                chain.link(v.tensor_tensor(coef[:, 2:3], coef[:, 1:2], mem["lam"][:, 0:1], ALU.mult))
                chain.link(v.tensor_tensor(coef[:, 3:4], coef[:, 2:3], coef[:, 0:1], ALU.add))
                SEQ_OWN = 4
                base0 = chain.n

                def k_start(b):
                    dve.wait_ge(s_done, b * STEPS + CREDIT)
                    dve.sem_inc(held_dve, 1)
                    for m in range(2):
                        rows = slice(DK * m, DK * (m + 1))
                        v.tensor_copy(q_cur[rows, :, DQ * m:DQ * (m + 1)], qT_new[rows, :, ds(b * DQ, DQ)])\
                            .then_inc(q_ready, 1)
                    dve.wait_ge(new_done, b + 1)
                    dve.sem_inc(held_dve, 1)
                    v.tensor_tensor(scores[:, ds(b % 2, 1), PAST:PAST + ST], ps_k[:, 0:1, 0:ST], mask_new[:, ds(b, 1)],
                                    ALU.add).then_inc(new_kept, 1)
                    dve.wait_ge(new_kept, b + 1)
                    dve.sem_inc(held_dve, 1)
                    v.tensor_reduce(maxes[:, ds(b, 1), STEPS:STEPS + 1], scores[:, ds(b % 2, 1), PAST:PAST + ST], AX.X,
                                    ALU.max).then_inc(max_new, 1)

                def k_step(b, i, u):
                    g = 2 * i + u
                    n = b * STEPS + g
                    dve.wait_ge(s_done, n + CREDIT - 1)
                    for h in (2, 3):
                        dve.wait_ge(kT_done[h], n + CREDIT + 1)
                        v.tensor_copy(kTs[:, u, h, :], ps_k[:, h, :]).then_inc(kT_kept[h], 1)
                    dve.wait_ge(s_kept, n + CREDIT + 1)
                    dve.sem_inc(held_dve, 1)
                    v.tensor_reduce(maxes[:, ds(b, 1), ds(g, 1)], scores[:, ds(b % 2, 1), ds(g * W, W)], AX.X,
                                    ALU.max).then_inc(max_done, 1)

                def bias(b):
                    c = Chain(dve, own, base0 + b * SEQ_OWN)
                    dve.wait_ge(max_done, (b + 1) * STEPS)
                    dve.wait_ge(max_new, b + 1)
                    dve.sem_inc(held_dve, 1)
                    c.link(v.tensor_reduce(top[:], maxes[:, ds(b, 1), :], AX.X, ALU.max))
                    dve.sem_inc(held_dve, 1)
                    v.tensor_scalar(neg_max[:, ds(b, 1)], top[:], -SCALE, None, ALU.mult).then_inc(bias_ready, 1)

                def v_start(b):
                    bias(b)
                    dve.wait_ge(pT_new_done, b + 2)
                    dve.wait_ge(pv_new, b + 1)
                    v.tensor_copy(pT_new[:], ps_p[0:ST, 0, :]).then_inc(pT_new_kept, 1)

                def v_step(b, i, u):
                    g = 2 * i + u
                    n = b * STEPS + g
                    dve.wait_ge(pv_done, n + CREDIT - 1)
                    dve.wait_ge(pT_done, n + CREDIT + 1)
                    v.tensor_copy(pT[:, u], ps_p[:]).then_inc(pT_kept, 1)

                def v_end(b):
                    c = Chain(dve, own, base0 + b * SEQ_OWN + 1)
                    dve.wait_ge(e_done, (b + 1) * STEPS)
                    dve.wait_ge(e_new, b + 1)
                    dve.sem_inc(held_dve, 1)
                    c.link(v.tensor_reduce(total[:, 0:1], sums[:, ds(b, 1), :], AX.X, ALU.add))
                    c.link(v.reciprocal(total[:, 1:2], total[:, 0:1]))
                    c.link(v.tensor_tensor(total[:, 0:1], total[:, 1:2], coef[:, 3:4], ALU.mult))
                    dve.wait_ge(pv_done, (b + 1) * STEPS + CREDIT)
                    dve.sem_inc(held_dve, 1)
                    v.tensor_scalar(o_all[:, ds(b, 1), :], ps_o[:, 0:DV], total[:, 0:1], None, ALU.mult)\
                        .then_inc(o_kept, 1)

                k_start(0)
                with dve.Fori(0, STEPS // 2) as i:
                    for u in range(2):
                        k_step(0, i, u)
                with dve.Fori(0, DB - 1) as b:
                    k_start(b + 1)
                    v_start(b)
                    with dve.Fori(0, STEPS // 2) as i:
                        for u in range(2):
                            v_step(b, i, u)
                            k_step(b + 1, i, u)
                    v_end(b)
                v_start(DB - 1)
                with dve.Fori(0, STEPS // 2) as i:
                    for u in range(2):
                        v_step(DB - 1, i, u)
                v_end(DB - 1)
                dve.wait_ge(picked, 1)
                v.tensor_copy(mem["o_new"][:], ps_s[0:ST, 0, :]).then_inc(own, 1)


def prompt(nc, io, dram, mem):
    with ExitStack() as ctx:
        def sb(name, shape, dt=F32):
            return ctx.enter_context(nc.sbuf_tensor(name, shape, dt))

        def sem(name):
            return ctx.enter_context(nc.semaphore(name))

        CW = 512
        NG = NT // 4
        SR = 4
        NR = NEG_G + NE
        PARAMS = 11
        ident, eps = mem["ident"], mem["eps"]
        kT, V = mem["kT"], mem["V"]
        w_out = sb("w_out_sb", [P, KD, D])
        w_r = sb("w_router", [P, KD, NR])
        b_r = sb("b_router", [P, NR])
        gate1 = sb("gate1", [P, D])
        gain2 = sb("gain2", [P, D])
        shift2 = sb("shift2", [P, D])
        g_attn = sb("g_attn_b", [P, AW])
        masks = sb("mask_p", [P, 4, CW])
        mask = sb("mask_tile", [P, CW])
        q_in = sb("q_tile", [P, H, P])
        qz = sb("q_zero_padded", [P, H, 2, P])
        probs = sb("p_probs", [P, 2, 2, NG * CW])
        nm = sb("neg_chunk_max", [P, 2, 2, NG])
        ls = sb("chunk_sums", [P, 2, 2, NG])
        mx = sb("chunk_max", [P, 2, NG])
        dd = sb("max_gap", [P, 2, NG])
        wt = sb("chunk_weights", [P, 2, NG])
        rr = sb("row_weights", [P, 2, NG])
        s2 = sb("small2", [P, 8])
        coef = sb("map_coef", [P, 2])
        aT = sb("aT", [P, 2, 4, P])
        o = sb("o_tile", [P, AW])
        osq = sb("o_sq", [P, AW])
        oa = sb("oa", [P, AW])
        oaT = sb("oaT", [P, H, P])
        obT = sb("obT_in", [P, GB, P])
        x = sb("x_res", [P, D])
        x2 = sb("x2_tile", [P, D])
        h2 = sb("h2_tile", [P, D])
        h2T = sb("h2T", [P, KD, P])
        st = sb("p_stats", [P, 24])
        ps_s = ctx.enter_context(nc.psum_tensor("p_scores", [P, SR, CW], F32))
        ps_t = ctx.enter_context(nc.psum_tensor("p_aT", [P, 4, P], F32))
        ps_o = ctx.enter_context(nc.psum_tensor("p_o", [P, AW], F32))
        ps_w = ctx.enter_context(nc.psum_tensor("p_w", [P, 2, 512], F32))

        par_in = sem("p_params_in")
        mod_in = sem("p_mod_in")
        q_loaded = sem("q_loaded")
        x_loaded = sem("x_loaded")
        ob_loaded = sem("ob_loaded")
        x2_out = sem("x2_out")
        h2_out = sem("h2_out")
        held_sp, held_act, held_dve, held_pool = (sem(f"p_held_{e}") for e in ("sp", "act", "dve", "pool"))
        mask_ready = sem("mask_ready")
        qz_ready = sem("qz_ready")
        s_done = sem("p_s_done")
        bias_done = sem("p_bias_done")
        e_done = sem("p_e_done")
        gap_ready = sem("gap_ready")
        w_ready = sem("w_ready")
        a_done = sem("a_done")
        t_done = sem("t_done")
        head_turned = sem("head_turned")
        aT_kept = sem("aT_kept")
        pv_done = sem("p_pv_done")
        o_kept = sem("p_o_kept")
        o_ss = sem("o_ss")
        o_std = sem("o_std")
        oa_ready = sem("oa_ready")
        oaT_done = sem("oaT_done")
        oaT_kept = sem("oaT_kept")
        w_done = sem("w_done")
        x2_ready = sem("x2_ready")
        x2_ss = sem("x2_ss")
        x2_std = sem("x2_std")
        h2_ready = sem("h2_ready")
        h2T_done = sem("h2T_done")
        h2T_kept = sem("h2T_kept")
        r_done = sem("r_done")
        lg_ready = sem("lg_ready")
        own = sem("p_dve_own")
        zeroed = sem("qz_zeroed")

        def c_slot(J, h, c):
            return (h * (J + 1) + c) % 2

        def chunk_at(J, r, h):
            return sum(4 * H * (j + 1) for j in range(J)) + (r * H + h) * (J + 1)

        def tiles(eng, body):
            body(0, 0, (0, 1))
            for J in range(NG):
                with eng.Fori(1 if J == 0 else 0, 3) as r:
                    body(J, r, (J, r + 1))
                body(J, 3, (J + 1, 0) if J < NG - 1 else None)

        def slots(J, r, following):
            for h in range(H):
                ahead = (J, r, h + 1) if h < H - 1 else (*following, 0) if following else None
                yield ahead, (J, r, h), h

        with nc.Block() as block:
            @block.sync
            def _(sp):
                n = 0
                for dst, src in ((w_out, io["w_out"][0].rearrange("(k p) n -> p k n", p=P)),
                                 (masks, io["c_mask_p"]), (coef, io["c_coef_p"]),
                                 (gate1, dram["mod"][1, MOD_GATE1]), (gain2, dram["mod"][1, MOD_GAIN2]),
                                 (shift2, dram["mod"][1, MOD_SHIFT2]), (g_attn, io["g_attn"].rearrange("o h e -> o (h e)").broadcast_to([P, AW]))):
                    sp.dma_start(dst[:], src).then_inc(par_in, 16)
                    n += 1
                sp.dma_start(b_r[:, 0:NEG_G], io["b_router_g"].broadcast_to([P, NEG_G])).then_inc(par_in, 16)
                sp.dma_start(b_r[:, NEG_G:], io["b_router_e"].broadcast_to([P, NE])).then_inc(par_in, 16)
                with nc.allow_non_contiguous_dma(reason="router weights, 16 and 128 bytes a row"):
                    sp.dma_start(w_r[:, :, 0:NEG_G], io["w_router_g"][0].rearrange("(k p) n -> p k n", p=P)).then_inc(par_in, 16)
                    sp.dma_start(w_r[:, :, NEG_G:], io["w_router_e"][0].rearrange("(k p) n -> p k n", p=P)).then_inc(par_in, 16)
                assert n + 4 == PARAMS
                sp.dma_start(q_in[:], dram["qT"][0]).then_inc(q_loaded, 16)
                sp.dma_start(x[0:ST, :], io["x_sample"].rearrange("b q d -> (b q) d")).then_inc(x_loaded, 16)

                def body(J, r, following):
                    i = 4 * J + r
                    if following:
                        sp.wait_ge(qz_ready, 8 * (i + 1))
                        sp.sem_inc(held_sp, 1)
                        sp.dma_start(q_in[:], dram["qT"][ds(i + 1, 1)]).then_inc(q_loaded, 16)
                    residual(i, True)

                def residual(k, more):
                    first = isinstance(k, int) and k == 0
                    if more:
                        sp.wait_ge(w_done, k + 1)
                        sp.sem_inc(held_sp, 1)
                        sp.dma_start(obT[:], dram["obT"][ds(k, 1)]).then_inc(ob_loaded, 16)
                    sp.wait_ge(x2_ready, k + 1)
                    sp.sem_inc(held_sp, 1)
                    if first:
                        sp.dma_start(dram["x2"][SEQ:NTOK, :], x2[0:ST, :]).then_inc(x2_out, 16)
                    else:
                        sp.dma_start(dram["x2"][ds((k - 1) * P, P), :], x2[:]).then_inc(x2_out, 16)
                    if more:
                        sp.dma_start(x[:], io["x_prompt"][0, ds(k * P, P), :]).then_inc(x_loaded, 16)
                    sp.wait_ge(h2_ready, k + 1)
                    sp.sem_inc(held_sp, 1)
                    if first:
                        sp.dma_start(dram["h2"][SEQ:NTOK, :], h2[0:ST, :]).then_inc(h2_out, 16)
                        for dst, part in ((gate1, MOD_GATE1), (gain2, MOD_GAIN2), (shift2, MOD_SHIFT2)):
                            sp.dma_start(dst[:], dram["mod"][0, part]).then_inc(mod_in, 16)
                    else:
                        sp.dma_start(dram["h2"][ds((k - 1) * P, P), :], h2[:]).then_inc(h2_out, 16)
                tiles(sp, body)
                residual(NT, False)
                sp.wait_ge(x2_out, 16 * (NT + 1))
                sp.wait_ge(h2_out, 16 * (NT + 1))

            @block.gpsimd
            def _(pool):
                nc.gpsimd.memset(qz[:], 0.0).then_inc(zeroed, 1)
                pool.wait_ge(zeroed, 1)

                def pad(J, r, h):
                    i = 4 * J + r
                    if h == 0:
                        pool.wait_ge(q_loaded, 16 * (i + 1))
                        waited(pool, mask_ready, i)
                    waited(pool, s_done, 2 * chunk_before(J, r, h))
                    pool.sem_inc(held_pool, 1)
                    for m in range(2):
                        if m or h:
                            pool.wait_ge(qz_ready, 8 * i + 2 * h + m)
                            pool.sem_inc(held_pool, 1)
                        rows = slice(DK * m, DK * (m + 1))
                        nc.gpsimd.tensor_copy(qz[rows, h, m, :], q_in[rows, h, :]).then_inc(qz_ready, 1)

                def chunk_before(J, r, h):
                    if isinstance(r, int) and r == 0:
                        return chunk_at(J - 1, 3, h) + J if J else 0
                    return chunk_at(J, r - 1, h + 1)

                def place_mask(J, r):
                    pool.wait_ge(qz_ready, 8 * (4 * J + r + 1))
                    if not (isinstance(r, int) and J == r == 0):
                        pool.wait_ge(bias_done, 2 * chunk_before(J, r, H - 1))
                        pool.sem_inc(held_pool, 1)
                    nc.gpsimd.tensor_copy(mask[:], masks[:, ds(r, 1), :].rearrange("p o k -> p (o k)")).then_inc(mask_ready, 1)

                def body(J, r, following):
                    if following:
                        for h in range(H):
                            pad(*following, h)
                        place_mask(*following)
                for h in range(H):
                    pad(0, 0, h)
                pool.wait_ge(par_in, 16 * PARAMS)
                place_mask(0, 0)
                tiles(pool, body)

            @block.tensor
            def _(pe):
                for _ in range(1):
                    pe.sem_inc(t_done, 1)
                for s, credit in ((head_turned, 2), (pv_done, 2)):
                    for _ in range(credit):
                        pe.sem_inc(s, 1)

                def score(J, r, h, c, m):
                    n = 2 * (chunk_at(J, r, h) + c) + m
                    bank = (2 * c + m + 2 * h * (J + 1)) % SR
                    if c == 0 and m == 0:
                        pe.wait_ge(qz_ready, 8 * (4 * J + r) + 2 * h + 2)
                    pe.wait_ge(e_done, n + 1)
                    pe.matmul(ps_s[:, bank, :], qz[:, h, m, :], kT[:, h, c * CW:(c + 1) * CW],
                              start=True, stop=True).then_inc(s_done, 1)

                def turn(J, r, h, c):
                    n = chunk_at(J, r, h) + c
                    pe.wait_ge(a_done, n + 1)
                    pe.wait_ge(aT_kept, n + 2)
                    for j in range(4):
                        last = pe.transpose(ps_t[:, j, :], probs[:, h % 2, 0, c * CW + j * P:c * CW + (j + 1) * P], ident[:])
                    last.then_inc(t_done, 1)

                def times_v(J, r, h, c):
                    n = chunk_at(J, r, h) + c
                    pe.wait_ge(aT_kept, n + 3)
                    if h == 0 and c == 0:
                        pe.wait_ge(o_kept, 4 * J + r + 1)
                    for j in range(4):
                        if c == J and j == 1:
                            last.then_inc(head_turned, 1)
                        last = pe.matmul(ps_o[:, h * DV:(h + 1) * DV], aT[:, c_slot(J, h, c), j, :],
                                         V[:, 4 * c + j, h * DV:(h + 1) * DV], start=(c == 0 and j == 0),
                                         stop=(c == J and j == 3))
                    last.then_inc(pv_done, 1)

                def oa_turn(k, R):
                    pe.wait_ge(oa_ready, k + 1)
                    waited(pe, lg_ready, k)
                    for h in range(H):
                        last = pe.transpose(ps_w[:, 0, h * P:h * P + R], oa[0:R, h * P:(h + 1) * P], ident[0:R, 0:R])
                    last.then_inc(oaT_done, 1)

                def project(k, R, ob_src):
                    pe.wait_ge(oaT_kept, k + 1)
                    waited(pe, ob_loaded, 16 * k)
                    for half in range(2):
                        for kk in range(KD):
                            lhs = oaT[:, kk, 0:R] if kk < H else ob_src[:, kk - H, 0:R]
                            last = pe.matmul(ps_w[0:R, half, :], lhs, w_out[:, kk, half * 512:(half + 1) * 512],
                                             start=(kk == 0), stop=(kk == KD - 1))
                    last.then_inc(w_done, 1)

                def h2_turn(k, R):
                    pe.wait_ge(h2_ready, k + 1)
                    for b in range(KD):
                        last = pe.transpose(ps_w[:, b // 4, (b % 4) * P:(b % 4) * P + R], h2[0:R, b * P:(b + 1) * P],
                                            ident[0:R, 0:R])
                    last.then_inc(h2T_done, 1)

                def route(k, R):
                    pe.wait_ge(h2T_kept, k + 1)
                    for b in range(KD):
                        last = pe.matmul(ps_w[0:R, 0, 0:NR], h2T[:, b, 0:R], w_r[:, b, :], start=(b == 0), stop=(b == KD - 1))
                    last.then_inc(r_done, 1)

                def body(J, r, following):
                    k = 4 * J + r
                    R = ST if isinstance(k, int) and k == 0 else P
                    for ahead, now, h in slots(J, r, following):
                        todo = [(c, m) for c in range(ahead[0] + 1) for m in range(2)] if ahead else []
                        for c, m in todo[:-1]:
                            score(*ahead, c, m)
                        if h == 3:
                            h2_turn(k, R)
                        turn(*now, 0)
                        for c, m in todo[-1:]:
                            score(*ahead, c, m)
                        for c in range(1, J + 1):
                            turn(*now, c)
                            times_v(*now, c - 1)
                        times_v(*now, J)
                        if h == 0:
                            oa_turn(k, R)
                        if h == 1:
                            project(k, R, mem["obT_new"] if R == ST else obT)
                        if h == 3:
                            route(k, R)

                pe.wait_ge(par_in, 16 * PARAMS)
                for c, m in ((0, 0), (0, 1)):
                    score(0, 0, 0, c, m)
                tiles(pe, body)
                oa_turn(NT, P)
                project(NT, P, obT)
                h2_turn(NT, P)
                route(NT, P)

            @block.scalar
            def _(act):
                for _ in range(SR):
                    act.sem_inc(e_done, 1)
                for s, credit in ((aT_kept, 2), (o_kept, 1)):
                    for _ in range(credit):
                        act.sem_inc(s, 1)

                def exps(J, r, h, c, m):
                    n = 2 * (chunk_at(J, r, h) + c) + m
                    bank = (2 * c + m + 2 * h * (J + 1)) % SR
                    act.wait_ge(bias_done, n + 1)
                    if c == 0 and m == 0:
                        act.wait_ge(head_turned, 4 * (4 * J + r) + h + 1)
                    dst = probs[:, h % 2, m, c * CW:(c + 1) * CW]
                    nc.scalar.activation(dst, dst if c == J else ps_s[:, bank, :], ACT.Exp, bias=nm[:, h % 2, m, c:c + 1],
                                         scale=SCALE, accum_out=ls[:, h % 2, m, c:c + 1]).then_inc(e_done, 1)

                def weights(J, r, h):
                    act.wait_ge(gap_ready, 4 * (4 * J + r) + h + 1)
                    nc.scalar.activation(wt[:, :, 0:J + 1], dd[:, :, 0:J + 1], ACT.Exp).then_inc(w_ready, 1)

                def keep_aT(J, r, h, c):
                    n = chunk_at(J, r, h) + c
                    act.wait_ge(pv_done, n + 1)
                    act.wait_ge(t_done, n + 2)
                    nc.scalar.activation(aT[:, c_slot(J, h, c)], ps_t[:], ACT.Copy).then_inc(aT_kept, 1)

                def root(done, ready, k, R, s, cnt, width):
                    act.wait_ge(done, k + 1)
                    nc.scalar.activation(st[0:R, s + 4:s + 4 + cnt], st[0:R, s:s + cnt], ACT.Sqrt, bias=eps[0:R, 0:1],
                                         scale=1.0 / width).then_inc(ready, 1)

                def keep_o(J, r):
                    act.wait_ge(pv_done, chunk_at(J, r, 3) + J + 1 + 2)
                    nc.scalar.activation(o[:], ps_o[:], ACT.Copy).then_inc(o_kept, 1)

                def keep_oaT(k, R):
                    act.wait_ge(oaT_done, k + 1)
                    nc.scalar.activation(oaT[:, :, 0:R], ps_w[:, 0, :].rearrange("p (h t) -> p h t", h=H)[:, :, 0:R],
                                         ACT.Copy).then_inc(oaT_kept, 1)

                def keep_h2T(k, R):
                    act.wait_ge(h2T_done, k + 1)
                    nc.scalar.activation(h2T[:, :, 0:R],
                                         ps_w[:].rearrange("p a (b t) -> p (a b) t", t=P)[:, :, 0:R], ACT.Copy)\
                        .then_inc(h2T_kept, 1)

                def body(J, r, following):
                    k = 4 * J + r
                    R = ST if isinstance(k, int) and k == 0 else P
                    for ahead, now, h in slots(J, r, following):
                        todo = [(c, m) for c in range(ahead[0] + 1) for m in range(2)] if ahead else []
                        for c, m in todo[:-1]:
                            exps(*ahead, c, m)
                        if h == 3:
                            keep_h2T(k, R)
                        keep_aT(*now, 0)
                        for c, m in todo[-1:]:
                            exps(*ahead, c, m)
                        if ahead:
                            weights(*ahead)
                        for c in range(1, J + 1):
                            keep_aT(*now, c)
                        if h == 0:
                            root(o_ss, o_std, k, R, 0, H, DV)
                            keep_oaT(k, R)
                        if h == 2:
                            root(x2_ss, x2_std, k, R, 8, 1, D)
                    keep_o(J, r)

                for c, m in ((0, 0), (0, 1)):
                    exps(0, 0, 0, c, m)
                weights(0, 0, 0)
                tiles(act, body)
                root(o_ss, o_std, NT, P, 0, H, DV)
                keep_oaT(NT, P)
                root(x2_ss, x2_std, NT, P, 8, 1, D)
                keep_h2T(NT, P)

            @block.vector
            def _(dve):
                v = nc.vector

                def own_count(J):
                    return 3 * (J + 1) + 6
                BACK = 6

                def scores(J, r, h, chain):
                    i4 = 4 * (4 * J + r) + h
                    dve.wait_ge(head_turned, i4 + 1)
                    par = h % 2
                    for c in range(J + 1):
                        for m in range(2):
                            n = 2 * (chunk_at(J, r, h) + c) + m
                            bank = (2 * c + m + 2 * h * (J + 1)) % SR
                            dve.wait_ge(s_done, n + 1)
                            if c == J:
                                if h == 0 and m == 0:
                                    dve.wait_ge(mask_ready, 4 * J + r + 1)
                                dve.sem_inc(held_dve, 1)
                                chain.link(v.tensor_tensor_reduce(
                                    out=probs[:, par, m, c * CW:(c + 1) * CW], in0=ps_s[:, bank, :],
                                    in1=mask[:], scale=1.0, scalar=-3.0e38, op0=ALU.add, op1=ALU.max, accum_out=mx[:, m, c:c + 1]))
                            else:
                                chain.link(v.tensor_reduce(mx[:, m, c:c + 1], ps_s[:, bank, :], AX.X, ALU.max))
                            v.tensor_scalar(nm[:, par, m, c:c + 1], mx[:, m, c:c + 1], -SCALE, None, ALU.mult).then_inc(bias_done, 1)
                    ch = slice(0, J + 1)
                    dve.wait_ge(bias_done, 2 * (chunk_at(J, r, h) + J + 1))
                    chain.link(v.tensor_reduce(s2[:, 0:2], nm[:, par, :, ch], AX.X, ALU.min))
                    v.tensor_tensor(dd[:, :, ch], s2[:, 0:2].unsqueeze(2).to_broadcast([P, 2, J + 1]), nm[:, par, :, ch],
                                    ALU.subtract).then_inc(gap_ready, 1)
                    dve.wait_ge(w_ready, i4 + 1)
                    dve.wait_ge(e_done, 2 * (chunk_at(J, r, h) + J + 1) + SR)
                    chain.link(v.tensor_tensor(rr[:, :, ch], wt[:, :, ch], ls[:, par, :, ch], ALU.mult))
                    chain.link(v.tensor_reduce(s2[:, 2:4], rr[:, :, ch], AX.X, ALU.add))
                    chain.link(v.reciprocal(s2[:, 4:6], s2[:, 2:4]))
                    chain.link(v.tensor_tensor(s2[:, 6:8], s2[:, 4:6], coef[:], ALU.mult))
                    chain.link(v.tensor_tensor(rr[:, :, ch], wt[:, :, ch], s2[:, 6:8].unsqueeze(2).to_broadcast([P, 2, J + 1]),
                                               ALU.mult))
                    for c in range(J + 1):
                        p0, p1 = (probs[:, par, m, c * CW:(c + 1) * CW] for m in range(2))
                        chain.link(v.tensor_scalar(p1, p1, rr[:, 1, c:c + 1], None, ALU.mult))
                        v.scalar_tensor_tensor(out=p0, in0=p0, scalar=rr[:, 0, c:c + 1], in1=p1, op0=ALU.mult, op1=ALU.add)\
                            .then_inc(a_done, 1)

                def norm_o(k, R, src, chain):
                    g3 = "p (g c) -> p g c"
                    if R == P:
                        dve.wait_ge(o_kept, k + 1)
                    chain.link(v.tensor_tensor(osq[0:R, :], src[0:R, :], src[0:R, :], ALU.mult))
                    v.tensor_reduce(st[0:R, 0:H], osq[0:R, :].rearrange(g3, g=H), AX.X, ALU.add).then_inc(o_ss, 1)
                    dve.wait_ge(o_std, k + 1)
                    chain.link(v.reciprocal(st[0:R, 16:16 + H], st[0:R, 4:4 + H]))
                    chain.link(v.tensor_tensor(osq[0:R, :].rearrange(g3, g=H), src[0:R, :].rearrange(g3, g=H),
                                               st[0:R, 16:16 + H].unsqueeze(2).to_broadcast([R, H, DV]), ALU.mult))
                    waited(dve, oaT_done, k)
                    v.tensor_tensor(oa[0:R, :], osq[0:R, :], g_attn[0:R, :], ALU.mult).then_inc(oa_ready, 1)

                def residual(k, R, chain):
                    dve.wait_ge(w_done, k + 1)
                    if R == P:
                        dve.wait_ge(mod_in, 48)
                    waited(dve, x2_out, 16 * k)
                    chain.link(v.tensor_tensor(x2[0:R, :], ps_w[0:R].rearrange("p a n -> p (a n)"), gate1[0:R, :], ALU.mult))
                    dve.wait_ge(x_loaded, 16 * (k + 1))
                    v.tensor_tensor(x2[0:R, :], x2[0:R, :], x[0:R, :], ALU.add).then_inc(x2_ready, 1)
                    dve.wait_ge(x2_ready, k + 1)
                    waited(dve, h2_out, 16 * k)
                    v.tensor_tensor_reduce(out=h2[0:R, :], in0=x2[0:R, :], in1=x2[0:R, :], scale=1.0, scalar=0.0,
                                           op0=ALU.mult, op1=ALU.add, accum_out=st[0:R, 8:9]).then_inc(x2_ss, 1)
                    dve.wait_ge(x2_std, k + 1)
                    chain.link(v.reciprocal(st[0:R, 20:21], st[0:R, 12:13]))
                    chain.link(v.scalar_tensor_tensor(out=h2[0:R, :], in0=x2[0:R, :], scalar=st[0:R, 20:21],
                                                      in1=gain2[0:R, :], op0=ALU.mult, op1=ALU.mult))
                    v.tensor_tensor(h2[0:R, :], h2[0:R, :], shift2[0:R, :], ALU.add).then_inc(h2_ready, 1)

                def logits(k, R):
                    dve.wait_ge(r_done, k + 1)
                    dve.sem_inc(held_dve, 1)
                    v.tensor_tensor(mem["lg"][0:R, ds(k, 1), :], ps_w[0:R, 0:1, 0:NR], b_r[0:R, :].unsqueeze(1), ALU.add)\
                        .then_inc(lg_ready, 1)

                start = 1 + 2 + own_count(0)
                per = {J: 4 * own_count(J) + BACK for J in range(NG)}

                def base(J, r):
                    return start + sum(4 * per[j] + own_count(j + 1) - own_count(j) for j in range(J)) + r * per[J]

                def body(J, r, following):
                    k = 4 * J + r
                    R = ST if isinstance(k, int) and k == 0 else P
                    chain = Chain(dve, own, base(J, r))
                    for ahead, now, h in slots(J, r, following):
                        if ahead:
                            scores(*ahead, chain)
                        if h == 0:
                            norm_o(k, R, mem["o_new"] if R == ST else o, chain)
                        if h == 2:
                            residual(k, R, chain)
                    logits(k, R)
                    assert chain.n == 3 * own_count(J) + BACK + (own_count(following[0]) if following else 0)

                chain = Chain(dve, own)
                dve.wait_ge(par_in, 16 * PARAMS)
                chain.step(v.tensor_scalar(g_attn[:], g_attn[:], 1.0 - LAM_INIT, None, ALU.mult))
                chain.step(v.tensor_tensor(coef[:, 1:2], coef[:, 1:2], mem["lam"][:, 0:1], ALU.mult))
                chain.link(v.memset(mem["lg"][ST:P, 0, :], 0.0))
                scores(0, 0, 0, chain)
                assert chain.n == start
                tiles(dve, body)
                chain = Chain(dve, own, base(NG - 1, 3) + 3 * own_count(NG - 1) + BACK)
                norm_o(NT, P, o, chain)
                residual(NT, P, chain)
                logits(NT, P)


def routing(nc, io, mem, r):
    with ExitStack() as ctx:
        def sb(name, shape, dt=F32):
            return ctx.enter_context(nc.sbuf_tensor(name, shape, dt))

        def sem(name):
            return ctx.enter_context(nc.semaphore(name))

        T = NT + 1
        BIG = 1e30
        MAXB = (NTOK + P - 1) // P
        lg = mem["lg"]
        before = sb("before", [P, P])
        ones = sb("ones", [P, P])
        iota = sb("iota", [P, P])
        first = sb("first", [P, NE, NE])
        tok = sb("tok", [P, T])
        m1 = sb("rt_m1", [P, T])
        g_sum = sb("rt_gsum", [P, T])
        gd = sb("rt_gd", [P, T, NEG_G])
        cand_g = sb("rt_cand_g", [P, T, NEG_G])
        oh_g = sb("rt_oh_g", [P, T, NEG_G])
        ng_g = sb("rt_ng_g", [P, T, NEG_G])
        el = sb("rt_el", [P, T, NE])
        cand = sb("rt_cand", [P, T, NE])
        oh = [sb("rt_oh1", [P, T, NE]), sb("rt_oh2", [P, T, NE])]
        both = sb("rt_both", [P, T, NE])
        top = [sb("rt_top1", [P, T]), sb("rt_top2", [P, T])]
        de = sb("rt_de", [P, T])
        rank = sb("rt_rank", [P, T, NE])
        cnt = sb("rt_cnt", [P, T, NE])
        off = sb("rt_off", [P, T + 1, NE])
        nb = sb("rt_nb", [P, NE])
        cmp_b = sb("rt_cmp_b", [P, NE, MAXB])
        cmp_f = sb("rt_cmp_f", [P, NE, NE])
        start = sb("rt_start", [P, NE])
        end = sb("rt_end", [P, NE])
        dest = [sb("rt_dest1", [P, T]), sb("rt_dest2", [P, T])]
        blk = sb("rt_blk", [P, 2, T])
        row = sb("rt_row", [P, 2, T])
        ge = sb("rt_ge", [P, 2, T, NB])
        oh_row = sb("rt_oh_row", [P, 2, P])
        oh_blk = sb("rt_oh_blk", [P, 2, NB])
        be = sb("rt_be", [P, NB])
        cmp_e = sb("rt_cmp_e", [P, NB, NE])
        ps = ctx.enter_context(nc.psum_tensor("rt_ps", [P, 4, 512], F32))
        ps_tok = ctx.enter_context(nc.psum_tensor("rt_ps_tok", [P, 512], F32))

        params_in = sem("rt_params_in")
        own = sem("rt_dve_own")
        g_ready = sem("rt_g_ready")
        g_exp = sem("rt_g_exp")
        de_ready = sem("rt_de_ready")
        de_exp = sem("rt_de_exp")
        chosen = sem("rt_chosen")
        counted = sem("rt_counted")
        pair_ready = sem("rt_pair_ready")
        pair_done = sem("rt_pair_done")
        E3 = "p t (g e) -> p t g e"

        with nc.Block() as block:
            @block.sync
            def _(sp):
                for dst, src in ((before, io["c_before"]), (iota, io["c_iota"]), (tok, io["c_tok"]),
                                 (first, io["c_first"].broadcast_to([P, NE * NE]).rearrange("p (a b) -> p a b", a=NE))):
                    sp.dma_start(dst[:], src).then_inc(params_in, 16)

            @block.scalar
            def _(act):
                act.wait_ge(g_ready, 1)
                nc.scalar.activation(gd[:], gd[:], ACT.Exp).then_inc(g_exp, 1)
                act.wait_ge(de_ready, 1)
                nc.scalar.activation(de[:], de[:], ACT.Exp).then_inc(de_exp, 1)

            @block.tensor
            def _(pe):
                pe.wait_ge(chosen, 1)
                pe.wait_ge(params_in, 64)
                flat = both[:].rearrange("p t e -> p (t e)")
                for n, w in enumerate((before, ones)):
                    pe.matmul(ps[:, 2 * n, 0:512], w[:], flat[:, 0:512], start=True, stop=True)
                    last = pe.matmul(ps[:, 2 * n + 1, 0:T * NE - 512], w[:], flat[:, 512:T * NE], start=True, stop=True)
                last.then_inc(counted, 1)
                for n in range(2 * T):
                    pe.wait_ge(pair_ready, n + 1)
                    pe.matmul(ps_tok[:, 0:NB], oh_row[:, n % 2, :], oh_blk[:, n % 2, :], start=(n == 0),
                              stop=(n == 2 * T - 1)).then_inc(pair_done, 1)

            @block.vector
            def _(dve):
                v = nc.vector
                c = Chain(dve, own)

                def spread(x, n):
                    return x.unsqueeze(2).to_broadcast([P, T, n])

                def first_max(x, n, best, cand, onehot):
                    c.link(v.tensor_reduce(best, x, AX.X, ALU.max))
                    c.link(v.tensor_tensor(cand, x, spread(best, n), ALU.is_lt))
                    c.link(v.tensor_scalar(cand, cand, BIG, None, ALU.mult))
                    c.link(v.tensor_tensor(cand, cand, iota[:, 0:n].unsqueeze(1).to_broadcast([P, T, n]), ALU.add))
                    c.link(v.tensor_reduce(m1[:], cand, AX.X, ALU.min))
                    c.link(v.tensor_tensor(onehot, iota[:, 0:n].unsqueeze(1).to_broadcast([P, T, n]), spread(m1[:], n),
                                           ALU.is_equal))

                dve.wait_ge(params_in, 64)
                c.link(v.memset(ones[:], 1.0))
                lgg = lg[:, :, 0:NEG_G]
                first_max(lgg, NEG_G, g_sum[:], cand_g[:], oh_g[:])
                v.tensor_tensor(gd[:], lgg, spread(g_sum[:], NEG_G), ALU.subtract).then_inc(g_ready, 1)
                c.link(v.tensor_scalar(ng_g[:], oh_g[:], BIG, -BIG, ALU.mult, ALU.add))
                lge = lg[:, :, NEG_G:]
                for g in range(NEG_G):
                    c.step(v.tensor_tensor(el[:, :, g * EPG:(g + 1) * EPG], lge[:, :, g * EPG:(g + 1) * EPG],
                                           oh_g[:, :, g:g + 1].to_broadcast([P, T, EPG]), ALU.mult))
                c.wait()
                for g in range(NEG_G):
                    c.step(v.tensor_tensor(el[:, :, g * EPG:(g + 1) * EPG], el[:, :, g * EPG:(g + 1) * EPG],
                                           ng_g[:, :, g:g + 1].to_broadcast([P, T, EPG]), ALU.add))
                c.wait()
                first_max(el[:], NE, top[0][:], cand[:], oh[0][:])
                c.link(v.tensor_scalar(cand[:], oh[0][:], -3.0 * BIG, None, ALU.mult))
                c.link(v.tensor_tensor(el[:], el[:], cand[:], ALU.add))
                first_max(el[:], NE, top[1][:], cand[:], oh[1][:])
                v.tensor_tensor(de[:], top[1][:], top[0][:], ALU.subtract).then_inc(de_ready, 1)
                c.step(v.memset(oh[0][ST:P, 0, :], 0.0))
                c.link(v.memset(oh[1][ST:P, 0, :], 0.0))
                v.tensor_tensor(both[:], oh[0][:], oh[1][:], ALU.add).then_inc(chosen, 1)
                dve.wait_ge(g_exp, 1)
                c.link(v.tensor_reduce(g_sum[:], gd[:], AX.X, ALU.add))
                dve.wait_ge(de_exp, 1)
                c.link(v.tensor_scalar(m1[:], de[:], 1.0, None, ALU.add))
                c.link(v.tensor_tensor(m1[:], m1[:], g_sum[:], ALU.mult))
                c.link(v.reciprocal(r["gate"][:, 0, :], m1[:]))
                c.link(v.tensor_tensor(r["gate"][:, 1, :], r["gate"][:, 0, :], de[:], ALU.mult))
                dve.wait_ge(counted, 1)
                c.step(v.tensor_copy(rank[:].rearrange("p t e -> p (t e)"),
                                     ps[:, 0:2, :].rearrange("p a n -> p (a n)")[:, 0:T * NE]))
                c.step(v.tensor_copy(cnt[:].rearrange("p t e -> p (t e)"),
                                     ps[:, 2:4, :].rearrange("p a n -> p (a n)")[:, 0:T * NE]))
                c.link(v.memset(off[:, 0, :], 0.0))
                for t in range(T):
                    c.link(v.tensor_tensor(off[:, t + 1, :], off[:, t, :], cnt[:, t, :], ALU.add))
                c.link(v.tensor_scalar(nb[:], off[:, T, :], 1.0 / P, None, ALU.mult))
                c.link(v.tensor_tensor(cmp_b[:], nb[:].unsqueeze(2).to_broadcast([P, NE, MAXB]),
                                       iota[:, 0:MAXB].unsqueeze(1).to_broadcast([P, NE, MAXB]), ALU.is_gt))
                c.link(v.tensor_reduce(nb[:], cmp_b[:], AX.X, ALU.add))
                c.link(v.tensor_tensor(cmp_f[:], first[:], nb[:].unsqueeze(1).to_broadcast([P, NE, NE]), ALU.mult))
                c.link(v.tensor_reduce(start[:], cmp_f[:], AX.X, ALU.add))
                c.link(v.tensor_tensor(end[:], start[:], nb[:], ALU.add))
                c.link(v.tensor_tensor(cmp_e[:], iota[:, 0:NB].unsqueeze(2).to_broadcast([P, NB, NE]),
                                       end[:].unsqueeze(1).to_broadcast([P, NB, NE]), ALU.is_ge))
                c.link(v.tensor_reduce(be[:], cmp_e[:], AX.X, ALU.add))
                c.link(v.tensor_scalar(be[:], be[:], float(NE - 1), None, ALU.min))
                c.link(v.tensor_copy(r["block_expert"][:], be[0:1, :]))
                c.link(v.tensor_scalar(start[:], start[:], float(P), None, ALU.mult))
                c.link(v.tensor_tensor(rank[:], rank[:], off[:, 0:T, :], ALU.add))
                c.link(v.tensor_tensor(rank[:], rank[:], start[:].unsqueeze(1).to_broadcast([P, T, NE]), ALU.add))
                for k in range(2):
                    c.link(v.tensor_tensor(cand[:], rank[:], oh[k][:], ALU.mult))
                    c.link(v.tensor_reduce(dest[k][:], cand[:], AX.X, ALU.add))
                    c.step(v.tensor_copy(r["dest"][:, k, :], dest[k][:]))
                    c.link(v.tensor_scalar(blk[:, k, :], dest[k][:], 1.0 / P, None, ALU.mult))
                    c.link(v.tensor_tensor(ge[:, k], blk[:, k, :].unsqueeze(2).to_broadcast([P, T, NB]),
                                           iota[:, 0:NB].unsqueeze(1).to_broadcast([P, T, NB]), ALU.is_ge))
                    c.link(v.tensor_reduce(blk[:, k, :], ge[:, k], AX.X, ALU.add))
                    c.link(v.tensor_scalar(blk[:, k, :], blk[:, k, :], -1.0, None, ALU.add))
                    c.link(v.tensor_scalar(row[:, k, :], blk[:, k, :], -float(P), None, ALU.mult))
                    c.link(v.tensor_tensor(row[:, k, :], row[:, k, :], dest[k][:], ALU.add))
                for n in range(2 * T):
                    t, k = n // 2, n % 2
                    waited(dve, pair_done, n - 1)
                    R = ST if t == 0 else P
                    if t == 0:
                        c.link(v.memset(oh_row[:, n % 2, :], 0.0))
                        c.link(v.memset(oh_blk[:, n % 2, :], 0.0))
                    c.link(v.tensor_scalar(oh_row[0:R, n % 2, :], iota[0:R, :], row[0:R, k, t:t + 1], None, ALU.is_equal))
                    v.tensor_scalar(oh_blk[0:R, n % 2, :], iota[0:R, 0:NB], blk[0:R, k, t:t + 1], tok[0:R, t:t + 1],
                                    ALU.is_equal, ALU.mult).then_inc(pair_ready, 1)
                dve.wait_ge(pair_done, 2 * T)
                c.link(v.tensor_copy(r["row_token"][:], ps_tok[:, 0:NB]))


def experts(nc, io, dram, mem, r):
    with ExitStack() as ctx:
        def sb(name, shape, dt=F32):
            return ctx.enter_context(nc.sbuf_tensor(name, shape, dt))

        def sem(name):
            return ctx.enter_context(nc.semaphore(name))

        ident = mem["ident"]
        KF = DE // P
        wg = sb("wg", [P, 2, KD, DE])
        wu = sb("wu", [P, 2, KD, DE])
        wd = sb("wd", [P, 2, KF, D])
        idx = sb("gather_idx", [P, 2], I32)
        xg = sb("xg", [P, 2, D])
        xT = sb("xT", [P, KD, P])
        sg = sb("sg", [P, DE])
        hh = sb("hh", [P, DE])
        hT = sb("ehT", [P, KF, P])
        y = sb("y", [P, 2, D])
        ps_x = ctx.enter_context(nc.psum_tensor("e_x", [P, KD, P], F32))
        ps_gu = ctx.enter_context(nc.psum_tensor("e_gu", [P, 2, 512], F32))
        ps_h = ctx.enter_context(nc.psum_tensor("e_h", [P, KF, P], F32))
        ps_y = ctx.enter_context(nc.psum_tensor("e_y", [P, 2, 512], F32))

        held_sp, held_pool = sem("e_held_sp"), sem("e_held_pool")
        gu_in = [sem("gu_in0"), sem("gu_in1")]
        wd_in = [sem("wd_in0"), sem("wd_in1")]
        idx_ready = sem("idx_ready")
        x_in = [sem("xg_in0"), sem("xg_in1")]
        xT_done = sem("xT_done")
        xT_kept = sem("xT_kept")
        gu_done = sem("gu_done")
        sg_ready = sem("sg_ready")
        hh_ready = sem("hh_ready")
        hT_done = sem("ehT_done")
        hT_kept = sem("ehT_kept")
        y_done = sem("y_done")
        y_kept = sem("y_kept")
        y_out = [sem("y_out0"), sem("y_out1")]
        LEAD = 4

        def each_block(eng, step):
            for b in range(LEAD):
                step(b, b % 2, b // 2)
            with eng.Fori(LEAD // 2, NB // 2 - 1) as i:
                for u in range(2):
                    step(2 * i + u, u, i)
            for b in range(NB - 2, NB):
                step(b, b % 2, b // 2)

        with nc.Block() as block:
            @block.sync
            def _(sp):
                def expert_of(b):
                    return sp.value_load(r["block_expert"][0:1, ds(b, 1)], min_val=0, max_val=NE - 1)

                def load_gu(b, u):
                    e = expert_of(b)
                    waited(sp, gu_done, b - 1)
                    sp.sem_inc(held_sp, 1)
                    for dst, src in ((wg, io["w_exp_gate"]), (wu, io["w_exp_up"])):
                        sp.dma_start(dst[:, u], src[0, ds(e, 1)].rearrange("o (k p) n -> p (o k) n", p=P)).then_inc(gu_in[u], 16)

                def load_d(b, u):
                    e = expert_of(b)
                    waited(sp, y_done, b - 1)
                    sp.sem_inc(held_sp, 1)
                    sp.dma_start(wd[:, u], io["w_exp_down"][0, ds(e, 1)].rearrange("o (k p) n -> p (o k) n", p=P)).then_inc(wd_in[u], 16)

                def store_y(b, u):
                    sp.wait_ge(y_kept, b + 1)
                    sp.sem_inc(held_sp, 1)
                    sp.dma_start(dram["y"][ds(b * P, P), :], y[:, u, :]).then_inc(y_out[u], 16)

                def step(b, u, i):
                    load_gu(b, u)
                    if not isinstance(b, int) or b >= 1:
                        load_d(b - 1, 1 - u)
                    if not isinstance(b, int) or b >= 3:
                        store_y(b - 3, 1 - u)
                each_block(sp, step)
                load_d(NB - 1, (NB - 1) % 2)
                for b in range(NB - 3, NB):
                    store_y(b, b % 2)
                for u in range(2):
                    sp.wait_ge(y_out[u], 16 * (NB // 2))

            @block.gpsimd
            def _(pool):
                def gather(b, u, i):
                    waited(pool, xT_done, b - 1)
                    pool.sem_inc(held_pool, 1)
                    nc.gpsimd.tensor_copy(idx[:, u:u + 1], r["row_token"][:, ds(b, 1)]).then_inc(idx_ready, 1)
                    pool.wait_ge(idx_ready, b + 1)
                    pool.sem_inc(held_pool, 1)
                    pool.indirect_dma_start(xg[:, u, :], None, dram["h2"][:, :],
                                            bass.IndirectOffsetOnAxis(ap=idx[:, u:u + 1], axis=0)).then_inc(x_in[u], 16)
                each_block(pool, gather)

            @block.tensor
            def _(pe):
                def turn_x(b, u, i):
                    pe.wait_ge(x_in[u], 16 * (i + 1))
                    for k in range(KD):
                        last = pe.transpose(ps_x[:, k, :], xg[:, u, k * P:(k + 1) * P], ident[:])
                    last.then_inc(xT_done, 1)

                def gate_up(b, u, i):
                    pe.wait_ge(xT_kept, b + 1)
                    pe.wait_ge(gu_in[u], 32 * (i + 1))
                    for n, w in enumerate((wg, wu)):
                        for k in range(KD):
                            last = pe.matmul(ps_gu[:, n, :], xT[:, k, :], w[:, u, k, :], start=(k == 0), stop=(k == KD - 1))
                    last.then_inc(gu_done, 1)

                def turn_h(b):
                    pe.wait_ge(hh_ready, b + 1)
                    for k in range(KF):
                        last = pe.transpose(ps_h[:, k, :], hh[:, k * P:(k + 1) * P], ident[:])
                    last.then_inc(hT_done, 1)

                def down(b, u, i):
                    pe.wait_ge(hT_kept, b + 1)
                    pe.wait_ge(wd_in[u], 16 * (i + 1))
                    waited(pe, y_kept, b)
                    for half in range(2):
                        for k in range(KF):
                            last = pe.matmul(ps_y[:, half, :], hT[:, k, :], wd[:, u, k, half * 512:(half + 1) * 512],
                                             start=(k == 0), stop=(k == KF - 1))
                    last.then_inc(y_done, 1)

                def step(b, u, i):
                    gate_up(b, u, i)
                    if not (isinstance(b, int) and b == NB - 1):
                        turn_x(b + 1, 1 - u, i + u)
                    if not (isinstance(b, int) and b == 0):
                        down(b - 1, 1 - u, i + u - 1)
                    turn_h(b)
                turn_x(0, 0, 0)
                each_block(pe, step)
                down(NB - 1, 1, NB // 2 - 1)

            @block.scalar
            def _(act):
                def keep_x(b):
                    act.wait_ge(xT_done, b + 1)
                    nc.scalar.activation(xT[:], ps_x[:], ACT.Copy).then_inc(xT_kept, 1)

                def silu(b):
                    act.wait_ge(gu_done, b + 1)
                    waited(act, hh_ready, b)
                    nc.scalar.activation(sg[:], ps_gu[:, 0, :], ACT.Silu).then_inc(sg_ready, 1)

                def keep_y(b, u, i):
                    waited(act, y_out[u], 16 * i)
                    act.wait_ge(y_done, b + 1)
                    nc.scalar.activation(y[:, u, :].rearrange("p (a n) -> p a n", a=2), ps_y[:], ACT.Copy).then_inc(y_kept, 1)

                def step(b, u, i):
                    silu(b)
                    if not (isinstance(b, int) and b == NB - 1):
                        keep_x(b + 1)
                    if not (isinstance(b, int) and b == 0):
                        keep_y(b - 1, 1 - u, i + u - 1)
                keep_x(0)
                each_block(act, step)
                keep_y(NB - 1, 1, NB // 2 - 1)

            @block.vector
            def _(dve):
                def step(b, u, i):
                    waited(dve, hT_done, b)
                    dve.wait_ge(sg_ready, b + 1)
                    nc.vector.tensor_tensor(hh[:], ps_gu[:, 1, :], sg[:], ALU.mult).then_inc(hh_ready, 1)
                    dve.wait_ge(hT_done, b + 1)
                    nc.vector.tensor_copy(hT[:], ps_h[:]).then_inc(hT_kept, 1)
                each_block(dve, step)


def combine(nc, io, out, dram, mem, r):
    with ExitStack() as ctx:
        def sb(name, shape, dt=F32):
            return ctx.enter_context(nc.sbuf_tensor(name, shape, dt))

        def sem(name):
            return ctx.enter_context(nc.semaphore(name))

        gate2 = sb("gate2", [P, 2, D])
        g_final = sb("g_final_b", [P, D])
        x = sb("c_x", [P, 2, D])
        ya = sb("c_ya", [P, 2, D])
        yb = sb("c_yb", [P, 2, D])
        yo = sb("c_out", [P, 2, D])
        idx = sb("c_idx", [P, 4], I32)
        st = sb("c_stats", [P, 6])
        eps = mem["eps"]
        par_in = sem("c_params_in")
        held_sp, held_pool, held_act, held_dve = (sem(f"c_held_{e}") for e in ("sp", "pool", "act", "dve"))
        x_in = [sem("c_x_in0"), sem("c_x_in1")]
        y_in = [sem("c_y_in0"), sem("c_y_in1")]
        idx_ready = sem("c_idx_ready")
        scaled = sem("c_scaled")
        mixed = sem("c_mixed")
        rooted = sem("c_rooted")
        out_ready = sem("c_out_ready")
        stored = [sem("c_stored0"), sem("c_stored1")]
        own = sem("c_dve_own")
        LEAD = 4

        def each_tile(eng, step):
            for n in range(LEAD):
                step(n, n % 2, n // 2)
            with eng.Fori(LEAD // 2, NT // 2 - 1) as i:
                for u in range(2):
                    step(2 * i + u, u, i)
            for n in range(NT - 2, NT + 1):
                step(n, n % 2, n // 2)

        def is_sample(n):
            return isinstance(n, int) and n == NT

        with nc.Block() as block:
            @block.sync
            def _(sp):
                sp.dma_start(gate2[:, 0, :], dram["mod"][0, MOD_GATE2]).then_inc(par_in, 16)
                sp.dma_start(gate2[:, 1, :], dram["mod"][1, MOD_GATE2]).then_inc(par_in, 16)
                sp.dma_start(g_final[:], io["g_final"].rearrange("(o d) -> o d", o=1).broadcast_to([P, D])).then_inc(par_in, 16)

                def load(n, u, i):
                    waited(sp, mixed, n - 1)
                    waited(sp, out_ready, n - 1)
                    sp.sem_inc(held_sp, 1)
                    if is_sample(n):
                        sp.dma_start(x[0:ST, u, :], dram["x2"][SEQ:NTOK, :]).then_inc(x_in[u], 16)
                    else:
                        sp.dma_start(x[:, u, :], dram["x2"][ds(n * P, P), :]).then_inc(x_in[u], 16)
                each_tile(sp, load)

            @block.gpsimd
            def _(pool):
                def gather(n, u, i):
                    waited(pool, mixed, n - 1)
                    pool.sem_inc(held_pool, 1)
                    col = 0 if is_sample(n) else n + 1
                    for k, dst in ((0, ya), (1, yb)):
                        at = idx[:, 2 * u + k:2 * u + k + 1]
                        nc.gpsimd.tensor_copy(at, r["dest"][:, k:k + 1, ds(col, 1)].rearrange("p o t -> p (o t)")).then_inc(idx_ready, 1)
                        pool.wait_ge(idx_ready, 2 * n + k + 1)
                        pool.sem_inc(held_pool, 1)
                        pool.indirect_dma_start(dst[:, u, :], None, dram["y"][:, :],
                                                bass.IndirectOffsetOnAxis(ap=at, axis=0)).then_inc(y_in[u], 16)
                each_tile(pool, gather)

            @block.scalar
            def _(act):
                def scale(n, u, i):
                    R, col = (ST, 0) if is_sample(n) else (P, n + 1)
                    act.wait_ge(y_in[u], 32 * (i + 1))
                    act.sem_inc(held_act, 1)
                    nc.scalar.activation(ya[0:R, u, :], ya[0:R, u, :], ACT.Copy,
                                         scale=r["gate"][0:R, 0:1, ds(col, 1)].rearrange("p o t -> p (o t)")).then_inc(scaled, 1)

                def root(n, u):
                    R = ST if is_sample(n) else P
                    act.wait_ge(mixed, n + 1)
                    nc.scalar.activation(st[0:R, 2 + u:3 + u], st[0:R, u:u + 1], ACT.Sqrt, bias=eps[0:R, 0:1],
                                         scale=1.0 / D).then_inc(rooted, 1)

                def store(n, u):
                    act.wait_ge(out_ready, n + 1)
                    act.sem_inc(held_act, 1)
                    if is_sample(n):
                        act.dma_start(out["y_sample"], yo[0:ST, u, :]).then_inc(stored[u], 16)
                    else:
                        act.dma_start(out["y_prompt"][ds(n * P, P), :], yo[:, u, :]).then_inc(stored[u], 16)

                def step(n, u, i):
                    if not is_sample(n):
                        scale(n + 1, 1 - u, i + u)
                    root(n, u)
                    if not (isinstance(n, int) and n == 0):
                        store(n - 1, 1 - u)
                scale(0, 0, 0)
                each_tile(act, step)
                store(NT, 0)
                act.wait_ge(stored[0], 16 * (NT // 2 + 1))
                act.wait_ge(stored[1], 16 * (NT // 2))

            @block.vector
            def _(dve):
                v = nc.vector
                LINKS = 3

                def mix(n, u, i, c):
                    R, col = (ST, 0) if is_sample(n) else (P, n + 1)
                    dve.wait_ge(scaled, n + 1)
                    dve.sem_inc(held_dve, 1)
                    c.link(v.scalar_tensor_tensor(out=yb[0:R, u, :], in0=yb[0:R, u, :],
                                                  scalar=r["gate"][0:R, 1:2, ds(col, 1)].rearrange("p o t -> p (o t)"),
                                                  in1=ya[0:R, u, :], op0=ALU.mult, op1=ALU.add))
                    c.link(v.tensor_tensor(yb[0:R, u, :], yb[0:R, u, :], gate2[0:R, 1 if is_sample(n) else 0, :], ALU.mult))
                    dve.wait_ge(x_in[u], 16 * (i + 1))
                    c.link(v.tensor_tensor(x[0:R, u, :], x[0:R, u, :], yb[0:R, u, :], ALU.add))
                    v.tensor_tensor_reduce(out=ya[0:R, u, :], in0=x[0:R, u, :], in1=x[0:R, u, :], scale=1.0, scalar=0.0,
                                           op0=ALU.mult, op1=ALU.add, accum_out=st[0:R, u:u + 1]).then_inc(mixed, 1)

                def finish(n, u, i, c):
                    R = ST if is_sample(n) else P
                    dve.wait_ge(rooted, n + 1)
                    c.link(v.reciprocal(st[0:R, 4 + u:5 + u], st[0:R, 2 + u:3 + u]))
                    waited(dve, stored[u], 16 * i)
                    v.scalar_tensor_tensor(out=yo[0:R, u, :], in0=x[0:R, u, :], scalar=st[0:R, 4 + u:5 + u],
                                           in1=g_final[0:R, :], op0=ALU.mult, op1=ALU.mult).then_inc(out_ready, 1)

                def step(n, u, i):
                    c = Chain(dve, own, (LINKS + 1) * n - (0 if isinstance(n, int) and n == 0 else 1))
                    mix(n, u, i, c)
                    if not (isinstance(n, int) and n == 0):
                        finish(n - 1, 1 - u, i + u - 1, c)
                dve.wait_ge(par_in, 48)
                each_tile(dve, step)
                finish(NT, 0, NT // 2, Chain(dve, own, (LINKS + 1) * (NT + 1) - 1))
def setup(nc, io, mem, ident, sel):
    with ExitStack() as ctx:
        def sb(name, shape, dt=F32):
            return ctx.enter_context(nc.sbuf_tensor(name, shape, dt))

        def sem(name):
            return stage_semaphore(nc, mem["used_semaphores"], name)

        ws = sb("ws", [P, GB, P])
        ws_s = sb("ws_s", [ST, GB, ST])
        tril = sb("tril", [P, P])
        tril_s = sb("tril_s", [ST, ST])
        pt = ctx.enter_context(nc.psum_tensor("ws_t", [P, GB, P], F32))
        pts = ctx.enter_context(nc.psum_tensor("ws_ts", [P, 512], F32))
        small_in = sem("setup_in")
        masked = sem("ws_masked")
        turned = sem("ws_turned")
        kept = sem("ws_kept")
        loads = [0]
        lam_rows = sb("lam_rows", [P, 4, DK])
        lam_prod = sb("lam_prod", [P, 2, DK])
        lam_sum = sb("lam_sum", [P, 2])
        lam_exp = sb("lam_exp", [P, 2])
        lam_sums = sem("lam_sums")
        lam_exps = sem("lam_exps")
        own = sem("setup_dve_own")
        with nc.Block() as block:
            @block.sync
            def _(sp):
                def load(dst, src):
                    sp.dma_start(dst, src).then_inc(small_in, 16)
                    loads[0] += 16

                load(ident[:], io["c_ident"])
                load(sel[:], io["c_sel"])
                load(lam_rows[:], io["lam_p"].broadcast_to([P, 4, DK]))
                load(mem["rope"][:], io["c_rope"])
                load(tril[:], io["c_tril"])
                load(tril_s[:], io["c_tril_s"])
                load(ws[:], io["w_s"][0].rearrange("g t s -> t g s"))
                w8 = io["w_s"][0, :, 0:DQ, 0:DQ].rearrange("g t s -> t g s")
                with nc.allow_non_contiguous_dma(reason="b_s by position, 8x8 corners of W_s"):
                    for b in range(DB):
                        for c in range(DB):
                            load(ws_s[DQ * b:DQ * (b + 1), :, DQ * c:DQ * (c + 1)], w8)
                        load(mem["bs_s"][DQ * b:DQ * (b + 1), :], io["b_s"][0, :, 0:DQ].rearrange("g t -> t g"))
                    load(mem["bs_p"][:], io["b_s"][0].rearrange("g t -> t g"))
                sp.wait_ge(small_in, loads[0])
                wd = io["w_in"][0].rearrange("(k p) n -> p k n", p=P)
                for k in range(KD):
                    sp.dma_start(mem["w_in"][:, k, :], wd[:, k, :]).then_inc(mem["w_in_sem"], 16)

            @block.vector
            def _(dve):
                nc.vector.memset(mem["eps"][:], EPS)
                dve.wait_ge(small_in, loads[0])
                nc.vector.tensor_tensor(ws[:], ws[:], tril[:].unsqueeze(1).to_broadcast([P, GB, P]), ALU.mult)\
                    .then_inc(masked, 1)
                nc.vector.tensor_tensor(ws_s[:], ws_s[:], tril_s[:].unsqueeze(1).to_broadcast([ST, GB, ST]), ALU.mult)\
                    .then_inc(masked, 1)
                chain = Chain(dve, own)
                chain.link(nc.vector.tensor_tensor(lam_prod[:], lam_rows[:, 0:4:2, :], lam_rows[:, 1:4:2, :], ALU.mult))
                nc.vector.tensor_reduce(lam_sum[:], lam_prod[:], AX.X, ALU.add).then_inc(lam_sums, 1)
                dve.wait_ge(lam_exps, 1)
                chain.link(nc.vector.tensor_tensor(mem["lam"][:], lam_exp[:, 0:1], lam_exp[:, 1:2], ALU.subtract))
                chain.link(nc.vector.tensor_scalar(mem["lam"][:], mem["lam"][:], LAM_INIT, None, ALU.add))
                dve.wait_ge(turned, 1)
                nc.vector.tensor_copy(mem["wsT_p"][:], pt[:]).then_inc(kept, 1)
                nc.vector.tensor_copy(mem["wsT_s"][:], pts[0:ST, 0:GB * ST].rearrange("s (g t) -> s g t", g=GB))\
                    .then_inc(kept, 1)

            @block.scalar
            def _(act):
                act.wait_ge(lam_sums, 1)
                nc.scalar.activation(lam_exp[:], lam_sum[:], ACT.Exp).then_inc(lam_exps, 1)

            @block.tensor
            def _(pe):
                pe.wait_ge(masked, 2)
                for g in range(GB):
                    pe.transpose(pt[:, g, :], ws[:, g, :], ident[:])
                    last = pe.transpose(pts[0:ST, g * ST:(g + 1) * ST], ws_s[:, g, :], ident[0:ST, 0:ST])
                last.then_inc(turned, 1)


def program(nc, io, out):
    def scratch(name, shape):
        return nc.dram_tensor(name, shape, F32).ap()

    dram = {
        "mod": scratch("scratch_mod", [2, 6, P, D]),
        "qT": scratch("scratch_qT", [NT, P, H, P]),
        "obT": scratch("scratch_obT", [NT, P, GB, P]),
        "x2": scratch("scratch_x2", [NTOK, D]),
        "h2": scratch("scratch_h2", [NTOK, D]),
        "y": scratch("scratch_y", [NB * P, D]),
    }
    with ExitStack() as ctx:
        def sb(name, shape, dt=F32, ctx=ctx):
            return ctx.enter_context(nc.sbuf_tensor(name, shape, dt))

        ident = sb("ident", [P, P])
        mem = {
            "ident": ident,
            "eps": sb("eps", [P, 1]),
            "lam": sb("lam", [P, 1]),
            "lg": sb("router_logits", [P, NT + 1, NEG_G + NE]),
            "w_in_sem": ctx.enter_context(nc.semaphore("w_in_loaded")),
            "w_in_count": 16 * KD,
            "used_semaphores": [],
        }
        with ExitStack() as attn:
            mem["kT"] = sb("kT", [P, H, SEQ], ctx=attn)
            mem["V"] = sb("V", [P, NT, AW], ctx=attn)
            mem["kT_new"] = sb("kT_new", [P, H, ST], ctx=attn)
            mem["V_new"] = sb("V_new", [ST, AW], ctx=attn)
            mem["qT_new"] = sb("qT_new", [P, H, ST], ctx=attn)
            mem["obT_new"] = sb("obT_new", [P, GB, ST], ctx=attn)
            mem["o_new"] = sb("o_new", [ST, AW], ctx=attn)
            with ExitStack() as proj:
                mem["w_in"] = sb("w_in_sb", [P, KD, INW], ctx=proj)
                mem["rope"] = sb("rope", [P, NT + 1, 2, 2, ROT // 2], ctx=proj)
                mem["wsT_p"] = sb("wsT_p", [P, GB, P], ctx=proj)
                mem["wsT_s"] = sb("wsT_s", [ST, GB, ST], ctx=proj)
                mem["bs_p"] = sb("bs_p", [P, GB], ctx=proj)
                mem["bs_s"] = sb("bs_s", [ST, GB], ctx=proj)
                with ExitStack() as first:
                    sel = sb("sel", [1 + DB, 2 * P], ctx=first)
                    setup(nc, io, mem, ident, sel)
                    modulation(nc, io, dram["mod"], ident, sel, mem["kT"][:], mem["used_semaphores"])
                front(nc, io, out, dram, mem)
            decode(nc, io, dram, mem)
            prompt(nc, io, dram, mem)
        routed = {
            "gate": sb("gate_weights", [P, 2, NT + 1]),
            "dest": sb("dest_rows", [P, 2, NT + 1], I32),
            "block_expert": sb("block_expert", [1, NB], I32),
            "row_token": sb("row_token", [P, NB]),
        }
        nc.clear_and_free_semaphores(mem["used_semaphores"])
        nc.all_engine_barrier()
        routing(nc, io, mem, routed)
        experts(nc, io, dram, mem, routed)
        combine(nc, io, out, dram, mem, routed)


_INS = ["x_prompt", "x_sample", "cache_k", "cache_v", "page_table", "c_prompt", "c_sample", "w_ada", "b_ada", "g_norm1",
        "w_in", "lam_p", "g_attn", "g_v", "w_s", "b_s", "g_mlp", "w_out", "g_norm2", "w_router_g", "b_router_g",
        "w_router_e", "b_router_e", "w_exp_gate", "w_exp_up", "w_exp_down", "g_final"]
_OUTS = {
    "y_prompt": ((SEQ, D), (1, SEQ, D)),
    "y_sample": ((ST, D), (DB, DQ, D)),
    "k_prompt": ((SEQ, QKW), (1, 1, SEQ, H, 2, DK)),
    "v_prompt": ((SEQ, AW), (1, 1, SEQ, H, DV)),
    "k_sample": ((ST, QKW), (1, DB, DQ, H, 2, DK)),
    "v_sample": ((ST, AW), (1, DB, DQ, H, DV)),
    "cv_sample": ((ST, BW), (1, DB, DQ, BW)),
}


def kernel(**inputs):
    import numpy as _np
    import concourse.bacc as _bacc
    from concourse import mybir as _mybir
    from concourse.bass_utils import run_bass_kernel_spmd as _run

    nc = _bacc.Bacc("TRN2", target_bir_lowering=False, num_devices=1)
    arrays = {n: _np.ascontiguousarray(inputs[n]) for n in _INS}
    arrays.update(constants())
    io, out = {}, {}
    for name, a in arrays.items():
        io[name] = nc.dram_tensor(name, a.shape, _mybir.dt.from_np(a.dtype), kind="ExternalInput").ap()
    for name, (shape, _) in _OUTS.items():
        out[name] = nc.dram_tensor(f"out_{name}", shape, _mybir.dt.float32, kind="ExternalOutput").ap()
    program(nc, io, out)
    r = _run(nc, [arrays], core_ids=[0])
    return tuple(r.results[0][f"out_{n}"].reshape(full) for n, (_, full) in _OUTS.items())
```

```python
import math
from contextlib import ExitStack

import numpy as np
import concourse.bass as bass
from concourse import mybir

F32 = mybir.dt.float32
I32 = mybir.dt.int32
ALU = mybir.AluOpType
ACT = mybir.ActivationFunctionType
AX = mybir.AxisListType
ds = bass.ds

P = 128
D = 1024
KD = D // P
SEQ = 2048
NT = SEQ // P
DB, DQ = 8, 8
ST = DB * DQ
PAST, PAGE = 8192, 128
NPG = PAST // PAGE
H, DK, DV = 4, 64, 128
AW = H * DV
QKW = H * 2 * DK
BW = D - AW
GB = 4
ROT = DK // 4
INW = 2 * QKW + AW + 2 * BW
NEG_G, EPG = 4, 8
NE = NEG_G * EPG
DE = 512
EPS = 1e-6
NEG = -1e30
LAM_INIT = 0.8 - 0.6 * math.exp(0.0)
SCALE = DK ** -0.5
NTOK = SEQ + ST
NB = (2 * NTOK + NE * (P - 1)) // P
ADA_RING = 4
W_IN_ORDER = (4, 3, 0, 1, 2)
SURE_BLOCKS = -(-2 * NTOK // P // 2) * 2
MOD_SHIFT1, MOD_GAIN1, MOD_GATE1, MOD_SHIFT2, MOD_GAIN2, MOD_GATE2 = range(6)


def waited(eng, sem, value):
    if not isinstance(value, int) or value > 0:
        eng.wait_ge(sem, value)


def stage_semaphore(nc, used, name):
    used.append(nc.alloc_semaphore(name=name))
    return used[-1]


class Chain:

    def __init__(self, eng, sem, base=0):
        self.eng, self.sem, self.base, self.n = eng, sem, base, 0

    def step(self, ins):
        ins.then_inc(self.sem, 1)
        self.n += 1

    def wait(self):
        self.eng.wait_ge(self.sem, self.base + self.n)

    def link(self, ins):
        self.step(ins)
        self.wait()


def modulation_inputs(nc, ctx, mem):
    def sb(name, shape):
        return ctx.enter_context(nc.sbuf_tensor(name, shape, F32))

    def sem(name):
        return stage_semaphore(nc, mem["used_semaphores"], name)

    return {
        "c_rows": sb("c_rows", [1 + DB, D]),
        "sel": sb("sel", [P, 1 + ST]),
        "w_ring": [x.rearrange("p (k n) -> p k n", k=KD)
                   for place in (mem["kT"][:].rearrange("p h t -> p (h t)"), mem["V"][:].rearrange("p t e -> p (t e)"))
                   for x in (place[:, 0:KD * 512], place[:, KD * 512:])],
        "b_rows": sb("b_ada_rows", [P, ADA_RING, 512]),
        "gains": sb("mod_gains", [1 + ST, 2, D]),
        "c_in": sem("c_in"),
        "g_in": sem("mod_g_in"),
        "w_in": [sem(f"w_ada_in{r}") for r in range(ADA_RING)],
        "b_in": [sem(f"b_ada_in{r}") for r in range(ADA_RING)],
    }


def load_ada_chunk(sp, io, m, c):
    cols = slice(c * 512, (c + 1) * 512)
    r = c % ADA_RING
    sp.dma_start(m["w_ring"][r], io["w_ada"][0].rearrange("(k p) n -> p k n", p=P)[:, :, cols]).then_inc(m["w_in"][r], 16)
    sp.dma_start(m["b_rows"][0:32, r, :], io["b_ada"][:, cols].broadcast_to([32, 512])).then_inc(m["b_in"][r], 16)


def load_w_in(sp, io, mem, c):
    cols = slice(c * 512, (c + 1) * 512)
    sp.dma_start(mem["w_in"][:, :, cols], io["w_in"][0].rearrange("(k p) n -> p k n", p=P)[:, :, cols])\
        .then_inc(mem["w_in_loaded"][c], 16)


def modulation(nc, io, mod_dram, mem, m, small):
    with ExitStack() as ctx:
        def sb(name, shape, dt=F32):
            return ctx.enter_context(nc.sbuf_tensor(name, shape, dt))

        def sem(name):
            return stage_semaphore(nc, mem["used_semaphores"], name)

        NC9 = 1 + DB
        ROWS = 1 + ST
        CH = 6 * D // 512
        ident, sel = mem["ident"], m["sel"]
        c_rows, w_ring, b_rows, gains = m["c_rows"], m["w_ring"], m["b_rows"], m["gains"]
        c_in, g_in, w_in, b_in = m["c_in"], m["g_in"], m["w_in"], m["b_in"]
        c_silu = sb("c_silu", [NC9, D])
        c_T = sb("c_T", [P, KD, 32])
        m_row = sb("mod_row", [P, 2, 512])
        spread = sb("mod_spread", [ROWS, 4, 512])
        ps_t = ctx.enter_context(nc.psum_tensor("mod_ps_t", [P, KD, 16], F32))
        ps_m = ctx.enter_context(nc.psum_tensor("mod_ps_m", [P, 2, 512], F32))
        ps_s = ctx.enter_context(nc.psum_tensor("mod_ps_s", [P, 2, 512], F32))
        zeroed = sem("mod_zeroed")
        silu_done = sem("silu_done")
        ct_done = sem("ct_done")
        ct_ready = sem("ct_ready")
        row_done = sem("mod_row_done")
        row_ready = sem("mod_row_ready")
        spread_done = sem("spread_done")
        spread_ready = sem("spread_ready")
        stored = [sem(f"mod_stored{r}") for r in range(4)]
        with nc.Block() as block:
            @block.sync
            def _(sp):
                sp.dma_start(c_rows[0:1, :], io["c_prompt"]).then_inc(c_in, 16)
                sp.dma_start(c_rows[1:NC9, :], io["c_sample"]).then_inc(c_in, 16)
                sp.dma_start(ident[:], io["c_ident"]).then_inc(c_in, 16)
                sp.dma_start(sel[:], io["c_sel"]).then_inc(c_in, 16)
                load_ada_chunk(sp, io, m, 0)
                sp.dma_start(gains[:, 0, :], io["g_norm1"].broadcast_to([ROWS, D])).then_inc(g_in, 16)
                sp.dma_start(gains[:, 1, :], io["g_norm2"].broadcast_to([ROWS, D])).then_inc(g_in, 16)
                for c in range(1, CH):
                    waited(sp, row_done, c - ADA_RING + 1)
                    waited(sp, row_ready, c - ADA_RING + 1)
                    load_ada_chunk(sp, io, m, c)
                load_w_in(sp, io, mem, W_IN_ORDER[0])

            @block.tensor
            def _(pe):
                pe.wait_ge(silu_done, 1)
                for k in range(KD):
                    last = pe.transpose(ps_t[:, k, 0:NC9], c_silu[:, k * P:(k + 1) * P], ident[0:NC9, 0:NC9])
                last.then_inc(ct_done, 1)
                pe.wait_ge(ct_ready, 1)
                for c in range(CH + 1):
                    if c < CH:
                        pe.wait_ge(w_in[c % ADA_RING], 16 * (c // ADA_RING + 1))
                        if c >= 2:
                            pe.wait_ge(row_ready, c - 1)
                        for k in range(KD):
                            g = 32 * (k % 4)
                            last = pe.matmul(ps_m[g:g + 32, c % 2, :], c_T[:, k, :], w_ring[c % ADA_RING][:, k, :],
                                             start=(k < 4), stop=(k >= KD - 4), skip_group_check=True)
                        last.then_inc(row_done, 1)
                    if c >= 1:
                        pe.wait_ge(row_ready, c)
                        if c >= 3:
                            pe.wait_ge(spread_ready, c - 2)
                        b = (c - 1) % 2
                        pe.matmul(ps_s[0:ROWS, b, :], sel[:], m_row[:, b, :], start=True, stop=True).then_inc(spread_done, 1)

            @block.scalar
            def _(act):
                act.wait_ge(c_in, 64)
                nc.scalar.activation(c_silu[:], c_rows[:], ACT.Silu).then_inc(silu_done, 1)
                load_small(nc, act, io, mem, small)
                for c in range(CH):
                    act.wait_ge(spread_ready, c + 1)
                    part, half = c // 2, c % 2
                    act.dma_start(mod_dram[part, :, half * 512:(half + 1) * 512], spread[:, c % 4, :]).then_inc(stored[c % 4], 16)
                for r in range(4):
                    act.wait_ge(stored[r], 16 * (CH // 4))

            @block.vector
            def _(dve):
                nc.vector.memset(c_T[:], 0.0).then_inc(zeroed, 1)
                nc.vector.memset(b_rows[32:P // 2], 0.0).then_inc(zeroed, 1)
                nc.vector.memset(b_rows[P // 2:P], 0.0).then_inc(zeroed, 1)
                dve.wait_ge(zeroed, 3)
                dve.wait_ge(ct_done, 1)
                nc.vector.tensor_copy(c_T[:, :, 0:NC9], ps_t[:, :, 0:NC9]).then_inc(ct_ready, 1)
                for c in range(CH + 1):
                    if c < CH:
                        dve.wait_ge(row_done, c + 1)
                        dve.wait_ge(b_in[c % ADA_RING], 16 * (c // ADA_RING + 1))
                        if c >= 2:
                            dve.wait_ge(spread_done, c - 1)
                        nc.vector.tensor_tensor(m_row[:, c % 2, :], ps_m[:, c % 2, :], b_rows[:, c % ADA_RING, :],
                                                ALU.add).then_inc(row_ready, 1)
                    if c >= 1:
                        j = c - 1
                        part, half = j // 2, j % 2
                        dve.wait_ge(spread_done, j + 1)
                        dve.wait_ge(g_in, 32)
                        waited(dve, stored[j % 4], 16 * (j // 4))
                        if part in (MOD_GAIN1, MOD_GAIN2):
                            g = gains[:, part // 3, half * 512:(half + 1) * 512]
                            nc.vector.scalar_tensor_tensor(out=spread[:, j % 4, :], in0=ps_s[0:ROWS, j % 2, :], scalar=1.0,
                                                           in1=g, op0=ALU.add, op1=ALU.mult).then_inc(spread_ready, 1)
                        else:
                            nc.vector.tensor_copy(spread[:, j % 4, :], ps_s[0:ROWS, j % 2, :]).then_inc(spread_ready, 1)


def prompt_mod(dram, part):
    return dram["mod"][part, 0:1, :].broadcast_to([P, D])


def sample_mod(dram, part):
    return dram["mod"][part, 1:1 + ST, :]


def front(nc, io, out, dram, mem):
    with ExitStack() as ctx:
        def sb(name, shape, dt=F32):
            return ctx.enter_context(nc.sbuf_tensor(name, shape, dt))

        def sem(name):
            return stage_semaphore(nc, used, name)

        ident, used = mem["ident"], mem["used_semaphores"]
        w = mem["w_in"]
        kT, V = mem["kT"], mem["V"]
        kT_new, V_new, qT_new, obT_new = mem["kT_new"], mem["V_new"], mem["qT_new"], mem["obT_new"]
        gain = sb("gain1", [P, D])
        shift = sb("shift1", [P, D])
        g_v = sb("g_v_b", [P, BW])
        g_mlp = sb("g_mlp_b", [P, BW])
        x = sb("x_in", [P, D])
        h = sb("h", [P, D])
        hT = sb("hT", [P, KD, P])
        qk = sb("qk", [P, 2 * QKW])
        r1 = sb("rope_t1", [P, 16, 2, ROT // 2])
        r2 = sb("rope_t2", [P, 16, 2, ROT // 2])
        u = sb("u", [P, BW])
        gv = sb("gv", [P, BW])
        sq = sb("sq", [P, BW])
        vn = sb("vn", [P, BW])
        ob = sb("ob", [P, BW])
        qT = sb("qT", [P, H, P])
        obT = sb("obT", [P, GB, P])
        st = sb("stats", [P, 32])
        eps = mem["eps"]
        wsT = [mem["wsT_s"], mem["wsT_p"]]
        bs = [mem["bs_s"], mem["bs_p"]]
        z = ctx.enter_context(nc.psum_tensor("z", [P, 5, 512], F32))
        tr = ctx.enter_context(nc.psum_tensor("tr", [P, 8, P], F32))
        mix = ctx.enter_context(nc.psum_tensor("mix", [P, GB, P], F32))
        ZQ, ZK, ZV, ZU, ZG = range(5)

        par_in = sem("front_params_in")
        par_p_in = sem("front_prompt_mod_in")
        held_sp = sem("front_held_sp")
        held_pool = sem("front_held_pool")
        held_act = sem("front_held_act")
        x_in = sem("x_in_sem")
        rope_in = [sem("rope_in0"), sem("rope_in1")]
        x_ss = sem("x_ss")
        x_std = sem("x_std")
        h_ready = sem("h_ready")
        hT_done = sem("hT_done")
        hT_ready = sem("hT_ready")
        z_done = [sem(f"z_done{i}") for i in range(5)]
        gv_ready = sem("gv_ready")
        u_ready = sem("u_ready")
        gv_ss = sem("gv_ss")
        gv_std = sem("gv_std")
        vn_ready = sem("vn_ready")
        mix_done = sem("mix_done")
        ob_ss = sem("ob_ss")
        ob_std = sem("ob_std")
        ob_ready = sem("ob_ready")
        qk_copied = sem("qk_copied")
        qk_ready = sem("qk_ready")
        v_ready = sem("v_ready")
        qkT_done = sem("qkT_done")
        obT_done = sem("obT_done")
        qT_ready = sem("qT_ready")
        kT_ready = sem("kT_ready")
        obT_ready = sem("obT_ready")
        k_out = sem("k_out")
        v_out = sem("v_out")
        cv_out = sem("cv_out")
        q_out = sem("q_out")
        ob_out = sem("ob_out")
        own = sem("front_dve_own")

        def each_tile(eng, step):
            step(0, None, ST, False)
            step(1, 0, P, False)
            with eng.Fori(1, NT - 1) as p:
                step(p + 1, p, P, False)
            step(NT, NT - 1, P, True)

        with nc.Block() as block:
            @block.sync
            def _(sp):
                sp.dma_start(gain[0:ST, :], sample_mod(dram, MOD_GAIN1)).then_inc(par_in, 16)
                sp.dma_start(shift[0:ST, :], sample_mod(dram, MOD_SHIFT1)).then_inc(par_in, 16)
                sp.dma_start(g_v[:], io["g_v"].broadcast_to([P, BW])).then_inc(par_in, 16)
                sp.dma_start(g_mlp[:], io["g_mlp"].broadcast_to([P, BW])).then_inc(par_in, 16)
                sp.dma_start(x[0:ST, :], io["x_sample"].rearrange("b q d -> (b q) d")).then_inc(x_in, 16)
                for c in W_IN_ORDER[1:]:
                    load_w_in(sp, io, mem, c)

                def step(n, p, R, last):
                    if not last:
                        sp.wait_ge(h_ready, n + 1)
                        nxt = 0 if p is None else p + 1
                        if p is None:
                            sp.dma_start(gain[:], prompt_mod(dram, MOD_GAIN1)).then_inc(par_p_in, 16)
                            sp.dma_start(shift[:], prompt_mod(dram, MOD_SHIFT1)).then_inc(par_p_in, 16)
                        sp.sem_inc(held_sp, 1)
                        sp.dma_start(x[:], io["x_prompt"][0, ds(nxt * P, P), :]).then_inc(x_in, 16)
                each_tile(sp, step)

            @block.gpsimd
            def _(pool):
                def step(n, p, R, last):
                    if p is not None:
                        pool.wait_ge(qk_ready, n + 1)
                        pool.sem_inc(held_pool, 1)
                        pool.dma_start(out["k_prompt"][ds(p * P, P), :], qk[:, QKW:2 * QKW]).then_inc(k_out, 16)
                        pool.wait_ge(v_ready, n + 1)
                        pool.sem_inc(held_pool, 1)
                        pool.dma_start(out["v_prompt"][ds(p * P, P), :], V[:, ds(p, 1), :]).then_inc(v_out, 16)
                        pool.wait_ge(qT_ready, n + 1)
                        pool.sem_inc(held_pool, 1)
                        pool.dma_start(dram["qT"][ds(p, 1)], qT[:]).then_inc(q_out, 16)
                        pool.wait_ge(obT_ready, n + 1)
                        pool.sem_inc(held_pool, 1)
                        pool.dma_start(dram["obT"][ds(p, 1)], obT[:]).then_inc(ob_out, 16)
                        pool.wait_ge(k_out, (n + 1) * 16)
                        pool.wait_ge(v_out, (n + 1) * 16)
                        pool.wait_ge(q_out, n * 16)
                        pool.wait_ge(ob_out, n * 16)
                    else:
                        pool.wait_ge(vn_ready, 1)
                        pool.dma_start(out["cv_sample"], vn[0:ST, :]).then_inc(cv_out, 16)
                        pool.wait_ge(qk_ready, 1)
                        pool.dma_start(out["k_sample"], qk[0:ST, QKW:2 * QKW]).then_inc(k_out, 16)
                        pool.wait_ge(v_ready, 1)
                        pool.dma_start(out["v_sample"], V_new[:]).then_inc(v_out, 16)
                        pool.wait_ge(cv_out, 16)
                        pool.wait_ge(k_out, 16)
                        pool.wait_ge(v_out, 16)
                each_tile(pool, step)

            @block.tensor
            def _(pe):
                def transpose_h(n, R):
                    pe.wait_ge(h_ready, n + 1)
                    for k in range(KD):
                        last = pe.transpose(z[:, ZQ + k // 4, (k % 4) * P:(k % 4) * P + R], h[0:R, k * P:(k + 1) * P],
                                            ident[0:R, 0:R])
                    last.then_inc(hT_done, 1)

                def step(n, p, R, last_tile):
                    who = int(p is not None)
                    pe.wait_ge(hT_ready, n + 1)
                    for c in (ZG, ZU, ZQ, ZK, ZV):
                        if c == ZG:
                            waited(pe, gv_ready, n)
                        if c == ZU:
                            waited(pe, u_ready, n)
                        if c == ZV:
                            waited(pe, v_ready, n)
                        if who == 0:
                            pe.wait_ge(mem["w_in_loaded"][c], 16)
                        for k in range(KD):
                            last = pe.matmul(z[0:R, c, :], hT[:, k, 0:R], w[:, k, c * 512:(c + 1) * 512],
                                             start=(k == 0), stop=(k == KD - 1))
                        last.then_inc(z_done[c], 1)
                        if c == ZK:
                            pe.wait_ge(vn_ready, n + 1)
                            waited(pe, obT_ready, n)
                            for g in range(GB):
                                last = pe.matmul(mix[0:R, g, :], wsT[who][0:R, g, 0:R], vn[0:R, g * P:(g + 1) * P],
                                                 start=True, stop=True)
                            last.then_inc(mix_done, 1)
                    if not last_tile:
                        pe.wait_ge(qk_ready, n + 1)
                        transpose_h(n + 1, P)
                    pe.wait_ge(qk_ready, n + 1)
                    waited(pe, kT_ready, n)
                    for b in range(8):
                        last = pe.transpose(tr[:, b, 0:R], qk[0:R, b * P:(b + 1) * P], ident[0:R, 0:R])
                    last.then_inc(qkT_done, 1)
                    pe.wait_ge(ob_ready, n + 1)
                    for b in range(GB):
                        last = pe.transpose(mix[:, b, 0:R], ob[0:R, b * P:(b + 1) * P], ident[0:R, 0:R])
                    last.then_inc(obT_done, 1)

                transpose_h(0, ST)
                each_tile(pe, step)

            @block.scalar
            def _(act):
                def root(done, ready, n, R, s, cnt, width):
                    act.wait_ge(done, n + 1)
                    nc.scalar.activation(st[0:R, s + 8:s + 8 + cnt], st[0:R, s:s + cnt], ACT.Sqrt,
                                         bias=eps[0:R, 0:1], scale=1.0 / width).then_inc(ready, 1)

                def hT_copy(n, R):
                    act.wait_ge(hT_done, n + 1)
                    nc.scalar.activation(hT[:, :, 0:R],
                                         z[:, ZQ:ZQ + 2, :].rearrange("p a (b r) -> p (a b) r", r=P)[:, :, 0:R],
                                         ACT.Copy).then_inc(hT_ready, 1)

                def step(n, p, R, last):
                    act.wait_ge(z_done[ZG], n + 1)
                    nc.scalar.activation(gv[0:R, :], z[0:R, ZG, :], ACT.Gelu_apprx_tanh).then_inc(gv_ready, 1)
                    act.wait_ge(z_done[ZU], n + 1)
                    waited(act, ob_ready, n)
                    nc.scalar.activation(u[0:R, :], z[0:R, ZU, :], ACT.Gelu_apprx_tanh).then_inc(u_ready, 1)
                    root(gv_ss, gv_std, n, R, 0, GB, P)
                    act.wait_ge(z_done[ZK], n + 1)
                    waited(act, qkT_done, n)
                    waited(act, k_out, 16 * n)
                    nc.scalar.activation(qk[0:R, :], z[0:R, ZQ:ZQ + 2, :].rearrange("p a b -> p (a b)"),
                                         ACT.Copy).then_inc(qk_copied, 1)
                    if not last:
                        root(x_ss, x_std, n + 1, P, 4, 1, D)
                    act.wait_ge(z_done[ZV], n + 1)
                    act.sem_inc(held_act, 1)
                    dst = V_new[:] if p is None else V[:, ds(p, 1), :]
                    nc.scalar.activation(dst, z[0:R, ZV, :], ACT.Copy).then_inc(v_ready, 1)
                    root(ob_ss, ob_std, n, R, 16, GB, P)
                    if not last:
                        hT_copy(n + 1, P)
                    act.wait_ge(qkT_done, n + 1)
                    waited(act, q_out, 16 * (n - 1))
                    nc.scalar.activation((qT_new if p is None else qT)[:, :, 0:R], tr[:, 0:4, 0:R],
                                         ACT.Copy).then_inc(qT_ready, 1)
                    dst = kT_new[:] if p is None else kT[:, :, ds(p * P, P)]
                    nc.scalar.activation(dst, tr[:, 4:8, 0:R], ACT.Copy).then_inc(kT_ready, 1)
                    act.wait_ge(obT_done, n + 1)
                    waited(act, ob_out, 16 * (n - 1))
                    nc.scalar.activation((obT_new if p is None else obT)[:, :, 0:R], mix[:, :, 0:R],
                                         ACT.Copy).then_inc(obT_ready, 1)

                root(x_ss, x_std, 0, ST, 4, 1, D)
                hT_copy(0, ST)
                each_tile(act, step)

            LINKS = 14

            @block.vector
            def _(dve):
                v = nc.vector

                def norm_x(n, R, chain):
                    dve.wait_ge(x_in, 16 * (n + 1))
                    if isinstance(n, int) and n == 1:
                        dve.wait_ge(par_p_in, 32)
                    v.tensor_tensor_reduce(out=h[0:R, :], in0=x[0:R, :], in1=x[0:R, :], scale=1.0, scalar=0.0,
                                           op0=ALU.mult, op1=ALU.add, accum_out=st[0:R, 4:5]).then_inc(x_ss, 1)
                    dve.wait_ge(x_std, n + 1)
                    chain.link(v.reciprocal(st[0:R, 5:6], st[0:R, 12:13]))
                    chain.link(v.scalar_tensor_tensor(out=h[0:R, :], in0=x[0:R, :], scalar=st[0:R, 5:6],
                                                      in1=gain[0:R, :], op0=ALU.mult, op1=ALU.mult))
                    v.tensor_tensor(h[0:R, :], h[0:R, :], shift[0:R, :], ALU.add).then_inc(h_ready, 1)

                def group_norm(src, dst, gains, R, s, ss, std, done, n, chain):
                    g3 = "p (g c) -> p g c"
                    chain.link(v.tensor_tensor(sq[0:R, :], src[0:R, :], src[0:R, :], ALU.mult))
                    v.tensor_reduce(st[0:R, s:s + GB], sq[0:R, :].rearrange(g3, g=GB), AX.X, ALU.add).then_inc(ss, 1)
                    dve.wait_ge(std, n + 1)
                    chain.link(v.reciprocal(st[0:R, 28:28 + GB], st[0:R, s + 8:s + 8 + GB]))
                    chain.link(v.tensor_tensor(sq[0:R, :].rearrange(g3, g=GB), src[0:R, :].rearrange(g3, g=GB),
                                               st[0:R, 28:28 + GB].unsqueeze(2).to_broadcast([R, GB, P]), ALU.mult))
                    v.tensor_tensor(dst[0:R, :], sq[0:R, :], gains[0:R, :], ALU.mult).then_inc(done, 1)

                def step(n, p, R, last):
                    who = int(p is not None)
                    chain = Chain(dve, own, n * LINKS + 2)
                    waited(dve, cv_out, 16 if not isinstance(n, int) or n else 0)
                    dve.wait_ge(gv_ready, n + 1)
                    group_norm(gv, vn, g_v, R, 0, gv_ss, gv_std, vn_ready, n, chain)
                    dve.wait_ge(qk_copied, n + 1)
                    zz = qk[0:R, :].rearrange("p (m d) -> p m d", d=DK)
                    hr = ROT // 2
                    tab = rope_at(n, R)
                    chain.step(v.tensor_tensor(r1[0:R], zz[:, :, 0:hr].unsqueeze(2).to_broadcast([R, 16, 2, hr]),
                                               tab(0), ALU.mult))
                    chain.link(v.tensor_tensor(r2[0:R], zz[:, :, hr:ROT].unsqueeze(2).to_broadcast([R, 16, 2, hr]),
                                               tab(1), ALU.mult))
                    v.tensor_tensor(qk[0:R, :].rearrange("p (m d) -> p m d", d=DK)[:, :, 0:ROT],
                                    r1[0:R].rearrange("p m t j -> p m (t j)"), r2[0:R].rearrange("p m t j -> p m (t j)"),
                                    ALU.add).then_inc(qk_ready, 1)
                    if not last:
                        dve.wait_ge(hT_done, n + 1)
                        norm_x(n + 1, P, chain)
                    dve.wait_ge(mix_done, n + 1)
                    dve.wait_ge(u_ready, n + 1)
                    waited(dve, obT_done, n)
                    for g in range(GB):
                        chain.step(v.scalar_tensor_tensor(out=u[0:R, g * P:(g + 1) * P], in0=mix[0:R, g, :],
                                                          scalar=bs[who][0:R, g:g + 1], in1=u[0:R, g * P:(g + 1) * P],
                                                          op0=ALU.add, op1=ALU.mult))
                    chain.wait()
                    group_norm(u, ob, g_mlp, R, 16, ob_ss, ob_std, ob_ready, n, chain)
                    assert chain.n == (LINKS if not last else LINKS - 2), chain.n

                def rope_at(n, R):
                    t = mem["rope"]
                    src = t[0:R, ds(n, 1)].rearrange("p o a t j -> p (o a) t j")
                    return lambda a: src[:, a].unsqueeze(1).to_broadcast([R, 16, 2, ROT // 2])

                dve.wait_ge(par_in, 64)
                norm_x(0, ST, Chain(dve, own, 0))
                each_tile(dve, step)
def constants():
    f = np.float32
    inv = (f(500000.0) ** (-np.arange(0, ROT, 2, dtype=f) / f(ROT))).astype(f)
    pos = np.zeros((NT + 1, P), f)
    pos[0, :ST] = PAST + np.arange(ST) % DQ
    pos[1:] = np.arange(SEQ).reshape(NT, P)
    ang = pos[:, :, None] * inv
    cos, sin = np.cos(ang), np.sin(ang)
    rope = np.stack([np.stack([cos, sin], 2), np.stack([-sin, cos], 2)], 2)
    t = np.arange(P)
    s = np.arange(ST)
    sel = np.zeros((P, 1 + ST), f)
    for j in range(4):
        sel[32 * j, 0] = 1
        sel[32 * j + 1 + s // DQ, 1 + s] = 1
    same = s[:, None] // DQ == s[None, :] // DQ
    row = np.arange(P)
    rq, rm, used = row % DQ, (row // DQ) % 2, row % 32 < 2 * DQ
    key_b, key_q = s // DQ, s % DQ
    ok = (key_b[None, :, None] == np.arange(DB)[:, None, None]) & (key_q[None, :, None] <= rq[None, None, :])
    mask_new = np.where(ok.transpose(2, 0, 1), 0, NEG).astype(f)
    pick = np.zeros((P, DB, H, ST), f)
    for b in range(DB):
        for r in row[used]:
            pick[r, b, r // 32, DQ * b + rq[r]] = 1
    kk = np.arange(512)
    mask_p = np.where(kk[None, None, :] <= (np.arange(4)[None, :, None] * P + t[:, None, None]), 0, NEG).astype(f)
    e = np.arange(NE)
    return {
        "c_ident": np.eye(P, dtype=f),
        "c_rope": np.ascontiguousarray(rope.transpose(1, 0, 2, 3, 4)).astype(f),
        "c_tril": (t[None, :] <= t[:, None]).astype(f),
        "c_tril_s": (same & (s[None, :] <= s[:, None])).astype(f),
        "c_sel": sel,
        "c_mask_new": mask_new,
        "c_pick": pick,
        "c_coef": np.stack([(used & (rm == 0)), -1.0 * (used & (rm == 1))], 1).astype(f),
        "c_coef_p": np.tile(np.array([1, -1], f), (P, 1)),
        "c_mask_p": mask_p,
        "c_before": (t[:, None] < t[None, :]).astype(f),
        "c_iota": np.tile(np.arange(P, dtype=f), (P, 1)),
        "c_first": (e[None, :] < e[:, None]).astype(f).reshape(1, NE * NE),
        "c_tok": (np.arange(P)[:, None] + np.array([SEQ] + [P * i for i in range(NT)])[None, :]).astype(f),
    }


def decode(nc, io, dram, mem):
    with ExitStack() as ctx:
        def sb(name, shape, dt=F32):
            return ctx.enter_context(nc.sbuf_tensor(name, shape, dt))

        def sem(name):
            return stage_semaphore(nc, mem["used_semaphores"], name)

        PS = 4
        STEPS = NPG // PS
        ALL = DB * STEPS
        W = PS * PAGE
        RING = 4
        GROUPS = STEPS // RING
        ident = mem["ident"]
        kT_new, V_new, qT_new = mem["kT_new"], mem["V_new"], mem["qT_new"]
        table = sb("pages", [1, DB * NPG], I32)
        k_ring = sb("k_ring", [P, RING, PS, QKW])
        v_ring = sb("v_ring", [P, RING, PS, AW])
        kTs = sb("kTs", [P, 2, H, W])
        probs = sb("probs", [P, 2, W])
        pT = sb("pT", [P, 2, PS, P])
        q_all = sb("q_all", [P, DB, H, 32])
        q_cur = sb("q_cur", [P, H, 32])
        mask_new = sb("mask_new", [P, DB, ST])
        o_new = sb("o_of_new", [P, DB, DV])
        mx_new = sb("mx_new", [P, DB])
        neg_new = sb("neg_new", [P, DB])
        sums_new = sb("sums_new", [P, DB])
        mx = sb("step_max", [P, 2])
        neg_max = sb("neg_max", [P, ALL])
        sums = sb("sums", [P, ALL])
        o_steps = sb("o_steps", [P, 2, STEPS, DV])
        weighted = sb("o_weighted", [P, STEPS, DV])
        scores_new, probs_new = (weighted[:, 4 * k:4 * (k + 1), :].rearrange("p g (two s) -> p (g two) s", two=2) for k in range(2))
        pT_new = weighted[0:ST, 8:16, :]
        o_sum = sb("o_sum", [P, DV])
        gap = sb("gap", [P, STEPS + 1])
        wt = sb("step_weights", [P, STEPS + 1])
        lw = sb("weighted_sums", [P, STEPS + 1])
        top = sb("top", [P, 4])
        coef = sb("coef", [P, 4])
        o_all = sb("o_all", [P, DB, DV])
        pick = k_ring[:, 0].rearrange("p j n -> p (j n)").rearrange("p (b h s) -> p b h s", b=DB, h=H)
        ps_k = ctx.enter_context(nc.psum_tensor("ps_k", [P, H, W], F32))
        ps_s = ctx.enter_context(nc.psum_tensor("ps_s", [P, 2, W], F32))
        ps_p = ctx.enter_context(nc.psum_tensor("ps_p", [P, PS, P], F32))
        ps_o = ctx.enter_context(nc.psum_tensor("ps_o", [P, 512], F32))
        ps_pT_new = ps_k[:, 0:2, :].rearrange("p a (b t) -> p (a b) t", t=P)
        ps_o_new = ps_k[:, 2:4, :].rearrange("p a (b t) -> p (a b) t", t=DV)

        params_in = sem("dec_params_in")
        table_in = sem("table_in")
        k_in = [sem(f"k_in{u}") for u in range(RING)]
        v_in = [sem(f"v_in{u}") for u in range(RING)]
        pick_in = sem("pick_in")
        held_sp, held_act, held_dve, held_pool = (sem(f"dec_held_{e}") for e in ("sp", "act", "dve", "pool"))
        q_made = sem("q_made")
        new_done = sem("new_done")
        bias_new = sem("bias_new")
        e_new = sem("e_new")
        pT_new_done = sem("pT_new_done")
        pT_new_kept = sem("pT_new_kept")
        pv_new = sem("pv_new")
        o_new_kept = sem("o_new_kept")
        q_ready = sem("q_ready")
        kT_done = [sem(f"dkT_done{h}") for h in range(H)]
        kT_kept = [sem(f"dkT_kept{h}") for h in range(H)]
        s_done = sem("s_done")
        mx_done = sem("mx_done")
        bias_done = sem("bias_done")
        e_done = sem("e_done")
        pT_done = sem("pT_done")
        pT_kept = sem("pT_kept")
        pv_done = sem("pv_done")
        o_kept = sem("o_kept")
        gap_ready = sem("dec_gap_ready")
        w_ready = sem("dec_w_ready")
        seq_done = sem("seq_done")
        picked = sem("picked")
        own = sem("dec_dve_own")

        def every_step(eng, start, step, finish, drain):
            def group(b, i):
                for u in range(RING):
                    step(STEPS * b + RING * i + u, u, GROUPS * b + i)
            start(0)
            group(0, 0)
            with eng.Fori(1, GROUPS) as i:
                group(0, i)
            with eng.Fori(1, DB - 1) as b:
                start(b)
                group(b, 0)
                finish(b - 1)
                with eng.Fori(1, GROUPS) as i:
                    group(b, i)
            start(DB - 1)
            group(DB - 1, 0)
            finish(DB - 2)
            with eng.Fori(1, GROUPS - 1) as i:
                group(DB - 1, i)
            group(DB - 1, GROUPS - 1)
            drain()
            finish(DB - 1)

        def every_page_slot(eng, load):
            for n in range(RING):
                load(n, n)
            with eng.Fori(1, ALL // RING) as i:
                for u in range(RING):
                    load(RING * i + u, u)

        def pages(eng, cache, layout, ring, n, u, arrived):
            for j in range(PS):
                page = eng.value_load(table[0:1, ds(n * PS + j, 1)], min_val=0, max_val=cache.shape[1] - 1)
                eng.dma_start(ring[:, u, j, :], cache[0, ds(page, 1)].rearrange(layout)).then_inc(arrived[u], 16)

        def nothing(*_):
            return None

        def is_first(n):
            return isinstance(n, int) and n == 0

        def is_last(n):
            return isinstance(n, int) and n == ALL - 1

        with nc.Block() as block:
            @block.sync
            def _(sp):
                sp.dma_start(table[:], io["page_table"].rearrange("(o b) n -> o (b n)", o=1)).then_inc(table_in, 16)
                sp.dma_start(mask_new[:], io["c_mask_new"]).then_inc(params_in, 16)
                sp.dma_start(coef[:, 0:2], io["c_coef"]).then_inc(params_in, 16)
                sp.wait_ge(table_in, 16)

                def load_k(n, u):
                    waited(sp, kT_done[H - 1], n - RING + 1)
                    sp.sem_inc(held_sp, 1)
                    pages(sp, io["cache_k"], "o p h m d -> p (o h m d)", k_ring, n, u, k_in)
                every_page_slot(sp, load_k)
                sp.wait_ge(kT_done[H - 1], ALL - RING + 1)
                sp.dma_start(pick, io["c_pick"]).then_inc(pick_in, 16)

            @block.gpsimd
            def _(pool):
                pool.wait_ge(table_in, 16)

                def load_v(n, u):
                    waited(pool, pv_done, n - RING + 1)
                    pool.sem_inc(held_pool, 1)
                    pages(pool, io["cache_v"], "o p h e -> p (o h e)", v_ring, n, u, v_in)
                every_page_slot(pool, load_v)

            @block.tensor
            def _(pe):
                pe.wait_ge(q_made, 2)
                for b in range(DB):
                    for h in range(H):
                        last = pe.matmul(ps_s[32 * h:32 * h + 32, 0, b * ST:(b + 1) * ST], q_all[:, b, h, :], kT_new[:, h, :],
                                         start=True, stop=True, skip_group_check=True)
                last.then_inc(new_done, 1)
                pe.wait_ge(e_new, DB)
                for b in range(DB):
                    last = pe.transpose(ps_pT_new[0:ST, b, :], probs_new[:, b, :], ident[:])
                last.then_inc(pT_new_done, 1)
                pe.wait_ge(pT_new_kept, 1)
                for b in range(DB):
                    for h in range(H):
                        last = pe.matmul(ps_o_new[32 * h:32 * h + 32, b, :], pT_new[:, b, 32 * h:32 * h + 32],
                                         V_new[:, h * DV:(h + 1) * DV], start=True, stop=True, skip_group_check=True)
                last.then_inc(pv_new, 1)
                pe.wait_ge(o_new_kept, 1)

                def turn_k(n, u, round_):
                    pe.wait_ge(k_in[u], 16 * PS * (round_ + 1))
                    for h in range(H):
                        waited(pe, kT_kept[h], n)
                        for j in range(PS):
                            last = pe.transpose(ps_k[:, h, j * P:(j + 1) * P], k_ring[:, u, j, h * P:(h + 1) * P], ident[:])
                        last.then_inc(kT_done[h], 1)

                def score(n, u):
                    for h in range(H):
                        pe.wait_ge(kT_kept[h], n + 1)
                    waited(pe, e_done, n - 1)
                    for h in range(H):
                        last = pe.matmul(ps_s[32 * h:32 * h + 32, u % 2, :], q_cur[:, h, :], kTs[:, u % 2, h, :],
                                         start=True, stop=True, skip_group_check=True)
                    last.then_inc(s_done, 1)

                def turn_p(n, u):
                    pe.wait_ge(e_done, n + 1)
                    waited(pe, pT_kept, n)
                    for j in range(PS):
                        last = pe.transpose(ps_p[:, j, :], probs[:, u % 2, j * P:(j + 1) * P], ident[:])
                    last.then_inc(pT_done, 1)

                def times_v(n, u, round_):
                    pe.wait_ge(pT_kept, n + 1)
                    pe.wait_ge(v_in[u], 16 * PS * (round_ + 1))
                    waited(pe, o_kept, n)
                    for j in range(PS):
                        for h in range(H):
                            last = pe.matmul(ps_o[32 * h:32 * h + 32, 0:DV], pT[:, u % 2, j, 32 * h:32 * h + 32],
                                             v_ring[:, u, j, h * DV:(h + 1) * DV], start=(j == 0), stop=(j == PS - 1),
                                             skip_group_check=True)
                    last.then_inc(pv_done, 1)

                def start(b):
                    pe.wait_ge(q_ready, b + 1)

                def step(n, u, round_):
                    before = (n - 1, (u - 1) % RING, round_ - (u == 0))
                    if not is_last(n):
                        turn_k(n + 1, (u + 1) % RING, round_ + (u == RING - 1))
                    if not is_first(n):
                        turn_p(*before[:2])
                    score(n, u)
                    if not is_first(n):
                        times_v(*before)

                def drain():
                    turn_p(ALL - 1, RING - 1)
                    times_v(ALL - 1, RING - 1, ALL // RING - 1)
                turn_k(0, 0, 0)
                every_step(pe, start, step, nothing, drain)
                pe.wait_ge(pick_in, 16)
                pe.wait_ge(seq_done, DB + 2)
                for h in range(H):
                    for b in range(DB):
                        last = pe.matmul(ps_s[0:ST, 0, h * DV:(h + 1) * DV], pick[:, b, h, :], o_all[:, b, :],
                                         start=(b == 0), stop=(b == DB - 1))
                last.then_inc(picked, 1)

            @block.scalar
            def _(act):
                act.wait_ge(bias_new, 1)
                for b in range(DB):
                    nc.scalar.activation(probs_new[:, b, :], scores_new[:, b, :], ACT.Exp, bias=neg_new[:, b:b + 1],
                                         scale=SCALE, accum_out=sums_new[:, b:b + 1]).then_inc(e_new, 1)

                def keep_k(n, u):
                    waited(act, s_done, n - 1)
                    for h in (0, 1):
                        act.wait_ge(kT_done[h], n + 1)
                        nc.scalar.activation(kTs[:, u % 2, h, :], ps_k[:, h, :], ACT.Copy).then_inc(kT_kept[h], 1)

                def exps(n, u):
                    waited(act, pT_done, n - 1)
                    act.wait_ge(bias_done, n + 1)
                    act.sem_inc(held_act, 1)
                    nc.scalar.activation(probs[:, u % 2, :], ps_s[:, u % 2, :], ACT.Exp, bias=neg_max[:, ds(n, 1)],
                                         scale=SCALE, accum_out=sums[:, ds(n, 1)]).then_inc(e_done, 1)

                def keep_o(n):
                    b, g = n // STEPS, n % STEPS
                    act.wait_ge(seq_done, b + 1)
                    act.wait_ge(pv_done, n + 1)
                    act.sem_inc(held_act, 1)
                    nc.scalar.activation(o_steps[:, ds(b % 2, 1), ds(g, 1), :].rearrange("p a g e -> p (a g e)"),
                                         ps_o[:, 0:DV], ACT.Copy).then_inc(o_kept, 1)

                def step(n, u, round_):
                    if not is_last(n):
                        keep_k(n + 1, u + 1)
                    exps(n, u)
                    if not is_first(n):
                        keep_o(n - 1)

                def finish(b):
                    act.wait_ge(gap_ready, b + 1)
                    nc.scalar.activation(wt[:], gap[:], ACT.Exp).then_inc(w_ready, 1)
                keep_k(0, 0)
                every_step(act, nothing, step, finish, lambda: keep_o(ALL - 1))

            @block.vector
            def _(dve):
                v = nc.vector
                dve.sem_inc(seq_done, 1)
                dve.sem_inc(seq_done, 1)
                chain = Chain(dve, own)
                chain.link(v.memset(q_all[:], 0.0))
                for m in range(2):
                    rows = slice(DK * m, DK * (m + 1))
                    v.tensor_copy(q_all[rows, :, :, DQ * m:DQ * (m + 1)].rearrange("p b h q -> p h b q"),
                                  qT_new[rows].rearrange("p h (b q) -> p h b q", b=DB)).then_inc(q_made, 1)
                dve.wait_ge(params_in, 32)
                chain.link(v.tensor_tensor(coef[:, 2:3], coef[:, 1:2], mem["lam"][:, 0:1], ALU.mult))
                chain.link(v.tensor_tensor(coef[:, 3:4], coef[:, 2:3], coef[:, 0:1], ALU.add))
                dve.wait_ge(new_done, 1)
                chain.link(v.tensor_tensor(scores_new, ps_s[:, 0, :].rearrange("p (b s) -> p b s", b=DB), mask_new[:], ALU.add))
                chain.link(v.tensor_reduce(mx_new[:], scores_new, AX.X, ALU.max))
                v.tensor_scalar(neg_new[:], mx_new[:], -SCALE, None, ALU.mult).then_inc(bias_new, 1)
                dve.wait_ge(pT_new_done, 1)
                v.tensor_copy(pT_new, ps_pT_new[0:ST]).then_inc(pT_new_kept, 1)
                dve.wait_ge(pv_new, 1)
                v.tensor_copy(o_new[:], ps_o_new).then_inc(o_new_kept, 1)
                dve.wait_ge(bias_new, 1)
                dve.wait_ge(o_new_kept, 1)
                dve.wait_ge(q_made, 2)
                own_start = chain.n
                LINKS = 10

                def start(b):
                    waited(dve, s_done, b * STEPS)
                    dve.sem_inc(held_dve, 1)
                    v.tensor_copy(q_cur[:], q_all[:, ds(b, 1)].rearrange("p o h c -> p (o h) c")).then_inc(q_ready, 1)

                def keep_k(n, u):
                    waited(dve, s_done, n - 1)
                    for h in (2, 3):
                        dve.wait_ge(kT_done[h], n + 1)
                        v.tensor_copy(kTs[:, u % 2, h, :], ps_k[:, h, :]).then_inc(kT_kept[h], 1)

                def keep_p(n, u):
                    waited(dve, pv_done, n - 1)
                    dve.wait_ge(pT_done, n + 1)
                    v.tensor_copy(pT[:, u % 2], ps_p[:]).then_inc(pT_kept, 1)

                def maximum(n, u):
                    waited(dve, bias_done, n - 1)
                    dve.wait_ge(s_done, n + 1)
                    v.tensor_reduce(mx[:, u % 2:u % 2 + 1], ps_s[:, u % 2, :], AX.X, ALU.max).then_inc(mx_done, 1)
                    dve.wait_ge(mx_done, n + 1)
                    dve.sem_inc(held_dve, 1)
                    v.tensor_scalar(neg_max[:, ds(n, 1)], mx[:, u % 2:u % 2 + 1], -SCALE, None, ALU.mult).then_inc(bias_done, 1)

                def step(n, u, round_):
                    if not is_last(n):
                        keep_k(n + 1, u + 1)
                    if not is_first(n):
                        keep_p(n - 1, u - 1)
                    maximum(n, u)

                def finish(b):
                    c = Chain(dve, own, own_start + LINKS * b)
                    mine = ds(b * STEPS, STEPS)
                    waited(dve, bias_done, (b + 1) * STEPS)
                    dve.wait_ge(seq_done, b + 2)
                    dve.sem_inc(held_dve, 1)
                    c.link(v.tensor_reduce(top[:, 0:1], neg_max[:, mine], AX.X, ALU.min))
                    dve.sem_inc(held_dve, 1)
                    c.link(v.tensor_tensor(top[:, 1:2], top[:, 0:1], neg_new[:, ds(b, 1)], ALU.min))
                    dve.sem_inc(held_dve, 1)
                    c.step(v.tensor_tensor(gap[:, 0:STEPS], top[:, 1:2].to_broadcast([P, STEPS]), neg_max[:, mine], ALU.subtract))
                    c.wait()
                    dve.sem_inc(held_dve, 1)
                    v.tensor_tensor(gap[:, STEPS:], top[:, 1:2], neg_new[:, ds(b, 1)], ALU.subtract).then_inc(gap_ready, 1)
                    dve.wait_ge(w_ready, b + 1)
                    dve.wait_ge(e_done, (b + 1) * STEPS)
                    dve.sem_inc(held_dve, 1)
                    c.step(v.tensor_tensor(lw[:, 0:STEPS], wt[:, 0:STEPS], sums[:, mine], ALU.mult))
                    c.link(v.tensor_tensor(lw[:, STEPS:], wt[:, STEPS:], sums_new[:, ds(b, 1)], ALU.mult))
                    c.link(v.tensor_reduce(top[:, 2:3], lw[:], AX.X, ALU.add))
                    c.link(v.reciprocal(top[:, 3:4], top[:, 2:3]))
                    c.link(v.tensor_scalar(lw[:], wt[:], top[:, 3:4], coef[:, 3:4], ALU.mult, ALU.mult))
                    dve.wait_ge(o_kept, (b + 1) * STEPS)
                    dve.sem_inc(held_dve, 1)
                    c.link(v.tensor_tensor(weighted[:], o_steps[:, ds(b % 2, 1)].rearrange("p o g e -> p (o g) e"),
                                           lw[:, 0:STEPS].unsqueeze(2).to_broadcast([P, STEPS, DV]), ALU.mult))
                    c.link(v.tensor_reduce(o_sum[:], weighted[:].rearrange("p g e -> p e g"), AX.X, ALU.add))
                    dve.sem_inc(held_dve, 1)
                    v.scalar_tensor_tensor(out=o_all[:, ds(b, 1), :].rearrange("p o e -> p (o e)"),
                                           in0=o_new[:, ds(b, 1), :].rearrange("p o e -> p (o e)"), scalar=lw[:, STEPS:],
                                           in1=o_sum[:], op0=ALU.mult, op1=ALU.add).then_inc(seq_done, 1)
                    assert c.n == LINKS
                keep_k(0, 0)
                every_step(dve, start, step, finish, lambda: keep_p(ALL - 1, RING - 1))
                dve.wait_ge(picked, 1)
                v.tensor_copy(mem["o_new"][:], ps_s[0:ST, 0, :]).then_inc(own, 1)


def prompt(nc, io, dram, mem):
    with ExitStack() as ctx:
        def sb(name, shape, dt=F32):
            return ctx.enter_context(nc.sbuf_tensor(name, shape, dt))

        def sem(name):
            return ctx.enter_context(nc.semaphore(name))

        CW = 512
        NG = NT // 4
        SR = 4
        NR = NEG_G + NE
        PARAMS, WEIGHTS = 3, 8
        ident, eps = mem["ident"], mem["eps"]
        kT, V = mem["kT"], mem["V"]
        w_out = sb("w_out_sb", [P, KD, D])
        w_r = sb("w_router", [P, KD, NR])
        b_r = sb("b_router", [P, NR])
        gate1 = sb("gate1", [P, D])
        gain2 = sb("gain2", [P, D])
        shift2 = sb("shift2", [P, D])
        g_attn = sb("g_attn_b", [P, AW])
        masks = sb("mask_p", [P, 4, CW])
        mask = sb("mask_tile", [P, CW])
        q_in = sb("q_tile", [P, H, P])
        qz = sb("q_zero_padded", [P, H, 2, P])
        probs = sb("p_probs", [P, 2, 2, NG * CW])
        nm = sb("neg_chunk_max", [P, 2, 2, NG])
        ls = sb("chunk_sums", [P, 2, 2, NG])
        mx = sb("chunk_max", [P, 2, NG])
        dd = sb("max_gap", [P, 2, NG])
        wt = sb("chunk_weights", [P, 2, NG])
        rr = sb("row_weights", [P, 2, NG])
        s2 = sb("small2", [P, 8])
        coef = sb("map_coef", [P, 2])
        aT = sb("aT", [P, 2, 4, P])
        o = sb("o_tile", [P, AW])
        osq = sb("o_sq", [P, AW])
        oa = sb("oa", [P, AW])
        oaT = sb("oaT", [P, H, P])
        obT = sb("obT_in", [P, GB, P])
        x = sb("x_res", [P, D])
        x2 = sb("x2_tile", [P, D])
        h2 = sb("h2_tile", [P, D])
        h2T = sb("h2T", [P, KD, P])
        st = sb("p_stats", [P, 24])
        zeros = sb("zero_rows", [P, D])
        ZB = (NB + 2 - SURE_BLOCKS) // NT
        assert ZB * NT + SURE_BLOCKS == NB + 2
        ps_s = ctx.enter_context(nc.psum_tensor("p_scores", [P, SR, CW], F32))
        ps_t = ctx.enter_context(nc.psum_tensor("p_aT", [P, 4, P], F32))
        ps_o = ctx.enter_context(nc.psum_tensor("p_o", [P, AW], F32))
        ps_w = ctx.enter_context(nc.psum_tensor("p_w", [P, 2, 512], F32))

        par_in = sem("p_params_in")
        weights_in = sem("p_weights_in")
        mod_in = sem("p_mod_in")
        q_loaded = sem("q_loaded")
        x_loaded = sem("x_loaded")
        ob_loaded = sem("ob_loaded")
        x2_out = sem("x2_out")
        h2_out = sem("h2_out")
        held_sp, held_act, held_dve, held_pool = (sem(f"p_held_{e}") for e in ("sp", "act", "dve", "pool"))
        mask_ready = sem("mask_ready")
        qz_ready = sem("qz_ready")
        s_done = sem("p_s_done")
        bias_done = sem("p_bias_done")
        e_done = sem("p_e_done")
        gap_ready = sem("gap_ready")
        w_ready = sem("w_ready")
        a_done = sem("a_done")
        t_done = sem("t_done")
        head_turned = sem("head_turned")
        aT_kept = sem("aT_kept")
        pv_done = sem("p_pv_done")
        o_kept = sem("p_o_kept")
        o_ss = sem("o_ss")
        o_std = sem("o_std")
        oa_ready = sem("oa_ready")
        oaT_done = sem("oaT_done")
        oaT_kept = sem("oaT_kept")
        w_done = sem("w_done")
        x2_ready = sem("x2_ready")
        x2_ss = sem("x2_ss")
        x2_std = sem("x2_std")
        h2_ready = sem("h2_ready")
        h2T_done = sem("h2T_done")
        h2T_kept = sem("h2T_kept")
        r_done = sem("r_done")
        lg_ready = sem("lg_ready")
        own = sem("p_dve_own")
        zeroed = sem("qz_zeroed")
        cleared = sem("rows_cleared")

        def c_slot(J, h, c):
            return (h * (J + 1) + c) % 2

        def bank_of(J, h, c):
            return (2 * c + 2 * h * (J + 1)) % SR

        def chunks(ahead):
            return ahead[0] + 1 if ahead else 0

        def chunk_at(J, r, h):
            return sum(4 * H * (j + 1) for j in range(J)) + (r * H + h) * (J + 1)

        def tiles(eng, body):
            body(0, 0, (0, 1))
            for J in range(NG):
                with eng.Fori(1 if J == 0 else 0, 3) as r:
                    body(J, r, (J, r + 1))
                body(J, 3, (J + 1, 0) if J < NG - 1 else None)

        def slots(J, r, following):
            for h in range(H):
                ahead = (J, r, h + 1) if h < H - 1 else (*following, 0) if following else None
                yield ahead, (J, r, h), h

        with nc.Block() as block:
            @block.sync
            def _(sp):
                sp.dma_start(q_in[:], dram["qT"][0]).then_inc(q_loaded, 16)
                for dst, src in ((masks, io["c_mask_p"]), (coef, io["c_coef_p"]),
                                 (g_attn, io["g_attn"].rearrange("o h e -> o (h e)").broadcast_to([P, AW]))):
                    sp.dma_start(dst[:], src).then_inc(par_in, 16)
                for dst, src in ((w_out[:], io["w_out"][0].rearrange("(k p) n -> p k n", p=P)),
                                 (gate1[0:ST, :], sample_mod(dram, MOD_GATE1)),
                                 (gain2[0:ST, :], sample_mod(dram, MOD_GAIN2)),
                                 (shift2[0:ST, :], sample_mod(dram, MOD_SHIFT2)),
                                 (b_r[:, 0:NEG_G], io["b_router_g"].broadcast_to([P, NEG_G])),
                                 (b_r[:, NEG_G:], io["b_router_e"].broadcast_to([P, NE]))):
                    sp.dma_start(dst, src).then_inc(weights_in, 16)
                with nc.allow_non_contiguous_dma(reason="router weights, 16 and 128 bytes a row"):
                    sp.dma_start(w_r[:, :, 0:NEG_G], io["w_router_g"][0].rearrange("(k p) n -> p k n", p=P)).then_inc(weights_in, 16)
                    sp.dma_start(w_r[:, :, NEG_G:], io["w_router_e"][0].rearrange("(k p) n -> p k n", p=P)).then_inc(weights_in, 16)
                sp.dma_start(x[0:ST, :], io["x_sample"].rearrange("b q d -> (b q) d")).then_inc(x_loaded, 16)

                def body(J, r, following):
                    i = 4 * J + r
                    sp.wait_ge(s_done, 2 * (chunk_at(J, r, 0) + J + 1))
                    sp.sem_inc(held_sp, 1)
                    sp.dma_start(dram["y"][ds((SURE_BLOCKS + ZB * i) * P, ZB * P), :].rearrange("(b p) d -> p b d", p=P),
                                 zeros[:].unsqueeze(1).to_broadcast([P, ZB, D])).then_inc(cleared, 16)
                    if following:
                        sp.wait_ge(qz_ready, 8 * (i + 1))
                        sp.sem_inc(held_sp, 1)
                        sp.dma_start(q_in[:], dram["qT"][ds(i + 1, 1)]).then_inc(q_loaded, 16)
                    residual(i, True)

                def residual(k, more):
                    first = isinstance(k, int) and k == 0
                    if more:
                        sp.wait_ge(w_done, k + 1)
                        sp.sem_inc(held_sp, 1)
                        sp.dma_start(obT[:], dram["obT"][ds(k, 1)]).then_inc(ob_loaded, 16)
                    sp.wait_ge(x2_ready, k + 1)
                    sp.sem_inc(held_sp, 1)
                    if first:
                        sp.dma_start(dram["x2"][SEQ:NTOK, :], x2[0:ST, :]).then_inc(x2_out, 16)
                    else:
                        sp.dma_start(dram["x2"][ds((k - 1) * P, P), :], x2[:]).then_inc(x2_out, 16)
                    if more:
                        sp.dma_start(x[:], io["x_prompt"][0, ds(k * P, P), :]).then_inc(x_loaded, 16)
                    sp.wait_ge(h2_ready, k + 1)
                    sp.sem_inc(held_sp, 1)
                    if first:
                        sp.dma_start(dram["h2"][SEQ:NTOK, :], h2[0:ST, :]).then_inc(h2_out, 16)
                        for dst, part in ((gate1, MOD_GATE1), (gain2, MOD_GAIN2), (shift2, MOD_SHIFT2)):
                            sp.dma_start(dst[:], prompt_mod(dram, part)).then_inc(mod_in, 16)
                    else:
                        sp.dma_start(dram["h2"][ds((k - 1) * P, P), :], h2[:]).then_inc(h2_out, 16)
                sp.wait_ge(zeroed, 2)
                tiles(sp, body)
                residual(NT, False)
                sp.wait_ge(cleared, 16 * NT)
                sp.wait_ge(x2_out, 16 * (NT + 1))
                sp.wait_ge(h2_out, 16 * (NT + 1))

            @block.gpsimd
            def _(pool):
                nc.gpsimd.memset(qz[:], 0.0).then_inc(zeroed, 1)
                nc.gpsimd.memset(zeros[:], 0.0).then_inc(zeroed, 1)
                pool.wait_ge(zeroed, 2)

                def pad(J, r, h):
                    i = 4 * J + r
                    if h == 0:
                        pool.wait_ge(q_loaded, 16 * (i + 1))
                        waited(pool, mask_ready, i)
                    waited(pool, s_done, 2 * chunk_before(J, r, h))
                    pool.sem_inc(held_pool, 1)
                    for m in range(2):
                        if m or h:
                            pool.wait_ge(qz_ready, 8 * i + 2 * h + m)
                            pool.sem_inc(held_pool, 1)
                        rows = slice(DK * m, DK * (m + 1))
                        nc.gpsimd.tensor_copy(qz[rows, h, m, :], q_in[rows, h, :]).then_inc(qz_ready, 1)

                def chunk_before(J, r, h):
                    if isinstance(r, int) and r == 0:
                        return chunk_at(J - 1, 3, h) + J if J else 0
                    return chunk_at(J, r - 1, h + 1)

                def place_mask(J, r):
                    pool.wait_ge(qz_ready, 8 * (4 * J + r + 1))
                    if not (isinstance(r, int) and J == r == 0):
                        pool.wait_ge(bias_done, chunk_before(J, r, H - 1))
                        pool.sem_inc(held_pool, 1)
                    nc.gpsimd.tensor_copy(mask[:], masks[:, ds(r, 1), :].rearrange("p o k -> p (o k)")).then_inc(mask_ready, 1)

                def body(J, r, following):
                    if following:
                        for h in range(H):
                            pad(*following, h)
                        place_mask(*following)
                for h in range(H):
                    pad(0, 0, h)
                pool.wait_ge(par_in, 16 * PARAMS)
                place_mask(0, 0)
                tiles(pool, body)

            @block.tensor
            def _(pe):
                for s, credit in ((t_done, 1), (head_turned, 2), (pv_done, 2)):
                    for _ in range(credit):
                        pe.sem_inc(s, 1)

                def score(J, r, h, c):
                    n = 2 * (chunk_at(J, r, h) + c)
                    if c == 0:
                        pe.wait_ge(qz_ready, 8 * (4 * J + r) + 2 * h + 2)
                    for m in range(2):
                        pe.wait_ge(e_done, n + m + 1)
                        pe.matmul(ps_s[:, bank_of(J, h, c) + m, :], qz[:, h, m, :], kT[:, h, c * CW:(c + 1) * CW],
                                  start=True, stop=True).then_inc(s_done, 1)

                def turn(J, r, h, c):
                    n = chunk_at(J, r, h) + c
                    pe.wait_ge(a_done, n + 1)
                    pe.wait_ge(aT_kept, n + 2)
                    for j in range(4):
                        last = pe.transpose(ps_t[:, j, :], probs[:, h % 2, 0, c * CW + j * P:c * CW + (j + 1) * P], ident[:])
                    last.then_inc(t_done, 1)

                def times_v(J, r, h, c):
                    n = chunk_at(J, r, h) + c
                    pe.wait_ge(aT_kept, n + 3)
                    if h == 0 and c == 0:
                        pe.wait_ge(o_kept, 4 * J + r + 1)
                    for j in range(4):
                        if c == J and j == 1:
                            last.then_inc(head_turned, 1)
                        last = pe.matmul(ps_o[:, h * DV:(h + 1) * DV], aT[:, c_slot(J, h, c), j, :],
                                         V[:, 4 * c + j, h * DV:(h + 1) * DV], start=(c == 0 and j == 0),
                                         stop=(c == J and j == 3))
                    last.then_inc(pv_done, 1)

                def oa_turn(k, R):
                    pe.wait_ge(oa_ready, k + 1)
                    waited(pe, lg_ready, k)
                    for h in range(H):
                        last = pe.transpose(ps_w[:, 0, h * P:h * P + R], oa[0:R, h * P:(h + 1) * P], ident[0:R, 0:R])
                    last.then_inc(oaT_done, 1)

                def project(k, R, ob_src, half):
                    if half == 0:
                        if isinstance(k, int) and k == 0:
                            pe.wait_ge(weights_in, 16 * WEIGHTS)
                        pe.wait_ge(oaT_kept, k + 1)
                        waited(pe, ob_loaded, 16 * k)
                    for kk in range(KD):
                        lhs = oaT[:, kk, 0:R] if kk < H else ob_src[:, kk - H, 0:R]
                        last = pe.matmul(ps_w[0:R, half, :], lhs, w_out[:, kk, half * 512:(half + 1) * 512],
                                         start=(kk == 0), stop=(kk == KD - 1))
                    if half == 1:
                        last.then_inc(w_done, 1)

                def h2_turn(k, R):
                    pe.wait_ge(h2_ready, k + 1)
                    for b in range(KD):
                        last = pe.transpose(ps_w[:, b // 4, (b % 4) * P:(b % 4) * P + R], h2[0:R, b * P:(b + 1) * P],
                                            ident[0:R, 0:R])
                    last.then_inc(h2T_done, 1)

                def route(k, R):
                    pe.wait_ge(h2T_kept, k + 1)
                    for b in range(KD):
                        last = pe.matmul(ps_w[0:R, 0, 0:NR], h2T[:, b, 0:R], w_r[:, b, :], start=(b == 0), stop=(b == KD - 1))
                    last.then_inc(r_done, 1)

                def body(J, r, following):
                    k = 4 * J + r
                    R = ST if isinstance(k, int) and k == 0 else P
                    for ahead, now, h in slots(J, r, following):
                        scored, turned = chunks(ahead), J + 1
                        for c in range(min(2, scored)):
                            score(*ahead, c)
                        if h in (1, 2):
                            project(k, R, mem["obT_new"] if R == ST else obT, h - 1)
                        for c in range(max(scored, turned + 1)):
                            if c < turned:
                                turn(*now, c)
                            if c == J and h == 3:
                                h2_turn(k, R)
                            if 1 <= c <= turned:
                                times_v(*now, c - 1)
                            if c + 2 < scored:
                                score(*ahead, c + 2)
                        if h == 0:
                            oa_turn(k, R)
                        if h == 3:
                            route(k, R)

                score(0, 0, 0, 0)
                tiles(pe, body)
                oa_turn(NT, P)
                for half in range(2):
                    project(NT, P, obT, half)
                h2_turn(NT, P)
                route(NT, P)

            @block.scalar
            def _(act):
                for _ in range(SR):
                    act.sem_inc(e_done, 1)
                for s, credit in ((aT_kept, 2), (o_kept, 1)):
                    for _ in range(credit):
                        act.sem_inc(s, 1)

                def exps(J, r, h, c):
                    n = chunk_at(J, r, h) + c
                    act.wait_ge(bias_done, n + 1)
                    if c == 0:
                        act.wait_ge(head_turned, 4 * (4 * J + r) + h + 1)
                    for m in range(2):
                        dst = probs[:, h % 2, m, c * CW:(c + 1) * CW]
                        nc.scalar.activation(dst, dst if c == J else ps_s[:, bank_of(J, h, c) + m, :], ACT.Exp,
                                             bias=nm[:, h % 2, m, c:c + 1], scale=SCALE,
                                             accum_out=ls[:, h % 2, m, c:c + 1]).then_inc(e_done, 1)

                def weights(J, r, h):
                    act.wait_ge(gap_ready, 4 * (4 * J + r) + h + 1)
                    nc.scalar.activation(wt[:, :, 0:J + 1], dd[:, :, 0:J + 1], ACT.Exp).then_inc(w_ready, 1)

                def keep_aT(J, r, h, c):
                    n = chunk_at(J, r, h) + c
                    act.wait_ge(pv_done, n + 1)
                    act.wait_ge(t_done, n + 2)
                    nc.scalar.activation(aT[:, c_slot(J, h, c)], ps_t[:], ACT.Copy).then_inc(aT_kept, 1)

                def root(done, ready, k, R, s, cnt, width):
                    act.wait_ge(done, k + 1)
                    nc.scalar.activation(st[0:R, s + 4:s + 4 + cnt], st[0:R, s:s + cnt], ACT.Sqrt, bias=eps[0:R, 0:1],
                                         scale=1.0 / width).then_inc(ready, 1)

                def keep_o(J, r):
                    act.wait_ge(pv_done, chunk_at(J, r, 3) + J + 1 + 2)
                    nc.scalar.activation(o[:], ps_o[:], ACT.Copy).then_inc(o_kept, 1)

                def keep_oaT(k, R):
                    act.wait_ge(oaT_done, k + 1)
                    nc.scalar.activation(oaT[:, :, 0:R], ps_w[:, 0, :].rearrange("p (h t) -> p h t", h=H)[:, :, 0:R],
                                         ACT.Copy).then_inc(oaT_kept, 1)

                def keep_h2T(k, R):
                    act.wait_ge(h2T_done, k + 1)
                    nc.scalar.activation(h2T[:, :, 0:R],
                                         ps_w[:].rearrange("p a (b t) -> p (a b) t", t=P)[:, :, 0:R], ACT.Copy)\
                        .then_inc(h2T_kept, 1)

                def body(J, r, following):
                    k = 4 * J + r
                    R = ST if isinstance(k, int) and k == 0 else P
                    for ahead, now, h in slots(J, r, following):
                        scored, turned = chunks(ahead), J + 1
                        if scored < 2:
                            keep_aT(*now, 0)
                        for c in range(max(scored, turned)):
                            if c < scored:
                                exps(*ahead, c)
                            if c == scored - 1:
                                weights(*ahead)
                            if c < turned and (c or scored >= 2):
                                keep_aT(*now, c)
                            if c == 0 and h == 0:
                                root(o_ss, o_std, k, R, 0, H, DV)
                        if h == 0:
                            keep_oaT(k, R)
                        if h == 2:
                            root(x2_ss, x2_std, k, R, 8, 1, D)
                        if h == 3:
                            keep_h2T(k, R)
                    keep_o(J, r)

                exps(0, 0, 0, 0)
                weights(0, 0, 0)
                tiles(act, body)
                root(o_ss, o_std, NT, P, 0, H, DV)
                keep_oaT(NT, P)
                root(x2_ss, x2_std, NT, P, 8, 1, D)
                keep_h2T(NT, P)

            @block.vector
            def _(dve):
                v = nc.vector

                def own_count(J):
                    return (J + 2) + 6 + (J + 1)
                BACK = 6

                def scores(J, r, h, chain, between=()):
                    between = list(between)

                    def other():
                        part = between.pop(0) if between else None
                        if part:
                            part()
                    i4 = 4 * (4 * J + r) + h
                    dve.wait_ge(head_turned, i4 + 1)
                    par = h % 2
                    for c in range(J + 1):
                        bank = bank_of(J, h, c)
                        dve.wait_ge(s_done, 2 * (chunk_at(J, r, h) + c + 1))
                        if c == J:
                            if h == 0:
                                dve.wait_ge(mask_ready, 4 * J + r + 1)
                            dve.sem_inc(held_dve, 1)
                            for m in range(2):
                                chain.step(v.tensor_tensor_reduce(
                                    out=probs[:, par, m, c * CW:(c + 1) * CW], in0=ps_s[:, bank + m, :],
                                    in1=mask[:], scale=1.0, scalar=-3.0e38, op0=ALU.add, op1=ALU.max, accum_out=mx[:, m, c:c + 1]))
                            chain.wait()
                        else:
                            chain.link(v.tensor_reduce(mx[:, :, c], ps_s[:, bank:bank + 2, :], AX.X, ALU.max))
                        v.tensor_scalar(nm[:, par, :, c], mx[:, :, c], -SCALE, None, ALU.mult).then_inc(bias_done, 1)
                        if c < J:
                            other()
                    ch = slice(0, J + 1)
                    dve.wait_ge(bias_done, chunk_at(J, r, h) + J + 1)
                    chain.link(v.tensor_reduce(s2[:, 0:2], nm[:, par, :, ch], AX.X, ALU.min))
                    v.tensor_tensor(dd[:, :, ch], s2[:, 0:2].unsqueeze(2).to_broadcast([P, 2, J + 1]), nm[:, par, :, ch],
                                    ALU.subtract).then_inc(gap_ready, 1)
                    other()
                    dve.wait_ge(w_ready, i4 + 1)
                    dve.wait_ge(e_done, 2 * (chunk_at(J, r, h) + J + 1) + SR)
                    chain.link(v.tensor_tensor(rr[:, :, ch], wt[:, :, ch], ls[:, par, :, ch], ALU.mult))
                    chain.link(v.tensor_reduce(s2[:, 2:4], rr[:, :, ch], AX.X, ALU.add))
                    chain.link(v.reciprocal(s2[:, 4:6], s2[:, 2:4]))
                    chain.link(v.tensor_tensor(s2[:, 6:8], s2[:, 4:6], coef[:], ALU.mult))
                    chain.link(v.tensor_tensor(rr[:, :, ch], wt[:, :, ch], s2[:, 6:8].unsqueeze(2).to_broadcast([P, 2, J + 1]),
                                               ALU.mult))
                    def scale_second(c):
                        p1 = probs[:, par, 1, c * CW:(c + 1) * CW]
                        chain.step(v.tensor_scalar(p1, p1, rr[:, 1, c:c + 1], None, ALU.mult))
                    scale_second(0)
                    for c in range(J + 1):
                        scaled = chain.base + chain.n
                        if c < J:
                            scale_second(c + 1)
                        dve.wait_ge(own, scaled)
                        p0, p1 = (probs[:, par, m, c * CW:(c + 1) * CW] for m in range(2))
                        v.scalar_tensor_tensor(out=p0, in0=p0, scalar=rr[:, 0, c:c + 1], in1=p1, op0=ALU.mult, op1=ALU.add)\
                            .then_inc(a_done, 1)
                    while between:
                        other()

                def norm_o(k, R, src, chain):
                    g3 = "p (g c) -> p g c"

                    def squares():
                        if R == P:
                            dve.wait_ge(o_kept, k + 1)
                        chain.link(v.tensor_tensor(osq[0:R, :], src[0:R, :], src[0:R, :], ALU.mult))
                        v.tensor_reduce(st[0:R, 0:H], osq[0:R, :].rearrange(g3, g=H), AX.X, ALU.add).then_inc(o_ss, 1)

                    def scale():
                        dve.wait_ge(o_std, k + 1)
                        chain.link(v.reciprocal(st[0:R, 16:16 + H], st[0:R, 4:4 + H]))
                        chain.link(v.tensor_tensor(osq[0:R, :].rearrange(g3, g=H), src[0:R, :].rearrange(g3, g=H),
                                                   st[0:R, 16:16 + H].unsqueeze(2).to_broadcast([R, H, DV]), ALU.mult))
                        waited(dve, oaT_done, k)
                        v.tensor_tensor(oa[0:R, :], osq[0:R, :], g_attn[0:R, :], ALU.mult).then_inc(oa_ready, 1)
                    return squares, scale

                def residual(k, R, chain):
                    def gated():
                        if isinstance(k, int) and k == 0:
                            dve.wait_ge(weights_in, 16 * WEIGHTS)
                        dve.wait_ge(w_done, k + 1)
                        if R == P:
                            dve.wait_ge(mod_in, 48)
                        waited(dve, x2_out, 16 * k)
                        chain.link(v.tensor_tensor(x2[0:R, :], ps_w[0:R].rearrange("p a n -> p (a n)"), gate1[0:R, :], ALU.mult))

                    def add_and_square():
                        dve.wait_ge(x_loaded, 16 * (k + 1))
                        v.tensor_tensor(x2[0:R, :], x2[0:R, :], x[0:R, :], ALU.add).then_inc(x2_ready, 1)
                        dve.wait_ge(x2_ready, k + 1)
                        waited(dve, h2_out, 16 * k)
                        v.tensor_tensor_reduce(out=h2[0:R, :], in0=x2[0:R, :], in1=x2[0:R, :], scale=1.0, scalar=0.0,
                                               op0=ALU.mult, op1=ALU.add, accum_out=st[0:R, 8:9]).then_inc(x2_ss, 1)
                    return gated, add_and_square

                def modulate(k, R, chain):
                    def scale():
                        dve.wait_ge(x2_std, k + 1)
                        chain.link(v.reciprocal(st[0:R, 20:21], st[0:R, 12:13]))
                        chain.link(v.scalar_tensor_tensor(out=h2[0:R, :], in0=x2[0:R, :], scalar=st[0:R, 20:21],
                                                          in1=gain2[0:R, :], op0=ALU.mult, op1=ALU.mult))

                    def shift():
                        v.tensor_tensor(h2[0:R, :], h2[0:R, :], shift2[0:R, :], ALU.add).then_inc(h2_ready, 1)
                    return scale, shift

                def logits(k, R):
                    dve.wait_ge(r_done, k + 1)
                    dve.sem_inc(held_dve, 1)
                    v.tensor_tensor(mem["lg"][0:R, ds(k, 1), :], ps_w[0:R, 0:1, 0:NR], b_r[0:R, :].unsqueeze(1), ALU.add)\
                        .then_inc(lg_ready, 1)

                start = 1 + 2 + own_count(0)
                per = {J: 4 * own_count(J) + BACK for J in range(NG)}

                def base(J, r):
                    return start + sum(4 * per[j] + own_count(j + 1) - own_count(j) for j in range(J)) + r * per[J]

                def body(J, r, following):
                    k = 4 * J + r
                    R = ST if isinstance(k, int) and k == 0 else P
                    chain = Chain(dve, own, base(J, r))
                    for ahead, now, h in slots(J, r, following):
                        between = {0: norm_o(k, R, mem["o_new"] if R == ST else o, chain), 1: (),
                                   2: (None, *residual(k, R, chain)), 3: modulate(k, R, chain)}[h]
                        if ahead:
                            scores(*ahead, chain, between)
                        else:
                            for part in between:
                                part()
                    logits(k, R)
                    assert chain.n == 3 * own_count(J) + BACK + (own_count(following[0]) if following else 0)

                chain = Chain(dve, own)
                dve.wait_ge(par_in, 16 * PARAMS)
                chain.step(v.tensor_scalar(g_attn[:], g_attn[:], 1.0 - LAM_INIT, None, ALU.mult))
                chain.step(v.tensor_tensor(coef[:, 1:2], coef[:, 1:2], mem["lam"][:, 0:1], ALU.mult))
                chain.link(v.memset(mem["lg"][ST:P, 0, :], 0.0))
                scores(0, 0, 0, chain)
                assert chain.n == start
                tiles(dve, body)
                chain = Chain(dve, own, base(NG - 1, 3) + 3 * own_count(NG - 1) + BACK)
                for part in (*norm_o(NT, P, o, chain), *residual(NT, P, chain), *modulate(NT, P, chain)):
                    part()
                logits(NT, P)


def routing(nc, io, mem, r):
    with ExitStack() as ctx:
        def sb(name, shape, dt=F32):
            return ctx.enter_context(nc.sbuf_tensor(name, shape, dt))

        def sem(name):
            return ctx.enter_context(nc.semaphore(name))

        T = NT + 1
        BIG = 1e30
        MAXB = (NTOK + P - 1) // P
        lg = mem["lg"]
        before = sb("before", [P, P])
        ones = sb("ones", [P, P])
        iota = sb("iota", [P, P])
        first = sb("first", [P, NE, NE])
        tok = sb("tok", [P, T])
        m1 = sb("rt_m1", [P, T])
        g_sum = sb("rt_gsum", [P, T])
        gd = sb("rt_gd", [P, T, NEG_G])
        cand_g = sb("rt_cand_g", [P, T, NEG_G])
        oh_g = sb("rt_oh_g", [P, T, NEG_G])
        ng_g = sb("rt_ng_g", [P, T, NEG_G])
        el = sb("rt_el", [P, T, NE])
        cand = sb("rt_cand", [P, T, NE])
        oh = [sb("rt_oh1", [P, T, NE]), sb("rt_oh2", [P, T, NE])]
        both = sb("rt_both", [P, T, NE])
        top = [sb("rt_top1", [P, T]), sb("rt_top2", [P, T])]
        de = sb("rt_de", [P, T])
        rank = sb("rt_rank", [P, T, NE])
        cnt = sb("rt_cnt", [P, T, NE])
        off = sb("rt_off", [P, T + 1, NE])
        nb = sb("rt_nb", [P, NE])
        cmp_b = sb("rt_cmp_b", [P, NE, MAXB])
        cmp_f = sb("rt_cmp_f", [P, NE, NE])
        start = sb("rt_start", [P, NE])
        end = sb("rt_end", [P, NE])
        dest = [sb("rt_dest1", [P, T]), sb("rt_dest2", [P, T])]
        blk = sb("rt_blk", [P, 2, T])
        row = sb("rt_row", [P, 2, T])
        ge = sb("rt_ge", [P, 2, T, NB])
        oh_row = sb("rt_oh_row", [P, 2, T, P])
        oh_blk = sb("rt_oh_blk", [P, 2, T, NB])
        tok_all = sb("rt_tok", [P, T])
        be = sb("rt_be", [P, NB])
        turn = sb("rt_turn", [P, NB])
        fresh = sb("rt_fresh", [1, NB])
        live = sb("rt_live", [1, NB // 2])
        cmp_e = sb("rt_cmp_e", [P, NB, NE])
        ps = ctx.enter_context(nc.psum_tensor("rt_ps", [P, 4, 512], F32))
        ps_tok = ctx.enter_context(nc.psum_tensor("rt_ps_tok", [P, 512], F32))

        params_in = sem("rt_params_in")
        own = sem("rt_dve_own")
        g_ready = sem("rt_g_ready")
        g_exp = sem("rt_g_exp")
        de_ready = sem("rt_de_ready")
        de_exp = sem("rt_de_exp")
        chosen = sem("rt_chosen")
        counted = sem("rt_counted")
        pair_ready = sem("rt_pair_ready")
        pair_done = sem("rt_pair_done")
        E3 = "p t (g e) -> p t g e"

        with nc.Block() as block:
            @block.sync
            def _(sp):
                for dst, src in ((before, io["c_before"]), (iota, io["c_iota"]), (tok, io["c_tok"]),
                                 (first, io["c_first"].broadcast_to([P, NE * NE]).rearrange("p (a b) -> p a b", a=NE))):
                    sp.dma_start(dst[:], src).then_inc(params_in, 16)

            @block.scalar
            def _(act):
                act.wait_ge(g_ready, 1)
                nc.scalar.activation(gd[:], gd[:], ACT.Exp).then_inc(g_exp, 1)
                act.wait_ge(de_ready, 1)
                nc.scalar.activation(de[:], de[:], ACT.Exp).then_inc(de_exp, 1)

            @block.tensor
            def _(pe):
                pe.wait_ge(chosen, 1)
                pe.wait_ge(params_in, 64)
                flat = both[:].rearrange("p t e -> p (t e)")
                for n, w in enumerate((before, ones)):
                    pe.matmul(ps[:, 2 * n, 0:512], w[:], flat[:, 0:512], start=True, stop=True)
                    last = pe.matmul(ps[:, 2 * n + 1, 0:T * NE - 512], w[:], flat[:, 512:T * NE], start=True, stop=True)
                last.then_inc(counted, 1)
                for k in range(2):
                    pe.wait_ge(pair_ready, k + 1)
                    for t in range(T):
                        last = pe.matmul(ps_tok[:, 0:NB], oh_row[:, k, t, :], oh_blk[:, k, t, :], start=(k == t == 0),
                                         stop=(k == 1 and t == T - 1))
                last.then_inc(pair_done, 1)

            @block.vector
            def _(dve):
                v = nc.vector
                c = Chain(dve, own)

                def spread(x, n):
                    return x.unsqueeze(2).to_broadcast([P, T, n])

                def first_max(x, n, best, cand, onehot):
                    c.link(v.tensor_reduce(best, x, AX.X, ALU.max))
                    c.link(v.tensor_tensor(cand, x, spread(best, n), ALU.is_lt))
                    c.link(v.tensor_scalar(cand, cand, BIG, None, ALU.mult))
                    c.link(v.tensor_tensor(cand, cand, iota[:, 0:n].unsqueeze(1).to_broadcast([P, T, n]), ALU.add))
                    c.link(v.tensor_reduce(m1[:], cand, AX.X, ALU.min))
                    c.link(v.tensor_tensor(onehot, iota[:, 0:n].unsqueeze(1).to_broadcast([P, T, n]), spread(m1[:], n),
                                           ALU.is_equal))

                dve.wait_ge(params_in, 64)
                c.link(v.memset(ones[:], 1.0))
                lgg = lg[:, :, 0:NEG_G]
                first_max(lgg, NEG_G, g_sum[:], cand_g[:], oh_g[:])
                v.tensor_tensor(gd[:], lgg, spread(g_sum[:], NEG_G), ALU.subtract).then_inc(g_ready, 1)
                c.link(v.tensor_scalar(ng_g[:], oh_g[:], BIG, -BIG, ALU.mult, ALU.add))
                lge = lg[:, :, NEG_G:]
                for g in range(NEG_G):
                    c.step(v.tensor_tensor(el[:, :, g * EPG:(g + 1) * EPG], lge[:, :, g * EPG:(g + 1) * EPG],
                                           oh_g[:, :, g:g + 1].to_broadcast([P, T, EPG]), ALU.mult))
                c.wait()
                for g in range(NEG_G):
                    c.step(v.tensor_tensor(el[:, :, g * EPG:(g + 1) * EPG], el[:, :, g * EPG:(g + 1) * EPG],
                                           ng_g[:, :, g:g + 1].to_broadcast([P, T, EPG]), ALU.add))
                c.wait()
                first_max(el[:], NE, top[0][:], cand[:], oh[0][:])
                c.link(v.tensor_scalar(cand[:], oh[0][:], -3.0 * BIG, None, ALU.mult))
                c.link(v.tensor_tensor(el[:], el[:], cand[:], ALU.add))
                first_max(el[:], NE, top[1][:], cand[:], oh[1][:])
                v.tensor_tensor(de[:], top[1][:], top[0][:], ALU.subtract).then_inc(de_ready, 1)
                c.step(v.memset(oh[0][ST:P, 0, :], 0.0))
                c.link(v.memset(oh[1][ST:P, 0, :], 0.0))
                v.tensor_tensor(both[:], oh[0][:], oh[1][:], ALU.add).then_inc(chosen, 1)
                dve.wait_ge(g_exp, 1)
                c.link(v.tensor_reduce(g_sum[:], gd[:], AX.X, ALU.add))
                dve.wait_ge(de_exp, 1)
                c.link(v.tensor_scalar(m1[:], de[:], 1.0, None, ALU.add))
                c.link(v.tensor_tensor(m1[:], m1[:], g_sum[:], ALU.mult))
                c.link(v.reciprocal(r["gate"][:, 0, :], m1[:]))
                c.link(v.tensor_tensor(r["gate"][:, 1, :], r["gate"][:, 0, :], de[:], ALU.mult))
                dve.wait_ge(counted, 1)
                c.step(v.tensor_copy(rank[:].rearrange("p t e -> p (t e)"),
                                     ps[:, 0:2, :].rearrange("p a n -> p (a n)")[:, 0:T * NE]))
                c.step(v.tensor_copy(cnt[:].rearrange("p t e -> p (t e)"),
                                     ps[:, 2:4, :].rearrange("p a n -> p (a n)")[:, 0:T * NE]))
                c.link(v.memset(off[:, 0, :], 0.0))
                for t in range(T):
                    c.link(v.tensor_tensor(off[:, t + 1, :], off[:, t, :], cnt[:, t, :], ALU.add))
                c.link(v.tensor_scalar(nb[:], off[:, T, :], 1.0 / P, None, ALU.mult))
                c.link(v.tensor_tensor(cmp_b[:], nb[:].unsqueeze(2).to_broadcast([P, NE, MAXB]),
                                       iota[:, 0:MAXB].unsqueeze(1).to_broadcast([P, NE, MAXB]), ALU.is_gt))
                c.link(v.tensor_reduce(nb[:], cmp_b[:], AX.X, ALU.add))
                c.link(v.tensor_tensor(cmp_f[:], first[:], nb[:].unsqueeze(1).to_broadcast([P, NE, NE]), ALU.mult))
                c.link(v.tensor_reduce(start[:], cmp_f[:], AX.X, ALU.add))
                c.link(v.tensor_tensor(end[:], start[:], nb[:], ALU.add))
                c.link(v.tensor_tensor(cmp_e[:], iota[:, 0:NB].unsqueeze(2).to_broadcast([P, NB, NE]),
                                       end[:].unsqueeze(1).to_broadcast([P, NB, NE]), ALU.is_ge))
                c.link(v.tensor_scalar(m1[0:1, 0:1], end[0:1, NE - 1:NE], 0.0, None, ALU.add))
                c.link(v.tensor_tensor(live[:], iota[0:1, 0:NB:2], m1[0:1, 0:1].to_broadcast([1, NB // 2]), ALU.is_lt))
                c.link(v.tensor_reduce(m1[0:1, 0:1], live[:], AX.X, ALU.add))
                c.link(v.tensor_copy(r["pairs"][:], m1[0:1, 0:1]))
                c.step(v.tensor_reduce(be[:], cmp_e[:], AX.X, ALU.add))
                c.link(v.tensor_scalar(nb[:], nb[:], 0.0, None, ALU.is_gt))
                c.link(v.tensor_tensor(cmp_e[:], cmp_e[:], nb[:].unsqueeze(1).to_broadcast([P, NB, NE]), ALU.mult))
                c.link(v.tensor_reduce(turn[:], cmp_e[:], AX.X, ALU.add))
                c.step(v.memset(fresh[:, 0:1], 1.0))
                c.step(v.memset(r["turn"][:, NB:], 0))
                c.step(v.memset(r["fresh"][:, NB:], 0))
                c.step(v.tensor_copy(r["turn"][:, 0:NB], turn[0:1, :]))
                c.link(v.tensor_tensor(fresh[:, 1:NB], turn[0:1, 1:NB], turn[0:1, 0:NB - 1], ALU.is_gt))
                c.link(v.tensor_copy(r["fresh"][:, 0:NB], fresh[:]))
                c.link(v.tensor_scalar(be[:], be[:], float(NE - 1), None, ALU.min))
                c.step(v.memset(r["block_expert"][:, NB:], 0))
                c.link(v.tensor_copy(r["block_expert"][:, 0:NB], be[0:1, :]))
                c.link(v.tensor_scalar(start[:], start[:], float(P), None, ALU.mult))
                c.link(v.tensor_tensor(rank[:], rank[:], off[:, 0:T, :], ALU.add))
                c.link(v.tensor_tensor(rank[:], rank[:], start[:].unsqueeze(1).to_broadcast([P, T, NE]), ALU.add))
                for k in range(2):
                    c.link(v.tensor_tensor(cand[:], rank[:], oh[k][:], ALU.mult))
                    c.link(v.tensor_reduce(dest[k][:], cand[:], AX.X, ALU.add))
                    c.step(v.tensor_copy(r["dest"][:, k, :], dest[k][:]))
                    c.link(v.tensor_scalar(blk[:, k, :], dest[k][:], 1.0 / P, None, ALU.mult))
                    c.link(v.tensor_tensor(ge[:, k], blk[:, k, :].unsqueeze(2).to_broadcast([P, T, NB]),
                                           iota[:, 0:NB].unsqueeze(1).to_broadcast([P, T, NB]), ALU.is_ge))
                    c.link(v.tensor_reduce(blk[:, k, :], ge[:, k], AX.X, ALU.add))
                    c.link(v.tensor_scalar(blk[:, k, :], blk[:, k, :], -1.0, None, ALU.add))
                    c.link(v.tensor_scalar(row[:, k, :], blk[:, k, :], -float(P), None, ALU.mult))
                    c.link(v.tensor_tensor(row[:, k, :], row[:, k, :], dest[k][:], ALU.add))
                def indicator(x, n, k):
                    return v.tensor_tensor(x, iota[:, 0:n].unsqueeze(1).to_broadcast([P, T, n]), spread(k, n), ALU.is_equal)
                c.link(v.tensor_copy(tok_all[:], tok[:]))
                c.link(v.memset(tok_all[ST:P, 0:1], 0.0))
                for k in range(2):
                    c.step(indicator(oh_row[:, k], P, row[:, k, :]))
                    c.link(indicator(oh_blk[:, k], NB, blk[:, k, :]))
                    v.tensor_tensor(oh_blk[:, k], oh_blk[:, k], spread(tok_all[:], NB), ALU.mult).then_inc(pair_ready, 1)
                dve.wait_ge(pair_done, 1)
                c.step(v.memset(r["row_token"][:, NB:], 0.0))
                c.link(v.tensor_copy(r["row_token"][:, 0:NB], ps_tok[:, 0:NB]))


def experts(nc, io, dram, mem, r):
    with ExitStack() as ctx:
        def sb(name, shape, dt=F32):
            return ctx.enter_context(nc.sbuf_tensor(name, shape, dt))

        def sem(name):
            return ctx.enter_context(nc.semaphore(name))

        ident = mem["ident"]
        KF = DE // P
        wg = sb("wg", [P, 2, KD, DE])
        wu = sb("wu", [P, 2, KD, DE])
        wd = sb("wd", [P, 2, KF, D])
        idx = sb("gather_idx", [P, 2], I32)
        xg = sb("xg", [P, 2, D])
        xT = sb("xT", [P, KD, P])
        sg = sb("sg", [P, DE])
        hh = sb("hh", [P, DE])
        hT = sb("ehT", [P, KF, P])
        y = sb("y", [P, 2, D])
        ps_x = ctx.enter_context(nc.psum_tensor("e_x", [P, KD, P], F32))
        ps_gu = ctx.enter_context(nc.psum_tensor("e_gu", [P, 2, 512], F32))
        ps_h = ctx.enter_context(nc.psum_tensor("e_h", [P, KF, P], F32))
        ps_y = ctx.enter_context(nc.psum_tensor("e_y", [P, 2, 512], F32))

        held_sp, held_pool, held_pe = sem("e_held_sp"), sem("e_held_pool"), sem("e_held_pe")
        gu_in = [sem("gu_in0"), sem("gu_in1")]
        wd_in = [sem("wd_in0"), sem("wd_in1")]
        idx_ready = sem("idx_ready")
        x_in = [sem("xg_in0"), sem("xg_in1")]
        xT_done = sem("xT_done")
        xT_kept = sem("xT_kept")
        gu_done = sem("gu_done")
        sg_ready = sem("sg_ready")
        hh_ready = sem("hh_ready")
        hT_done = sem("ehT_done")
        hT_kept = sem("ehT_kept")
        y_done = sem("y_done")
        y_kept = sem("y_kept")
        y_out = [sem("y_out0"), sem("y_out1")]
        LEAD = 4

        def each_block(eng, step, finish):
            pairs = eng.value_load(r["pairs"][0:1, 0:1], min_val=0, max_val=NB // 2)
            for b in range(LEAD):
                step(b, b % 2, b // 2)
            with eng.Fori(LEAD // 2, NB // 2 + 1) as i:
                with eng.If(i < pairs):
                    for u in range(2):
                        step(2 * i + u, u, i)
                with eng.If(i == pairs):
                    finish(i)

        with nc.Block() as block:
            @block.sync
            def _(sp):
                def load(b, weights, arrived):
                    fresh = sp.value_load(r["fresh"][0:1, ds(b, 1)], min_val=0, max_val=1)
                    with sp.If(fresh == 1):
                        e = sp.value_load(r["block_expert"][0:1, ds(b, 1)], min_val=0, max_val=NE - 1)
                        place = sp.value_load(r["turn"][0:1, ds(b, 1)], min_val=0, max_val=NE) % 2
                        for dst, src in weights:
                            sp.dma_start(dst[:, ds(place, 1)].rearrange("p o k n -> p (o k) n"),
                                         src[0, ds(e, 1)].rearrange("o (k p) n -> p (o k) n", p=P)).then_inc(arrived, 16)
                    with sp.Else():
                        sp.sem_inc(arrived, 16 * len(weights))

                def load_gu(b, u):
                    waited(sp, gu_done, b - 1)
                    sp.sem_inc(held_sp, 1)
                    load(b, ((wg, io["w_exp_gate"]), (wu, io["w_exp_up"])), gu_in[u])

                def load_d(b, u):
                    waited(sp, y_done, b - 1)
                    sp.sem_inc(held_sp, 1)
                    load(b, ((wd, io["w_exp_down"]),), wd_in[u])

                def store_y(b, u):
                    sp.wait_ge(y_kept, b + 1)
                    sp.sem_inc(held_sp, 1)
                    sp.dma_start(dram["y"][ds(b * P, P), :], y[:, u, :]).then_inc(y_out[u], 16)

                def step(b, u, i):
                    load_gu(b, u)
                    if not isinstance(b, int) or b >= 1:
                        load_d(b - 1, 1 - u)
                    if not isinstance(b, int) or b >= 3:
                        store_y(b - 3, 1 - u)

                def finish(pairs):
                    load_d(2 * pairs - 1, 1)
                    for back in (3, 2, 1):
                        store_y(2 * pairs - back, back % 2)
                    for u in range(2):
                        sp.wait_ge(y_out[u], 16 * pairs)
                        sp.sem_inc(held_sp, 1)
                each_block(sp, step, finish)

            @block.gpsimd
            def _(pool):
                def gather(b, u, i):
                    waited(pool, xT_done, b - 1)
                    pool.sem_inc(held_pool, 1)
                    nc.gpsimd.tensor_copy(idx[:, u:u + 1], r["row_token"][:, ds(b, 1)]).then_inc(idx_ready, 1)
                    pool.wait_ge(idx_ready, b + 1)
                    pool.sem_inc(held_pool, 1)
                    pool.indirect_dma_start(xg[:, u, :], None, dram["h2"][:, :],
                                            bass.IndirectOffsetOnAxis(ap=idx[:, u:u + 1], axis=0)).then_inc(x_in[u], 16)
                each_block(pool, gather, lambda pairs: gather(2 * pairs, 0, pairs))

            @block.tensor
            def _(pe):
                def turn_x(b, u, i):
                    pe.wait_ge(x_in[u], 16 * (i + 1))
                    for k in range(KD):
                        last = pe.transpose(ps_x[:, k, :], xg[:, u, k * P:(k + 1) * P], ident[:])
                    last.then_inc(xT_done, 1)

                def place_of(b):
                    return pe.value_load(r["turn"][0:1, ds(b, 1)], min_val=0, max_val=NE) % 2

                def gate_up(b, u, i):
                    place = place_of(b)
                    pe.wait_ge(xT_kept, b + 1)
                    pe.wait_ge(gu_in[u], 32 * (i + 1))
                    pe.sem_inc(held_pe, 1)
                    for n, w in enumerate((wg, wu)):
                        for k in range(KD):
                            last = pe.matmul(ps_gu[:, n, :], xT[:, k, :], w[:, ds(place, 1), k, :], start=(k == 0), stop=(k == KD - 1))
                    last.then_inc(gu_done, 1)

                def turn_h(b):
                    pe.wait_ge(hh_ready, b + 1)
                    for k in range(KF):
                        last = pe.transpose(ps_h[:, k, :], hh[:, k * P:(k + 1) * P], ident[:])
                    last.then_inc(hT_done, 1)

                def down(b, u, i):
                    place = place_of(b)
                    pe.wait_ge(hT_kept, b + 1)
                    pe.wait_ge(wd_in[u], 16 * (i + 1))
                    waited(pe, y_kept, b)
                    pe.sem_inc(held_pe, 1)
                    for half in range(2):
                        for k in range(KF):
                            last = pe.matmul(ps_y[:, half, :], hT[:, k, :], wd[:, ds(place, 1), k, half * 512:(half + 1) * 512],
                                             start=(k == 0), stop=(k == KF - 1))
                    last.then_inc(y_done, 1)

                def step(b, u, i):
                    gate_up(b, u, i)
                    turn_x(b + 1, 1 - u, i + u)
                    if not (isinstance(b, int) and b == 0):
                        down(b - 1, 1 - u, i + u - 1)
                    turn_h(b)
                turn_x(0, 0, 0)
                each_block(pe, step, lambda pairs: down(2 * pairs - 1, 1, pairs - 1))

            @block.scalar
            def _(act):
                def keep_x(b):
                    act.wait_ge(xT_done, b + 1)
                    nc.scalar.activation(xT[:], ps_x[:], ACT.Copy).then_inc(xT_kept, 1)

                def silu(b):
                    act.wait_ge(gu_done, b + 1)
                    waited(act, hh_ready, b)
                    nc.scalar.activation(sg[:], ps_gu[:, 0, :], ACT.Silu).then_inc(sg_ready, 1)

                def keep_y(b, u, i):
                    waited(act, y_out[u], 16 * i)
                    act.wait_ge(y_done, b + 1)
                    nc.scalar.activation(y[:, u, :].rearrange("p (a n) -> p a n", a=2), ps_y[:], ACT.Copy).then_inc(y_kept, 1)

                def step(b, u, i):
                    silu(b)
                    keep_x(b + 1)
                    if not (isinstance(b, int) and b == 0):
                        keep_y(b - 1, 1 - u, i + u - 1)
                keep_x(0)
                each_block(act, step, lambda pairs: keep_y(2 * pairs - 1, 1, pairs - 1))

            @block.vector
            def _(dve):
                def step(b, u, i):
                    waited(dve, hT_done, b)
                    dve.wait_ge(sg_ready, b + 1)
                    nc.vector.tensor_tensor(hh[:], ps_gu[:, 1, :], sg[:], ALU.mult).then_inc(hh_ready, 1)
                    dve.wait_ge(hT_done, b + 1)
                    nc.vector.tensor_copy(hT[:], ps_h[:]).then_inc(hT_kept, 1)
                each_block(dve, step, lambda pairs: None)


def combine(nc, io, out, dram, mem, r):
    with ExitStack() as ctx:
        def sb(name, shape, dt=F32):
            return ctx.enter_context(nc.sbuf_tensor(name, shape, dt))

        def sem(name):
            return ctx.enter_context(nc.semaphore(name))

        RING = 4
        gate2 = sb("gate2", [P, 2, D])
        g_final = sb("g_final_b", [P, D])
        x = sb("c_x", [P, RING, D])
        ya = sb("c_ya", [P, RING, D])
        yb = sb("c_yb", [P, RING, D])
        yo = sb("c_out", [P, RING, D])
        idx = sb("c_idx", [P, 2 * RING], I32)
        st = sb("c_stats", [P, 3 * RING])
        eps = mem["eps"]
        par_in = sem("c_params_in")
        held_sp, held_pool, held_act, held_dve = (sem(f"c_held_{e}") for e in ("sp", "pool", "act", "dve"))
        x_in = [sem(f"c_x_in{u}") for u in range(RING)]
        y_in = [sem(f"c_y_in{u}") for u in range(RING)]
        idx_ready = sem("c_idx_ready")
        scaled = sem("c_scaled")
        mixed = sem("c_mixed")
        squared = sem("c_squared")
        rooted = sem("c_rooted")
        out_ready = sem("c_out_ready")
        stored = [sem(f"c_stored{u}") for u in range(RING)]
        own = sem("c_dve_own")

        def each_tile(eng, step):
            for n in range(RING):
                step(n, n, 0)
            with eng.Fori(1, NT // RING - 1) as i:
                for u in range(RING):
                    step(RING * i + u, u, i)
            for n in range(NT - RING, NT + 1):
                step(n, n % RING, n // RING)

        def is_sample(n):
            return isinstance(n, int) and n == NT

        with nc.Block() as block:
            @block.sync
            def _(sp):
                sp.dma_start(gate2[:, 0, :], prompt_mod(dram, MOD_GATE2)).then_inc(par_in, 16)
                sp.dma_start(gate2[0:ST, 1, :], sample_mod(dram, MOD_GATE2)).then_inc(par_in, 16)
                sp.dma_start(g_final[:], io["g_final"].rearrange("(o d) -> o d", o=1).broadcast_to([P, D])).then_inc(par_in, 16)

                def load(n, u, i):
                    waited(sp, out_ready, n - RING + 1)
                    sp.sem_inc(held_sp, 1)
                    if is_sample(n):
                        sp.dma_start(x[0:ST, u, :], dram["x2"][SEQ:NTOK, :]).then_inc(x_in[u], 16)
                    else:
                        sp.dma_start(x[:, u, :], dram["x2"][ds(n * P, P), :]).then_inc(x_in[u], 16)
                each_tile(sp, load)

            @block.gpsimd
            def _(pool):
                def gather(n, u, i):
                    waited(pool, squared, n - RING + 1)
                    pool.sem_inc(held_pool, 1)
                    col = 0 if is_sample(n) else n + 1
                    for k, dst in ((0, ya), (1, yb)):
                        at = idx[:, 2 * u + k:2 * u + k + 1]
                        nc.gpsimd.tensor_copy(at, r["dest"][:, k:k + 1, ds(col, 1)].rearrange("p o t -> p (o t)")).then_inc(idx_ready, 1)
                        pool.wait_ge(idx_ready, 2 * n + k + 1)
                        pool.sem_inc(held_pool, 1)
                        pool.indirect_dma_start(dst[:, u, :], None, dram["y"][:, :],
                                                bass.IndirectOffsetOnAxis(ap=at, axis=0)).then_inc(y_in[u], 16)
                each_tile(pool, gather)

            @block.scalar
            def _(act):
                def scale(n, u, i):
                    R, col = (ST, 0) if is_sample(n) else (P, n + 1)
                    act.wait_ge(y_in[u], 32 * (i + 1))
                    act.sem_inc(held_act, 1)
                    nc.scalar.activation(ya[0:R, u, :], ya[0:R, u, :], ACT.Copy,
                                         scale=r["gate"][0:R, 0:1, ds(col, 1)].rearrange("p o t -> p (o t)")).then_inc(scaled, 1)

                def root(n, u):
                    R = ST if is_sample(n) else P
                    act.wait_ge(mixed, n + 1)
                    nc.scalar.activation(ya[0:R, u, :], x[0:R, u, :], ACT.Square, accum_out=st[0:R, u:u + 1]).then_inc(squared, 1)
                    act.wait_ge(squared, n + 1)
                    nc.scalar.activation(st[0:R, RING + u:RING + u + 1], st[0:R, u:u + 1], ACT.Sqrt, bias=eps[0:R, 0:1],
                                         scale=1.0 / D).then_inc(rooted, 1)

                def store(n, u):
                    act.wait_ge(out_ready, n + 1)
                    act.sem_inc(held_act, 1)
                    if is_sample(n):
                        act.dma_start(out["y_sample"], yo[0:ST, u, :]).then_inc(stored[u], 16)
                    else:
                        act.dma_start(out["y_prompt"][ds(n * P, P), :], yo[:, u, :]).then_inc(stored[u], 16)

                def step(n, u, i):
                    if not is_sample(n):
                        scale(n + 1, (u + 1) % RING, i + (u == RING - 1))
                    root(n, u)
                    if not (isinstance(n, int) and n == 0):
                        store(n - 1, (u - 1) % RING)
                scale(0, 0, 0)
                each_tile(act, step)
                store(NT, 0)
                for u in range(RING):
                    act.wait_ge(stored[u], 16 * (NT // RING + (u == 0)))

            @block.vector
            def _(dve):
                v = nc.vector
                LINKS = 2

                def mix(n, u, i, c):
                    R, col = (ST, 0) if is_sample(n) else (P, n + 1)
                    dve.wait_ge(scaled, n + 1)
                    dve.sem_inc(held_dve, 1)
                    c.link(v.scalar_tensor_tensor(out=yb[0:R, u, :], in0=yb[0:R, u, :],
                                                  scalar=r["gate"][0:R, 1:2, ds(col, 1)].rearrange("p o t -> p (o t)"),
                                                  in1=ya[0:R, u, :], op0=ALU.mult, op1=ALU.add))
                    c.link(v.tensor_tensor(yb[0:R, u, :], yb[0:R, u, :], gate2[0:R, 1 if is_sample(n) else 0, :], ALU.mult))
                    dve.wait_ge(x_in[u], 16 * (i + 1))
                    v.tensor_tensor(x[0:R, u, :], x[0:R, u, :], yb[0:R, u, :], ALU.add).then_inc(mixed, 1)

                def finish(n, u, i, c):
                    R = ST if is_sample(n) else P
                    dve.wait_ge(rooted, n + 1)
                    c.link(v.reciprocal(st[0:R, 2 * RING + u:2 * RING + u + 1], st[0:R, RING + u:RING + u + 1]))
                    waited(dve, stored[u], 16 * i)
                    v.scalar_tensor_tensor(out=yo[0:R, u, :], in0=x[0:R, u, :], scalar=st[0:R, 2 * RING + u:2 * RING + u + 1],
                                           in1=g_final[0:R, :], op0=ALU.mult, op1=ALU.mult).then_inc(out_ready, 1)

                def step(n, u, i):
                    c = Chain(dve, own, (LINKS + 1) * n - (0 if isinstance(n, int) and n == 0 else 1))
                    mix(n, u, i, c)
                    if not (isinstance(n, int) and n == 0):
                        finish(n - 1, (u - 1) % RING, i - (u == 0), c)
                dve.wait_ge(par_in, 48)
                each_tile(dve, step)
                finish(NT, 0, NT // RING, Chain(dve, own, (LINKS + 1) * (NT + 1) - 1))
def small_inputs(nc, ctx, mem):
    def sb(name, shape):
        return ctx.enter_context(nc.sbuf_tensor(name, shape, F32))

    return {
        "ws": sb("ws", [P, GB, P]),
        "ws_corner": sb("ws_corner", [ST, GB, DQ]),
        "tril": sb("tril", [P, P]),
        "tril_s": sb("tril_s", [ST, ST]),
        "lam_rows": sb("lam_rows", [P, 4, DK]),
        "in": stage_semaphore(nc, mem["used_semaphores"], "setup_in"),
    }


def load_small(nc, eng, io, mem, w):
    def load(dst, src):
        eng.dma_start(dst, src).then_inc(w["in"], 16)

    load(w["ws"][:], io["w_s"][0].rearrange("g t s -> t g s"))
    load(w["tril"][:], io["c_tril"])
    load(w["tril_s"][:], io["c_tril_s"])
    with nc.allow_non_contiguous_dma(reason="b_s by position, 8x8 corner of W_s"):
        for b in range(DB):
            load(w["ws_corner"][DQ * b:DQ * (b + 1)], io["w_s"][0, :, 0:DQ, 0:DQ].rearrange("g t s -> t g s"))
            load(mem["bs_s"][DQ * b:DQ * (b + 1), :], io["b_s"][0, :, 0:DQ].rearrange("g t -> t g"))
        load(mem["bs_p"][:], io["b_s"][0].rearrange("g t -> t g"))
    load(w["lam_rows"][:], io["lam_p"].broadcast_to([P, 4, DK]))
    load(mem["rope"][:], io["c_rope"])


def setup(nc, mem, w):
    with ExitStack() as ctx:
        def sb(name, shape, dt=F32):
            return ctx.enter_context(nc.sbuf_tensor(name, shape, dt))

        def sem(name):
            return stage_semaphore(nc, mem["used_semaphores"], name)

        ident = mem["ident"]
        ws, ws_corner, tril, tril_s, lam_rows = (w[n] for n in ("ws", "ws_corner", "tril", "tril_s", "lam_rows"))
        ws_s = sb("ws_s", [ST, GB, ST])
        pt = ctx.enter_context(nc.psum_tensor("ws_t", [P, GB, P], F32))
        pts = ctx.enter_context(nc.psum_tensor("ws_ts", [P, 512], F32))
        masked = sem("ws_masked")
        turned = sem("ws_turned")
        kept = sem("ws_kept")
        LOADS = 3 + 2 * DB + 3
        lam_prod = sb("lam_prod", [P, 2, DK])
        lam_sum = sb("lam_sum", [P, 2])
        lam_exp = sb("lam_exp", [P, 2])
        lam_sums = sem("lam_sums")
        lam_exps = sem("lam_exps")
        own = sem("setup_dve_own")
        with nc.Block() as block:
            @block.vector
            def _(dve):
                nc.vector.memset(mem["eps"][:], EPS)
                dve.wait_ge(w["in"], 16 * LOADS)
                nc.vector.tensor_tensor(ws[:], ws[:], tril[:].unsqueeze(1).to_broadcast([P, GB, P]), ALU.mult)\
                    .then_inc(masked, 1)
                for g in range(GB):
                    ins = nc.vector.tensor_tensor(ws_s[:, g, :].rearrange("t (c s) -> t c s", c=DB),
                                                  tril_s[:].rearrange("t (c s) -> t c s", c=DB),
                                                  ws_corner[:, g:g + 1, :].to_broadcast([ST, DB, DQ]), ALU.mult)
                    ins.then_inc(masked, 1)
                chain = Chain(dve, own)
                chain.link(nc.vector.tensor_tensor(lam_prod[:], lam_rows[:, 0:4:2, :], lam_rows[:, 1:4:2, :], ALU.mult))
                nc.vector.tensor_reduce(lam_sum[:], lam_prod[:], AX.X, ALU.add).then_inc(lam_sums, 1)
                dve.wait_ge(lam_exps, 1)
                chain.link(nc.vector.tensor_tensor(mem["lam"][:], lam_exp[:, 0:1], lam_exp[:, 1:2], ALU.subtract))
                chain.link(nc.vector.tensor_scalar(mem["lam"][:], mem["lam"][:], LAM_INIT, None, ALU.add))
                dve.wait_ge(turned, 1)
                nc.vector.tensor_copy(mem["wsT_p"][:], pt[:]).then_inc(kept, 1)
                nc.vector.tensor_copy(mem["wsT_s"][:], pts[0:ST, 0:GB * ST].rearrange("s (g t) -> s g t", g=GB))\
                    .then_inc(kept, 1)

            @block.scalar
            def _(act):
                act.wait_ge(lam_sums, 1)
                nc.scalar.activation(lam_exp[:], lam_sum[:], ACT.Exp).then_inc(lam_exps, 1)

            @block.tensor
            def _(pe):
                pe.wait_ge(masked, 1 + GB)
                for g in range(GB):
                    pe.transpose(pt[:, g, :], ws[:, g, :], ident[:])
                    last = pe.transpose(pts[0:ST, g * ST:(g + 1) * ST], ws_s[:, g, :], ident[0:ST, 0:ST])
                last.then_inc(turned, 1)


def program(nc, io, out):
    def scratch(name, shape):
        return nc.dram_tensor(name, shape, F32).ap()

    dram = {
        "mod": scratch("scratch_mod", [6, 1 + ST, D]),
        "qT": scratch("scratch_qT", [NT, P, H, P]),
        "obT": scratch("scratch_obT", [NT, P, GB, P]),
        "x2": scratch("scratch_x2", [NTOK, D]),
        "h2": scratch("scratch_h2", [NTOK, D]),
        "y": scratch("scratch_y", [(NB + 2) * P, D]),
    }
    with ExitStack() as ctx:
        def sb(name, shape, dt=F32, ctx=ctx):
            return ctx.enter_context(nc.sbuf_tensor(name, shape, dt))

        ident = sb("ident", [P, P])
        mem = {
            "ident": ident,
            "eps": sb("eps", [P, 1]),
            "lam": sb("lam", [P, 1]),
            "lg": sb("router_logits", [P, NT + 1, NEG_G + NE]),
            "w_in_loaded": [ctx.enter_context(nc.semaphore(f"w_in_loaded{c}")) for c in range(INW // 512)],
            "used_semaphores": [],
        }
        with ExitStack() as attn:
            mem["kT"] = sb("kT", [P, H, SEQ], ctx=attn)
            mem["V"] = sb("V", [P, NT, AW], ctx=attn)
            mem["kT_new"] = sb("kT_new", [P, H, ST], ctx=attn)
            mem["V_new"] = sb("V_new", [ST, AW], ctx=attn)
            mem["qT_new"] = sb("qT_new", [P, H, ST], ctx=attn)
            mem["obT_new"] = sb("obT_new", [P, GB, ST], ctx=attn)
            mem["o_new"] = sb("o_new", [ST, AW], ctx=attn)
            with ExitStack() as proj:
                mem["w_in"] = sb("w_in_sb", [P, KD, INW], ctx=proj)
                mem["rope"] = sb("rope", [P, NT + 1, 2, 2, ROT // 2], ctx=proj)
                mem["wsT_p"] = sb("wsT_p", [P, GB, P], ctx=proj)
                mem["wsT_s"] = sb("wsT_s", [ST, GB, ST], ctx=proj)
                mem["bs_p"] = sb("bs_p", [P, GB], ctx=proj)
                mem["bs_s"] = sb("bs_s", [ST, GB], ctx=proj)
                with ExitStack() as first:
                    m = modulation_inputs(nc, first, mem)
                    small = small_inputs(nc, first, mem)
                    modulation(nc, io, dram["mod"], mem, m, small)
                    setup(nc, mem, small)
                front(nc, io, out, dram, mem)
            decode(nc, io, dram, mem)
            nc.clear_and_free_semaphores(mem["used_semaphores"])
            nc.all_engine_barrier()
            prompt(nc, io, dram, mem)
        routed = {
            "gate": sb("gate_weights", [P, 2, NT + 1]),
            "dest": sb("dest_rows", [P, 2, NT + 1], I32),
            "block_expert": sb("block_expert", [1, NB + 2], I32),
            "turn": sb("block_turn", [1, NB + 2], I32),
            "fresh": sb("block_fresh", [1, NB + 2], I32),
            "row_token": sb("row_token", [P, NB + 2]),
            "pairs": sb("pairs_in_use", [1, 1], I32),
        }
        routing(nc, io, mem, routed)
        experts(nc, io, dram, mem, routed)
        combine(nc, io, out, dram, mem, routed)


_INS = ["x_prompt", "x_sample", "cache_k", "cache_v", "page_table", "c_prompt", "c_sample", "w_ada", "b_ada", "g_norm1",
        "w_in", "lam_p", "g_attn", "g_v", "w_s", "b_s", "g_mlp", "w_out", "g_norm2", "w_router_g", "b_router_g",
        "w_router_e", "b_router_e", "w_exp_gate", "w_exp_up", "w_exp_down", "g_final"]
_OUTS = {
    "y_prompt": ((SEQ, D), (1, SEQ, D)),
    "y_sample": ((ST, D), (DB, DQ, D)),
    "k_prompt": ((SEQ, QKW), (1, 1, SEQ, H, 2, DK)),
    "v_prompt": ((SEQ, AW), (1, 1, SEQ, H, DV)),
    "k_sample": ((ST, QKW), (1, DB, DQ, H, 2, DK)),
    "v_sample": ((ST, AW), (1, DB, DQ, H, DV)),
    "cv_sample": ((ST, BW), (1, DB, DQ, BW)),
}


def kernel(**inputs):
    import numpy as _np
    import concourse.bacc as _bacc
    from concourse import mybir as _mybir
    from concourse.bass_utils import run_bass_kernel_spmd as _run

    nc = _bacc.Bacc("TRN2", target_bir_lowering=False, num_devices=1)
    arrays = {n: _np.ascontiguousarray(inputs[n]) for n in _INS}
    arrays.update(constants())
    io, out = {}, {}
    for name, a in arrays.items():
        io[name] = nc.dram_tensor(name, a.shape, _mybir.dt.from_np(a.dtype), kind="ExternalInput").ap()
    for name, (shape, _) in _OUTS.items():
        out[name] = nc.dram_tensor(f"out_{name}", shape, _mybir.dt.float32, kind="ExternalOutput").ap()
    program(nc, io, out)
    r = _run(nc, [arrays], core_ids=[0])
    return tuple(r.results[0][f"out_{n}"].reshape(full) for n, (_, full) in _OUTS.items())
```
